# Optimizing a Trainium2 kernel written in Bass

```python
import jax
import jax.numpy as jnp
from jax import lax
import numpy as np

D_MODEL = 1024
BATCH = 1
SEQ = 256
DEPTH = 2

GRID_W = 64
CTX_LEN = 256
CHUNK = 128
Q_BLOCK = 128
ROPE_THETA = 10000.0
EPS = 1e-6

A_GROUPS = 4
A_GROUP_DIM = 128
A_WIDTH = A_GROUPS * A_GROUP_DIM
B_HEADS = 4
B_KV_HEADS = 2
B_HEAD_DIM = 128
B_Q_WIDTH = B_HEADS * B_HEAD_DIM
B_KV_WIDTH = B_KV_HEADS * B_HEAD_DIM
AB_IN_WIDTH = 2 * A_WIDTH + B_Q_WIDTH + 2 * B_KV_WIDTH
AB_OUT_WIDTH = A_WIDTH + B_Q_WIDTH
C_HEADS = 8
C_Q_RANK = 384
C_KV_RANK = 256
C_NOPE = 128
C_ROPE = 64
C_V = 128
D_FF = 2816
N_EXPERTS = 8
TOP_K = 2
D_FF_EXPERT = 3584

kernel_name = 'hybrid_gmlp_gqa_mla_moe_diffusion_trunk'

def rms_norm(x, g):
    xf = x.astype(jnp.float32)
    y = xf * lax.rsqrt(jnp.mean(xf * xf, axis=-1, keepdims=True) + EPS)
    return (y * g.astype(jnp.float32)).astype(x.dtype)

def modulate(x, g, shift, scale):
    return rms_norm(x, g) * (1 + scale) + shift

def split_heads(t, n_heads, head_dim):
    return t.reshape(t.shape[:2] + (n_heads, head_dim))

def axial_rope_table(rows, rot_dim):
    n = rows * GRID_W
    row_idx = jnp.repeat(jnp.arange(rows, dtype=jnp.float32), GRID_W)
    col_idx = jnp.tile(jnp.arange(GRID_W, dtype=jnp.float32), rows)
    n_freq = rot_dim // 4
    inv_freq = ROPE_THETA ** (-jnp.arange(n_freq, dtype=jnp.float32) / n_freq)
    ang = jnp.stack([row_idx[:, None] * inv_freq, col_idx[:, None] * inv_freq], axis=1)
    ang = jnp.broadcast_to(ang[:, :, None, :], (n, 2, 2, n_freq)).reshape(n, rot_dim)
    return jnp.cos(ang), jnp.sin(ang)

def apply_rope(x, cos, sin):
    d = x.shape[-1]
    xs = x.reshape(x.shape[:-1] + (2, 2, d // 4))
    rot = jnp.stack([-xs[..., 1, :], xs[..., 0, :]], axis=-2).reshape(x.shape)
    out = x.astype(jnp.float32) * cos[None, :, None, :] + rot.astype(jnp.float32) * sin[None, :, None, :]
    return out.astype(x.dtype)

def block_attention(q, k, v, scale):
    bsz, s, kh, g, dk = q.shape
    nb = s // Q_BLOCK
    qb = jnp.moveaxis(q.reshape(bsz, nb, Q_BLOCK, kh, g, dk), 1, 0)

    def attend(q_blk):
        sc = jnp.einsum('bqhgd,bthd->bhgqt', q_blk, k, preferred_element_type=jnp.float32) * scale
        p = jax.nn.softmax(sc, axis=-1).astype(v.dtype)
        return jnp.einsum('bhgqt,bthd->bqhgd', p, v)

    o = lax.map(attend, qb)
    return jnp.moveaxis(o, 0, 1).reshape(bsz, s, kh, g, v.shape[-1])

def chunk_spatial_gating(u, v, norm_g, ws, bs):
    u = jax.nn.gelu(u)
    v = jax.nn.gelu(v)
    bsz, n, _ = v.shape
    vg = rms_norm(v.reshape(bsz, n, A_GROUPS, A_GROUP_DIM), norm_g.reshape(A_GROUPS, A_GROUP_DIM))
    vc = vg.reshape(bsz, n // CHUNK, CHUNK, A_GROUPS, A_GROUP_DIM)
    mixed = jnp.einsum('gij,bnjgc->bnigc', ws, vc) + bs.T[:, :, None]
    return u * mixed.reshape(bsz, n, A_WIDTH)

def mixer_gmlp_gqa(h_lat, h_ctx, w_in, a_norm_g, a_ws, a_bs, q_norm_g, k_norm_g, w_out, cos, sin, need_ctx):
    bsz, n, _ = h_lat.shape
    cuts = [A_WIDTH, 2 * A_WIDTH, 2 * A_WIDTH + B_Q_WIDTH, 2 * A_WIDTH + B_Q_WIDTH + B_KV_WIDTH]
    group = B_HEADS // B_KV_HEADS
    scale = B_HEAD_DIM ** -0.5
    u_l, v_l, q_l, k_l, val_l = jnp.split(h_lat @ w_in, cuts, axis=-1)
    if need_ctx:
        u_c, v_c, q_c, k_c, val_c = jnp.split(h_ctx @ w_in, cuts, axis=-1)
    else:
        k_c, val_c = jnp.split(h_ctx @ w_in[:, cuts[2]:], [B_KV_WIDTH], axis=-1)
    k_c = rms_norm(split_heads(k_c, B_KV_HEADS, B_HEAD_DIM), k_norm_g)
    val_c = split_heads(val_c, B_KV_HEADS, B_HEAD_DIM)
    k_l = apply_rope(rms_norm(split_heads(k_l, B_KV_HEADS, B_HEAD_DIM), k_norm_g), cos, sin)
    q_l = apply_rope(rms_norm(split_heads(q_l, B_HEADS, B_HEAD_DIM), q_norm_g), cos, sin)
    keys = jnp.concatenate([k_l, k_c], axis=1)
    vals = jnp.concatenate([split_heads(val_l, B_KV_HEADS, B_HEAD_DIM), val_c], axis=1)
    o_l = block_attention(q_l.reshape(bsz, n, B_KV_HEADS, group, B_HEAD_DIM), keys, vals, scale)
    a_l = chunk_spatial_gating(u_l, v_l, a_norm_g, a_ws, a_bs)
    y_l = jnp.concatenate([a_l, o_l.reshape(bsz, n, B_Q_WIDTH)], axis=-1) @ w_out
    if not need_ctx:
        return y_l, None
    nc = h_ctx.shape[1]
    q_c = rms_norm(split_heads(q_c, B_HEADS, B_HEAD_DIM), q_norm_g)
    o_c = block_attention(q_c.reshape(bsz, nc, B_KV_HEADS, group, B_HEAD_DIM), k_c, val_c, scale)
    a_c = chunk_spatial_gating(u_c, v_c, a_norm_g, a_ws, a_bs)
    y_c = jnp.concatenate([a_c, o_c.reshape(bsz, nc, B_Q_WIDTH)], axis=-1) @ w_out
    return y_l, y_c

def mla_keys_values(h, w_dkv, kv_norm_g, w_ukv, cos, sin):
    bsz, n, _ = h.shape
    kv_in = h @ w_dkv
    c_kv = rms_norm(kv_in[..., :C_KV_RANK], kv_norm_g)
    k_rope = kv_in[..., C_KV_RANK:][:, :, None, :]
    if cos is not None:
        k_rope = apply_rope(k_rope, cos, sin)
    kv = (c_kv @ w_ukv).reshape(bsz, n, C_HEADS, C_NOPE + C_V)
    k_nope, v = kv[..., :C_NOPE], kv[..., C_NOPE:]
    k = jnp.concatenate([k_nope, jnp.broadcast_to(k_rope, (bsz, n, C_HEADS, C_ROPE))], axis=-1)
    return k, v

def mla_queries(h, w_dq, q_norm_g, w_uq, cos, sin):
    bsz, n, _ = h.shape
    c_q = rms_norm(h @ w_dq, q_norm_g)
    q = (c_q @ w_uq).reshape(bsz, n, C_HEADS, C_NOPE + C_ROPE)
    q_nope, q_rope = q[..., :C_NOPE], q[..., C_NOPE:]
    if cos is not None:
        q_rope = apply_rope(q_rope, cos, sin)
    return jnp.concatenate([q_nope, q_rope], axis=-1)[:, :, :, None, :]

def mixer_mla(h_lat, h_ctx, w_dq, q_norm_g, w_uq, w_dkv, kv_norm_g, w_ukv, w_o, cos, sin, need_ctx):
    bsz, n, _ = h_lat.shape
    scale = (C_NOPE + C_ROPE) ** -0.5
    k_c, v_c = mla_keys_values(h_ctx, w_dkv, kv_norm_g, w_ukv, None, None)
    k_l, v_l = mla_keys_values(h_lat, w_dkv, kv_norm_g, w_ukv, cos, sin)
    q_l = mla_queries(h_lat, w_dq, q_norm_g, w_uq, cos, sin)
    o_l = block_attention(q_l, jnp.concatenate([k_l, k_c], axis=1), jnp.concatenate([v_l, v_c], axis=1), scale)
    y_l = o_l.reshape(bsz, n, C_HEADS * C_V) @ w_o
    if not need_ctx:
        return y_l, None
    nc = h_ctx.shape[1]
    q_c = mla_queries(h_ctx, w_dq, q_norm_g, w_uq, None, None)
    o_c = block_attention(q_c, k_c, v_c, scale)
    y_c = o_c.reshape(bsz, nc, C_HEADS * C_V) @ w_o
    return y_l, y_c

def swiglu(h, w_in, w_out):
    g, u = jnp.split(h @ w_in, 2, axis=-1)
    return (jax.nn.silu(g) * u) @ w_out

def moe_swiglu(h, router, w_in, w_out):
    logits = jnp.einsum('bnd,de->bne', h, router).astype(jnp.float32)
    top_logit, top_idx = lax.top_k(logits, TOP_K)
    top_w = jax.nn.softmax(top_logit, axis=-1)
    gates = jnp.sum(jax.nn.one_hot(top_idx, N_EXPERTS, dtype=jnp.float32) * top_w[..., None], axis=-2)
    out = jnp.zeros_like(h)
    for e in range(N_EXPERTS):
        out = out + gates[..., e:e + 1].astype(h.dtype) * swiglu(h, w_in[e], w_out[e])
    return out

def setup_inputs(seed: int = 0) -> dict:
    key = jax.random.key(seed)
    keys = iter(jax.random.split(key, 40))
    f32 = jnp.float32

    def normal(shape, scale):
        return jax.random.normal(next(keys), shape, f32) * scale

    def gain(shape):
        return 1.0 + normal(shape, 0.02)

    ne = (DEPTH + 1) // 2
    no = DEPTH // 2
    return {
        'x': normal((BATCH, SEQ, D_MODEL), 1.0),
        'c': normal((BATCH, D_MODEL), 1.0),
        'ctx': normal((BATCH, CTX_LEN, D_MODEL), 1.0),
        'c_ctx': normal((D_MODEL,), 1.0),
        'ada_w': normal((DEPTH, D_MODEL, 6 * D_MODEL), 0.5 * D_MODEL ** -0.5),
        'ada_b': normal((DEPTH, 6 * D_MODEL), 0.02),
        'g_pre_mix': gain((DEPTH, D_MODEL)),
        'g_post_mix': gain((DEPTH, D_MODEL)),
        'g_pre_ffn': gain((DEPTH, D_MODEL)),
        'g_post_ffn': gain((DEPTH, D_MODEL)),
        'ab_w_in': normal((ne, D_MODEL, AB_IN_WIDTH), D_MODEL ** -0.5),
        'a_norm_g': gain((ne, A_WIDTH)),
        'a_ws': normal((ne, A_GROUPS, CHUNK, CHUNK), CHUNK ** -0.5),
        'a_bs': normal((ne, A_GROUPS, CHUNK), 0.02),
        'b_qnorm_g': gain((ne, B_HEAD_DIM)),
        'b_knorm_g': gain((ne, B_HEAD_DIM)),
        'ab_w_out': normal((ne, AB_OUT_WIDTH, D_MODEL), AB_OUT_WIDTH ** -0.5),
        'ffn_w_in': normal((ne, D_MODEL, 2 * D_FF), D_MODEL ** -0.5),
        'ffn_w_out': normal((ne, D_FF, D_MODEL), D_FF ** -0.5),
        'mla_w_dq': normal((no, D_MODEL, C_Q_RANK), D_MODEL ** -0.5),
        'mla_qnorm_g': gain((no, C_Q_RANK)),
        'mla_w_uq': normal((no, C_Q_RANK, C_HEADS * (C_NOPE + C_ROPE)), C_Q_RANK ** -0.5),
        'mla_w_dkv': normal((no, D_MODEL, C_KV_RANK + C_ROPE), D_MODEL ** -0.5),
        'mla_kvnorm_g': gain((no, C_KV_RANK)),
        'mla_w_ukv': normal((no, C_KV_RANK, C_HEADS * (C_NOPE + C_V)), C_KV_RANK ** -0.5),
        'mla_w_o': normal((no, C_HEADS * C_V, D_MODEL), (C_HEADS * C_V) ** -0.5),
        'moe_router': normal((no, D_MODEL, N_EXPERTS), D_MODEL ** -0.5),
        'moe_w_in': normal((no, N_EXPERTS, D_MODEL, 2 * D_FF_EXPERT), D_MODEL ** -0.5),
        'moe_w_out': normal((no, N_EXPERTS, D_FF_EXPERT, D_MODEL), D_FF_EXPERT ** -0.5),
    }

def reference(x, c, ctx, c_ctx, ada_w, ada_b, g_pre_mix, g_post_mix, g_pre_ffn, g_post_ffn,
              ab_w_in, a_norm_g, a_ws, a_bs, b_qnorm_g, b_knorm_g, ab_w_out, ffn_w_in, ffn_w_out,
              mla_w_dq, mla_qnorm_g, mla_w_uq, mla_w_dkv, mla_kvnorm_g, mla_w_ukv, mla_w_o,
              moe_router, moe_w_in, moe_w_out):
    n_ctx = ctx.shape[1]
    rows = x.shape[1] // GRID_W
    cos_b, sin_b = axial_rope_table(rows, B_HEAD_DIM)
    cos_c, sin_c = axial_rope_table(rows, C_ROPE)
    act_lat = jax.nn.silu(c)
    act_ctx = jax.nn.silu(c_ctx)[None, :]
    for layer in range(DEPTH):
        need_ctx = layer < DEPTH - 1
        i = layer // 2
        mod_lat = jnp.split((act_lat @ ada_w[layer] + ada_b[layer])[:, None, :], 6, axis=-1)
        mod_ctx = jnp.split((act_ctx @ ada_w[layer] + ada_b[layer])[:, None, :], 6, axis=-1)
        h_lat = modulate(x, g_pre_mix[layer], mod_lat[0], mod_lat[1])
        h_ctx = modulate(ctx, g_pre_mix[layer], mod_ctx[0], mod_ctx[1])
        if layer % 2 == 0:
            y_lat, y_ctx = mixer_gmlp_gqa(h_lat, h_ctx, ab_w_in[i], a_norm_g[i], a_ws[i], a_bs[i],
                                          b_qnorm_g[i], b_knorm_g[i], ab_w_out[i], cos_b, sin_b, need_ctx)
        else:
            y_lat, y_ctx = mixer_mla(h_lat, h_ctx, mla_w_dq[i], mla_qnorm_g[i], mla_w_uq[i], mla_w_dkv[i],
                                     mla_kvnorm_g[i], mla_w_ukv[i], mla_w_o[i], cos_c, sin_c, need_ctx)
        x = x + mod_lat[2] * rms_norm(y_lat, g_post_mix[layer])
        f_lat = modulate(x, g_pre_ffn[layer], mod_lat[3], mod_lat[4])
        if need_ctx:
            ctx = ctx + mod_ctx[2] * rms_norm(y_ctx, g_post_mix[layer])
            f_ctx = modulate(ctx, g_pre_ffn[layer], mod_ctx[3], mod_ctx[4])
            f_in = jnp.concatenate([f_ctx, f_lat], axis=1)
        else:
            f_in = f_lat
        if layer % 2 == 0:
            f_out = swiglu(f_in, ffn_w_in[i], ffn_w_out[i])
        else:
            f_out = moe_swiglu(f_in, moe_router[i], moe_w_in[i], moe_w_out[i])
        f_out = rms_norm(f_out, g_post_ffn[layer])
        if need_ctx:
            ctx = ctx + mod_ctx[5] * f_out[:, :n_ctx]
            x = x + mod_lat[5] * f_out[:, n_ctx:]
        else:
            x = x + mod_lat[5] * f_out
    return x


_drawn_inputs = setup_inputs


def setup_inputs(seed=0):
    import zlib

    import numpy as np

    out = dict(_drawn_inputs(seed))
    spreads = {}
    factors = {'g_pre_mix': 2.855,
     'g_post_mix': 2.866,
     'g_post_ffn': 5.996,
     'a_norm_g': 3.491,
     'a_bs': 3.044,
     'b_qnorm_g': 8.0,
     'b_knorm_g': 7.067,
     'mla_qnorm_g': 6.852,
     'mla_kvnorm_g': 3.679}
    for name, (base, spread) in spreads.items():
        noise = np.random.default_rng([zlib.crc32(name.encode()), seed]).standard_normal(out[name].shape)
        drawn = base * np.exp(spread * noise) if base else spread * noise
        out[name] = jnp.asarray(drawn.astype(out[name].dtype))
    for name, factor in factors.items():
        out[name] = (out[name] * factor).astype(out[name].dtype)
    return out
```

```python
from contextlib import ExitStack

import numpy as np

import concourse.bass as bass
from concourse import mybir

ALU = mybir.AluOpType
ACT = mybir.ActivationFunctionType
AXX = mybir.AxisListType.X
F32 = mybir.dt.float32
F32R = mybir.dt.float32r
BF16 = mybir.dt.bfloat16
I32 = mybir.dt.int32
U32 = mybir.dt.uint32

P = 128
D = 1024
KD = D // P
SEQ = 256
CTX = 256
NTOK = SEQ + CTX
NB = NTOK // P
LB = SEQ // P
GRID_W = 64
EPS = 1e-6
HD = 128
CROPE = 64
CQ, CKV = 384, 256
D_FF = 2816
NE = 8
D_FFE = 3584

UNIT = 2048
RAW = 6
SPL = 3
FCH = 512
NCH = D_FFE // FCH
VISIT = NCH * 6

N_ADA = 0
N_ABIN = N_ADA + 2 * 24
N_ABOUT = N_ABIN + 8
N_FIN = N_ABOUT + 4
N_FOUT = N_FIN + 22
N_MLA = N_FOUT + 11
N_MOE = N_MLA + 13

C_ID, C_TRI, C_IOTA = 0, 128, 256
C_CB, C_SB = 512, 768
C_CC, C_SC = 1024, 1152
C_SEL, C_BC, C_EPS, C_I8 = 1280, 1282, 1538, 1539
C_N = 1552


def constants():
    k = np.zeros((P, C_N), np.float32)
    k[:, C_ID:C_ID + P] = np.eye(P)
    k[:, C_TRI:C_TRI + P] = np.triu(np.ones((P, P)), 1)
    k[:, C_IOTA:C_IOTA + 256] = np.arange(256)
    tok = np.arange(SEQ)
    row, col = (tok // GRID_W).astype(np.float32), (tok % GRID_W).astype(np.float32)
    for width, c0, s0 in ((HD, C_CB, C_SB), (CROPE, C_CC, C_SC)):
        nf = width // 4
        inv = np.float32(10000.0) ** (-np.arange(nf, dtype=np.float32) / np.float32(nf))
        ang = np.stack([row[:, None] * inv, col[:, None] * inv], axis=1).astype(np.float32)
        ang = np.broadcast_to(ang[:, :, None, :], (SEQ, 2, 2, nf))
        sign = np.array([-1.0, 1.0], np.float32)[None, None, :, None]
        for b in range(LB):
            t = slice(b * P, b * P + P)
            k[:, c0 + b * width:c0 + (b + 1) * width] = np.cos(ang[t]).reshape(P, width)
            k[:, s0 + b * width:s0 + (b + 1) * width] = (np.sin(ang[t]) * sign).reshape(P, width)
    for q in range(3):
        for r, s in ((0, (1, 0)), (1, (0, 1)), (2, (1, 0)), (3, (0, 1)), (4, (1, 1))):
            k[32 * q + r, C_SEL:C_SEL + 2] = s
            k[32 * q + r, C_BC:C_BC + P] = s[0]
            k[32 * q + r, C_BC + P:C_BC + 2 * P] = s[1]
    k[:, C_EPS] = EPS
    k[:, C_I8:C_I8 + NE] = np.arange(NE)
    return k


def trunk(nc, x, c, ctx, c_ctx, ada_w, ada_b, g_pre_mix, g_post_mix, g_pre_ffn, g_post_ffn,
          ab_w_in, a_norm_g, a_ws, a_bs, b_qnorm_g, b_knorm_g, ab_w_out, ffn_w_in, ffn_w_out,
          mla_w_dq, mla_qnorm_g, mla_w_uq, mla_w_dkv, mla_kvnorm_g, mla_w_ukv, mla_w_o,
          moe_router, moe_w_in, moe_w_out, consts, out):
    es = ExitStack()
    with es:
        def sb(name, shape, dt=F32):
            return es.enter_context(nc.sbuf_tensor(name, shape, dt))

        def sem(name):
            return es.enter_context(nc.semaphore(name))

        raw = [sb(f"raw{i}", [P, UNIT]) for i in range(RAW)]
        high = [sb(f"high{i}", [P, UNIT], F32R) for i in range(SPL)]
        low = [sb(f"low{i}", [P, UNIT], F32R) for i in range(SPL)]
        X = sb("X", [P, NB, D])
        ah = sb("ah", [P, KD * NTOK], F32R)
        al = sb("al", [P, KD * NTOK], F32R)
        tmp = sb("tmp", [P, 2 * 512])
        K = sb("K", [P, C_N])
        mixc = sb("mixc", [P, 1280])
        vec = sb("vec", [P, 64])
        modc = sb("modc", [P, 2, 2, 2, KD, 2])
        scol = sb("scol", [P, 2, 2, KD, 2])
        sc = sb("sc", [P, 160])
        sil = sb("sil", [P, 2, KD])
        act4 = sb("act4", [P, KD, 4], F32R)
        cnt = sb("cnt", [P, NE], I32)
        work = sb("work", [P, 11 * 1024])
        PS = es.enter_context(nc.psum_tensor("PS", [P, 8, 512], F32))
        gg_dram = nc.dram_tensor("gg_scratch", [6, P, D], F32).ap()

        ident = K[:, C_ID:C_ID + P]
        xn = work[:, 0:NB * D].rearrange("p (b d) -> p b d", b=NB)
        raw_loaded = [sem(f"raw_loaded{i}") for i in range(RAW)]
        high_made = sem("high_made")
        low_made = [sem(f"low_made{i}") for i in range(SPL)]
        unit_used = sem("unit_used")

        def load_unit(sp, n, src, it=0):
            if n >= RAW:
                m = makers(n)
                sp.wait_ge(low_made[n % SPL], m * ((n - RAW) // SPL + 1) + it * (2 * m))
            dst = raw[n % RAW][:, 0:src.shape[1] * src.shape[2]].rearrange("p (a n) -> p a n", a=src.shape[1])
            sp.dma_start(dst, src).then_inc(raw_loaded[n % RAW], 16)

        def split_high(act, n, it=0, width=UNIT):
            act.wait_ge(raw_loaded[n % RAW], 16 * (n // RAW + 1) + it * 16)
            if n >= SPL:
                act.wait_ge(unit_used, n - SPL + 1 + it * 6)
            act.activation(high[n % SPL][:, 0:width], raw[n % RAW][:, 0:width], ACT.Copy).then_inc(high_made, 1)

        def makers(n):
            return 2 if n % SPL == SPL - 1 else 1

        def split_low(eng, n, it, c0, c1):
            eng.wait_ge(high_made, n + 1 + it * 6)
            eng.tensor_tensor(low[n % SPL][:, c0:c1], raw[n % RAW][:, c0:c1],
                              high[n % SPL][:, c0:c1].bitcast(F32), ALU.subtract).then_inc(low_made[n % SPL], 1)

        def vector_low(dve, n, it=0, width=UNIT):
            split_low(dve, n, it, 0 if makers(n) == 1 else width // 2, width)

        def pool_low(pool, n, it=0, width=UNIT):
            split_low(pool, n, it, 0, width // 2)

        def unit_ready(pe, n, it=0):
            m = makers(n)
            pe.wait_ge(low_made[n % SPL], m * (n // SPL + 1) + it * (2 * m))

        def halves(n, a, width=UNIT):
            return [t[n % SPL][:, 0:width].rearrange("p (a n) -> p a n", a=a) for t in (high, low)]

        def product(pe, o, sh, sl, mh, ml, start, stop):
            pe.matmul(o, sh, mh, start=start, stop=False)
            pe.matmul(o, sh, ml, start=False, stop=False)
            return pe.matmul(o, sl, mh, start=False, stop=stop)

        ahk = ah[:, :].rearrange("p (k t) -> p k t", k=KD)
        alk = al[:, :].rearrange("p (k t) -> p k t", k=KD)

        modrows = work[:, 0:4096]
        gpost = work[:, 4096:8192].rearrange("p (a n) -> p a n", a=4)
        ggmake = work[:, 8192:10240].rearrange("p (a n) -> p a n", a=2)
        U = work[:, 4096:6144].rearrange("p (b n) -> p b n", b=NB)
        V = work[:, 6144:8192].rearrange("p (b n) -> p b n", b=NB)
        Q = work[:, 0:2048].rearrange("p (b n) -> p b n", b=NB)
        KV = work[:, 2048:4096].rearrange("p (b n) -> p b n", b=NB)
        qT = work[:, 8192:10240].rearrange("p (h t) -> p h t", h=4)
        kT = work[:, 10240:11264].rearrange("p (h t) -> p h t", h=2)
        HID = work[:, 0:22 * 512].rearrange("p (f t) -> p f t", f=22)
        knT = work[:, 4096:8192].rearrange("p (h t) -> p h t", h=8)
        qnT = work[:, 8192:10240].rearrange("p (h t) -> p h t", h=8)
        krT = work[:, 10240:10752]
        V1 = work[:, 0:4096].rearrange("p (b n) -> p b n", b=NB)
        cqn = work[:, 0:768].rearrange("p (b n) -> p b n", b=2)
        ckvn = work[:, 768:1792].rearrange("p (b n) -> p b n", b=NB)
        kr2 = work[:, 1792:2304].rearrange("p (b n) -> p b n", b=NB)
        qrt = work[:, 2304:3328].rearrange("p (b n) -> p b n", b=2)
        rot = work[:, 4096:5120]
        GG = work[:, 4096:6144].rearrange("p (a n) -> p a n", a=2)
        ACC = work[:, 2048:4096].rearrange("p (b n) -> p b n", b=2)
        GGm = work[:, 4096:5120]
        sg = work[:, 5120:6144].rearrange("p (a n) -> p a n", a=2)
        hh = work[:, 6144:7168].rearrange("p (a n) -> p a n", a=2)
        yg = work[:, 7168:8192]
        SEL = work[:, 8192:8448].rearrange("p (b n) -> p b n", b=2)
        SELT = work[:, 8448:8704]
        RT = work[:, 8704:8768].rearrange("p (k n) -> p k n", k=KD)
        rs = work[:, 8768:9024]
        tab = work[:, 9024:9024 + 6 * (NE + 1)].rearrange("p (t b e) -> p t b e", t=3, b=LB)
        zero16 = work[:, 9216:9472].bitcast(BF16)
        anb, qgb, kgb = mixc[:, 0:512], mixc[:, 512:640], mixc[:, 640:768]
        wsT = mixc[:, 768:1280].rearrange("p (g i) -> p g i", g=4)
        XC = X[:, 2:4, :].rearrange("p b d -> p (b d)")
        sgf = tmp[:, :].rearrange("p (a n) -> p a n", a=2)
        fh = ah[:, 0:1024].rearrange("p (a t) -> p a t", a=2)
        fl = al[:, 0:1024].rearrange("p (a t) -> p a t", a=2)
        cqh, cql = (t[:, 0:768].rearrange("p (k t) -> p k t", k=3) for t in (ah, al))
        ckh, ckl = (t[:, 768:1792].rearrange("p (k t) -> p k t", k=2) for t in (ah, al))
        och, ocl = (t[:, 2048:4096].rearrange("p (k t) -> p k t", k=8) for t in (ah, al))
        xgh, xgl = (t[:, 0:1024].rearrange("p (k t) -> p k t", k=KD) for t in (ah, al))
        hth, htl = (t[:, 1024:2048].rearrange("p (a t) -> p a t", a=2) for t in (ah, al))

        s = {}
        for name in """consts_loaded pack_loaded x_loaded bias_loaded mixc_loaded gpost_loaded gg_loaded gg_stored0 gg_stored1
                rt_loaded out_stored
                pack_turned vec_ready silu_ready act_high act_ready rows_copied cols_done cols_ready
                gate_done gate_made ws_turned ws_ready dve_step
                gelu_made q_copied kv_copied gn_ms gn_root vn_ready mix_done gated cat_turned
                cat_high cat_low qk_turned qk_ready qn_ready kn_ready
                g_done u_done silu_made hid_made fd_high fd_ready fd_used
                c_copied c_turned c_scaled c_high c_ready kr_ready kr_turned kr_copied
                qr_done qr_copied qr_ready qr_turned qr_moved qn_done qn_moved kv_done kv_moved
                logits_done route1 route_exp mask_made pos_done route_ready
                sel_made gathered selt_done xg_scaled xg_high xg_ready selt_copied
                esilu_made h_made ht_done ht_high ht_ready y_gated scattered acc_made
                resid_done squared mean_made root_made""".split():
            s[name] = sem(name)

        PRE = [(NB, 0, 0), (NB, 0, 1), (NB, 1, 0), (LB, 1, 1)]
        pre = [{n: sem(f"pre{i}_{n}") for n in "xn turned scaled high low".split()} for i in range(4)]
        RES = [(NB, 0), (NB, 2), (LB, 4), (LB, 5)]
        squares = [0]
        for i in range(4):
            squares += [squares[-1] + PRE[i][0], squares[-1] + PRE[i][0] + RES[i][0]]
        att = [{n: sem(f"att{i}_{n}") for n in "scored bias exp p turned pt o high low".split()} for i in range(2)]

        SS, MS, RSTD = 0, 4, 8

        def pre_act(act, i):
            nb = PRE[i][0]
            m = pre[i]
            if i == 0:
                act.wait_ge(s["x_loaded"], 32)
            else:
                act.wait_ge(s["resid_done"], [0, 4, 8, 10][i])
            for b in range(nb):
                if b:
                    act.wait_ge(s["squared"], squares[2 * i] + b)
                act.activation(tmp[:, :], X[:, b, :], ACT.Square, accum_out=sc[:, SS + b:SS + b + 1]).then_inc(s["squared"], 1)
            act.wait_ge(s["mean_made"], 2 * i + 1)
            act.activation(sc[:, MS:MS + nb], sc[:, MS:MS + nb], ACT.Sqrt).then_inc(s["root_made"], 1)
            for k in range(KD):
                act.wait_ge(m["scaled"], k + 1)
                act.activation(ahk[:, k, 0:nb * P], tmp[:, (k % 2) * 512:(k % 2) * 512 + nb * P], ACT.Copy).then_inc(m["high"], 1)

        def pre_dve(dve, i, link):
            nb, layer, place = PRE[i]
            m = pre[i]
            dve.wait_ge(s["squared"], squares[2 * i] + nb)
            dve.tensor_scalar(sc[:, MS:MS + nb], sc[:, SS:SS + nb], 1.0 / D, EPS, ALU.mult, ALU.add).then_inc(s["mean_made"], 1)
            dve.wait_ge(s["root_made"], 2 * i + 1)
            link(dve.reciprocal(sc[:, RSTD:RSTD + nb], sc[:, MS:MS + nb]))
            for b in range(nb):
                dve.tensor_scalar(xn[:, b, :], X[:, b, :], sc[:, RSTD + b:RSTD + b + 1], None, ALU.mult).then_inc(m["xn"], 1)

            def lower(k):
                dve.wait_ge(m["high"], k + 1)
                dve.tensor_tensor(alk[:, k, 0:nb * P], tmp[:, (k % 2) * 512:(k % 2) * 512 + nb * P],
                                  ahk[:, k, 0:nb * P].bitcast(F32), ALU.subtract).then_inc(m["low"], 1)

            if i == 0:
                dve.wait_ge(s["cols_ready"], 2)
            for k in range(KD):
                dve.wait_ge(m["turned"], k + 1)
                if k >= 2:
                    dve.wait_ge(m["low"], k - 1)
                for st in range(nb // LB):
                    last = dve.tensor_scalar(tmp[:, (k % 2) * 512 + st * SEQ:(k % 2) * 512 + (st + 1) * SEQ],
                                             PS[:, k % 2, st * SEQ:(st + 1) * SEQ],
                                             scol[:, layer, place, k, st:st + 1], modc[:, layer, place, 0, k, st:st + 1],
                                             ALU.mult, ALU.add)
                last.then_inc(m["scaled"], 1)
                if k:
                    lower(k - 1)
            lower(KD - 1)

        def pre_pe(pe, i):
            nb = PRE[i][0]
            m = pre[i]
            pe.wait_ge(m["xn"], nb)
            for k in range(KD):
                if k >= 2:
                    pe.wait_ge(m["scaled"], k - 1)
                for b in range(nb):
                    last = pe.transpose(PS[:, k % 2, b * P:(b + 1) * P], xn[:, b, k * P:(k + 1) * P], ident)
                last.then_inc(m["turned"], 1)

        def res_act(act, i, y, done):
            nb = RES[i][0]
            act.wait_ge(*done)
            for b in range(nb):
                if b:
                    act.wait_ge(s["squared"], squares[2 * i + 1] + b)
                act.activation(tmp[:, :], y(b), ACT.Square, accum_out=sc[:, SS + b:SS + b + 1]).then_inc(s["squared"], 1)
            act.wait_ge(s["mean_made"], 2 * i + 1 + 1)
            act.activation(sc[:, MS:MS + nb], sc[:, MS:MS + nb], ACT.Sqrt).then_inc(s["root_made"], 1)

        def res_dve(dve, i, y, gate, link):
            nb = RES[i][0]
            dve.wait_ge(s["squared"], squares[2 * i + 1] + nb)
            dve.tensor_scalar(sc[:, MS:MS + nb], sc[:, SS:SS + nb], 1.0 / D, EPS, ALU.mult, ALU.add).then_inc(s["mean_made"], 1)
            dve.wait_ge(s["root_made"], 2 * i + 1 + 1)
            link(dve.reciprocal(sc[:, RSTD:RSTD + nb], sc[:, MS:MS + nb]))
            dve.wait_ge(s["gg_loaded"], 16 * (i + 1))
            for b in range(nb):
                link(dve.scalar_tensor_tensor(out=tmp[:, :], in0=y(b), scalar=sc[:, RSTD + b:RSTD + b + 1],
                                              in1=gate(b), op0=ALU.mult, op1=ALU.mult))
                dve.tensor_tensor(X[:, b, :], X[:, b, :], tmp[:, :], ALU.add).then_inc(s["resid_done"], 1)
                link.after_resid()

        def ps_rows(b):
            return PS[:, 2 * b:2 * b + 2, :].rearrange("p a n -> p (a n)")

        PB = [work[:, 4096:5120], XC[:, 0:1024]]
        PT = [[work[:, 6144:7168], work[:, 7168:8192]], [tmp[:, :], mixc[:, 0:1024]]]
        qrT = XC[:, 1024:2048].rearrange("p (h t) -> p h t", h=4)
        ATT = [dict(n=16, scale=HD ** -0.5), dict(n=16, scale=(HD + CROPE) ** -0.5)]
        MX, NBI, SUM, REC = 16, 32, 48, 64

        def att_keys(a, i):
            return (0, NTOK) if a == 1 or i < 8 else (SEQ, CTX)

        def att_pe(pe, a):
            m = att[a]
            n = ATT[a]["n"]

            def scores(i):
                k0, nk = att_keys(a, i)
                if i >= 2:
                    pe.wait_ge(m["exp"], i - 1)
                o = PS[:, i % 2, 0:nk]
                if a == 0:
                    h, t0 = (i // 2) % 4, (SEQ if i >= 8 else 0) + (i % 2) * P
                    last = pe.matmul(o, qT[:, h, t0:t0 + P], kT[:, h // 2, k0:k0 + nk], start=True, stop=True)
                else:
                    h, t0, r = i // 2, (i % 2) * P, 64 * ((i // 2) % 2)
                    pe.matmul(o, qnT[:, h, t0:t0 + P], knT[:, h, :], start=True, stop=False)
                    last = pe.matmul(o, qrT[r:r + 64, h // 2, t0:t0 + P], krT[r:r + 64, :], start=False, stop=True)
                last.then_inc(m["scored"], 1)

            def turn(i):
                k0, nk = att_keys(a, i)
                pe.wait_ge(m["p"], i + 1)
                if i >= 2:
                    pe.wait_ge(m["pt"], i - 1)
                for k in range(nk // P):
                    last = pe.transpose(PS[:, 2 + i % 2, k * P:(k + 1) * P],
                                        PB[a][:, (i % 2) * 512 + k * P:(i % 2) * 512 + (k + 1) * P], ident)
                last.then_inc(m["turned"], 1)

            def values(h):
                k0, nk = att_keys(a, 2 * h)
                pe.wait_ge(m["pt"], 2 * h + 2)
                if h >= 2:
                    pe.wait_ge(m["low"], h - 1)
                pt = PT[a][h % 2].rearrange("p (k q) -> p k q", k=4)
                for k in range(nk // P):
                    kb = k0 // P + k
                    v = KV[:, kb, 256 + ((h % 4) // 2) * P:256 + ((h % 4) // 2 + 1) * P] if a == 0 else V1[:, kb, h * P:(h + 1) * P]
                    last = pe.matmul(PS[:, 4 + h % 2, 0:256], v, pt[:, k, :], start=(k == 0), stop=(k == nk // P - 1))
                last.then_inc(m["o"], 1)

            for i in range(n + 3):
                if i < n:
                    scores(i)
                if 2 <= i < n + 2:
                    turn(i - 2)
                if i >= 3 and (i - 3) % 2 == 1:
                    values((i - 3) // 2)

        def att_out(a, h, t):
            if a == 0:
                return t[0][:, 4 + h % 4, (h // 4) * SEQ:(h // 4 + 1) * SEQ]
            return t[1][:, h, :]

        def att_act(act, a):
            m = att[a]
            n = ATT[a]["n"]

            def exp(i):
                nk = att_keys(a, i)[1]
                act.wait_ge(m["bias"], i + 1)
                if i >= 2:
                    act.wait_ge(m["turned"], i - 1)
                act.activation(PB[a][:, (i % 2) * 512:(i % 2) * 512 + nk], PS[:, i % 2, 0:nk], ACT.Exp,
                               bias=sc[:, NBI + i:NBI + i + 1], scale=ATT[a]["scale"],
                               accum_out=sc[:, SUM + i:SUM + i + 1]).then_inc(m["exp"], 1)

            def copy(i):
                nk = att_keys(a, i)[1]
                h = i // 2
                act.wait_ge(m["turned"], i + 1)
                if h >= 2:
                    act.wait_ge(m["o"], h - 1)
                pt = PT[a][h % 2].rearrange("p (k q) -> p k q", k=4)
                act.activation(pt[:, 0:nk // P, (i % 2) * P:(i % 2 + 1) * P],
                               PS[:, 2 + i % 2, 0:nk].rearrange("p (k q) -> p k q", q=P), ACT.Copy).then_inc(m["pt"], 1)

            def upper(h):
                act.wait_ge(m["o"], h + 1)
                act.activation(att_out(a, h, (ahk, och)), PS[:, 4 + h % 2, 0:256], ACT.Copy).then_inc(m["high"], 1)

            for i in range(n + 3):
                if i < n:
                    exp(i)
                if 2 <= i < n + 2:
                    copy(i - 2)
                if i >= 3 and (i - 3) % 2 == 1:
                    upper((i - 3) // 2)

        def att_dve(dve, a, link):
            m = att[a]
            n = ATT[a]["n"]

            def peak(i):
                nk = att_keys(a, i)[1]
                dve.wait_ge(m["scored"], i + 1)
                link(dve.tensor_reduce(sc[:, MX + i:MX + i + 1], PS[:, i % 2, 0:nk], AXX, ALU.max))
                dve.tensor_scalar(sc[:, NBI + i:NBI + i + 1], sc[:, MX + i:MX + i + 1], -ATT[a]["scale"], None,
                                  ALU.mult).then_inc(m["bias"], 1)

            def norm(i):
                nk = att_keys(a, i)[1]
                dve.wait_ge(m["exp"], i + 1)
                link(dve.reciprocal(sc[:, REC + i:REC + i + 1], sc[:, SUM + i:SUM + i + 1]))
                p = PB[a][:, (i % 2) * 512:(i % 2) * 512 + nk]
                dve.tensor_scalar(p, p, sc[:, REC + i:REC + i + 1], None, ALU.mult).then_inc(m["p"], 1)

            def lower(h):
                dve.wait_ge(m["high"], h + 1)
                dve.tensor_tensor(att_out(a, h, (alk, ocl)), PS[:, 4 + h % 2, 0:256],
                                  att_out(a, h, (ahk, och)).bitcast(F32), ALU.subtract).then_inc(m["low"], 1)

            for i in range(n + 3):
                if i < n:
                    peak(i)
                if 1 <= i < n + 1:
                    norm(i - 1)
                if i >= 3 and (i - 3) % 2 == 1:
                    lower((i - 3) // 2)

        def row(l, part, k):
            ch = 12 * l + 2 * part + k // 4
            return ch % 3, (ch // 3) * 512 + (k % 4) * P

        def rows_of(w):
            return w.rearrange("(k p) n -> p k n", p=P)

        abin, about = rows_of(ab_w_in[0]), rows_of(ab_w_out[0])
        fin, fout = rows_of(ffn_w_in[0]), rows_of(ffn_w_out[0])
        wdq, wdkv, wuq, wukv, wo = (rows_of(w[0]) for w in (mla_w_dq, mla_w_dkv, mla_w_uq, mla_w_ukv, mla_w_o))
        MLA_W = [4 * CQ] * 2 + [4 * (CKV + CROPE)] * 2 + [1536] * 3 + [2048] * 2 + [2048] * 4

        def mla_src(j):
            if j < 2:
                return wdq[:, 4 * j:4 * j + 4, :]
            if j < 4:
                return wdkv[:, 4 * (j - 2):4 * (j - 2) + 4, :]
            if j < 7:
                return wuq[:, j - 4:j - 3, :]
            if j < 9:
                return wukv[:, j - 7:j - 6, :]
            return wo[:, 2 * (j - 9):2 * (j - 9) + 2, :]

        NV = NE

        U0 = N_MOE
        UC = N_MOE + 4

        block = es.enter_context(nc.Block())

        @block.sync
        def _(sp):
            sp.dma_start(K[:, :], consts).then_inc(s["consts_loaded"], 16)
            pk = tmp[:, 0:P]
            for r, n, src in ((0, 8, c[0].rearrange("(k p) -> k p", p=P)), (8, 8, c_ctx.rearrange("(k p) -> k p", p=P)),
                              (16, 16, g_pre_mix.rearrange("l (k p) -> (l k) p", p=P)),
                              (32, 16, g_pre_ffn.rearrange("l (k p) -> (l k) p", p=P)),
                              (48, 3, mla_qnorm_g[0].rearrange("(k p) -> k p", p=P)),
                              (51, 2, mla_kvnorm_g[0].rearrange("(k p) -> k p", p=P)), (53, 4, a_bs[0])):
                sp.dma_start(pk[r:r + n, :], src).then_inc(s["pack_loaded"], 16)

            def ada_group(layer, n, it, col):
                w = rows_of(ada_w[layer])
                for q in range(3):
                    for kh in range(2):
                        load_unit(sp, n + 2 * q + kh, w[:, 4 * kh:4 * kh + 4, bass.ds(col + q * 512, 512)], it)

            ada_group(0, N_ADA, 0, 0)
            with sp.Fori(0, 3) as i:
                ada_group(0, N_ADA + 6, i, i * 1536 + 1536)
            with sp.Fori(0, 4) as i:
                ada_group(1, N_ADA + 24, i, i * 1536)
            for j in range(8):
                load_unit(sp, N_ABIN + j, abin[:, 4 * (j % 2):4 * (j % 2) + 4, (j // 2) * 512:(j // 2 + 1) * 512])
            for j in range(4):
                load_unit(sp, N_ABOUT + j, about[:, 2 * j:2 * j + 2, :])

            def fin_pair(n, it, col):
                load_unit(sp, n, fin[:, :, bass.ds(col, 256)], it)
                load_unit(sp, n + 1, fin[:, :, bass.ds(col + D_FF, 256)], it)

            with sp.Fori(0, 3) as i:
                for j in range(3):
                    fin_pair(N_FIN + 2 * j, i, i * 768 + j * 256)
            for j in range(9, 11):
                fin_pair(N_FIN + 2 * j, 0, j * 256)
            for j in range(11):
                load_unit(sp, N_FOUT + j, fout[:, 2 * j:2 * j + 2, :])
            for j in range(13):
                load_unit(sp, N_MLA + j, mla_src(j))

            def visit(v, e):
                wi, wo_ = rows_of(moe_w_in[0, e]), rows_of(moe_w_out[0, e])

                def up(n, it, col):
                    for j in range(4):
                        load_unit(sp, n + j, wi[:, 4 * (j % 2):4 * (j % 2) + 4, bass.ds(col + (j // 2) * D_FFE, FCH)], it)

                def down(n, it, blk):
                    for j in range(2):
                        load_unit(sp, n + j, wo_[:, bass.ds(blk + 2 * j, 2), :], it)

                up(U0, v * NCH, 0)
                with sp.Fori(0, 3) as i:
                    for j in range(2):
                        up(UC + 6 * j, v * NCH + i * 2, i * 1024 + (j + 1) * FCH)
                        down(UC + 4 + 6 * j, v * NCH + i * 2, i * 8 + j * 4)
                down(UC + 36, v * NCH, 24)

            with sp.Fori(0, NE) as e:
                visit(e, e)
            sp.wait_ge(s["route_ready"], 1)
            with sp.Fori(0, NE) as e:
                n = sp.value_load(cnt[0:1, bass.ds(e, 1)], min_val=0, max_val=SEQ)
                with sp.If(n > P):
                    visit(e + NV, e)
                with sp.Else():
                    for j in range(6):
                        r = (N_MOE + j) % RAW
                        sp.wait_ge(raw_loaded[r], 16 * ((N_MOE + j) // RAW) + (e + NV) * (16 * NCH))
                        sp.sem_inc(raw_loaded[r], 16 * NCH)
            for b in range(LB):
                sp.wait_ge(s["resid_done"], 11 + b)
                sp.dma_start(out[0, b * P:(b + 1) * P, :], X[:, b, :]).then_inc(s["out_stored"], 16)
            sp.wait_ge(s["out_stored"], 16 * LB)

        @block.gpsimd
        def _(pool):
            assert N_ADA == 0
            pool_low(pool, 2)
            pool_low(pool, 5)
            with pool.Fori(0, 7) as i:
                pool_low(pool, 8, i)
                pool_low(pool, 11, i)
            for n in range(N_ABIN, N_FIN):
                if n % SPL == SPL - 1:
                    pool_low(pool, n)
            with pool.Fori(0, 3) as i:
                pool_low(pool, N_FIN + 2, i)
                pool_low(pool, N_FIN + 5, i)
            for n in range(N_FIN + 18, N_MOE):
                if n % SPL == SPL - 1:
                    pool_low(pool, n, 0, MLA_W[n - N_MLA] if n >= N_MLA else UNIT)
            first = next(n for n in range(N_MOE, N_MOE + 3) if n % SPL == SPL - 1)
            with pool.Fori(0, NE) as e:
                with pool.Fori(0, NCH) as i:
                    pool_low(pool, first, e * NCH + i)
                    pool_low(pool, first + 3, e * NCH + i)
            pool.wait_ge(s["route_ready"], 1)
            with pool.Fori(0, NE) as e:
                n = pool.value_load(cnt[0:1, bass.ds(e, 1)], min_val=0, max_val=SEQ)
                with pool.If(n > P):
                    with pool.Fori(0, NCH) as i:
                        pool_low(pool, first, (e + NV) * NCH + i)
                        pool_low(pool, first + 3, (e + NV) * NCH + i)
                with pool.Else():
                    pool.wait_ge(low_made[SPL - 1], 2 * (first // SPL) + (e + NV) * (4 * NCH))
                    pool.sem_inc(low_made[SPL - 1], 2 * NCH)

        @block.scalar
        def _(act):
            for b, src in enumerate((x[0], ctx[0])):
                act.dma_start(X[:, 2 * b:2 * b + 2, :], src.rearrange("(b p) d -> p b d", p=P)).then_inc(s["x_loaded"], 16)
            for q in range(3):
                act.dma_start(modrows[32 * q + 4:32 * q + 5, :].rearrange("p (l a n) -> p l a n", l=2, n=512),
                              ada_b.rearrange("l (a q n) -> q l a n", q=3, n=512)[q:q + 1]).then_inc(s["bias_loaded"], 16)
            for j, g in enumerate((g_post_mix, g_post_ffn)):
                for l in range(2):
                    act.dma_start(gpost[:, 2 * j + l, :], g[l].partition_broadcast(P)).then_inc(s["gpost_loaded"], 16)
            act.dma_start(anb, a_norm_g[0].partition_broadcast(P)).then_inc(s["mixc_loaded"], 16)
            act.dma_start(qgb, b_qnorm_g[0].partition_broadcast(P)).then_inc(s["mixc_loaded"], 16)
            act.dma_start(kgb, b_knorm_g[0].partition_broadcast(P)).then_inc(s["mixc_loaded"], 16)
            act.dma_start(work[:, 10240:10752].rearrange("p (g i) -> p g i", g=4),
                          a_ws[0].rearrange("g i j -> i g j")).then_inc(s["mixc_loaded"], 16)

            act.wait_ge(s["pack_turned"], 1)
            act.activation(sil[:, :, :].rearrange("p s k -> p (s k)"), PS[:, 7, 0:16], ACT.Silu).then_inc(s["silu_ready"], 1)
            act.wait_ge(s["silu_ready"], 1)
            act.activation(act4[:, :, 0:2], sil[:, :, :].rearrange("p s k -> p k s"), ACT.Copy).then_inc(s["act_high"], 1)
            for n in range(6):
                split_high(act, n)
            with act.Fori(0, 7) as i:
                for j in range(6):
                    split_high(act, 6 + j, i)
            for n in range(N_ABIN, N_ABIN + 3):
                split_high(act, n)
            for i in range(6):
                act.wait_ge(s["gate_made"], i + 1)
                act.dma_start(gg_dram[i], ggmake[:, i % 2, :]).then_inc(s[f"gg_stored{i % 2}"], 16)

            pre_act(act, 0)
            for ch in range(4):
                for j in range(3 if ch == 0 else 2 * ch + 3, min(2 * ch + 5, 8)):
                    split_high(act, N_ABIN + j)
                act.wait_ge(unit_used, N_ABIN + 2 * ch + 2)
                for b in range(NB):
                    src = PS[:, (ch % 2) * 4 + b, :]
                    if ch < 2:
                        act.activation((U, V)[ch][:, b, :], src, ACT.Gelu_apprx_tanh).then_inc(s["gelu_made"], 1)
                    else:
                        act.activation((Q, KV)[ch - 2][:, b, :], src, ACT.Copy).then_inc(s[("q_copied", "kv_copied")[ch - 2]], 1)
                if ch >= 2:
                    act.wait_ge(s["gn_ms"], ch - 1)
                    act.activation(sc[:, 96:112], sc[:, 96:112], ACT.Sqrt).then_inc(s["gn_root"], 1)
            for g in range(4):
                act.wait_ge(s["cat_turned"], g + 1)
                act.activation(ahk[:, g, :], PS[:, 2 + g % 2, :], ACT.Copy).then_inc(s["cat_high"], 1)
            for n in range(N_ABOUT, N_ABOUT + 3):
                split_high(act, n)
            for h in range(6):
                if h == 4:
                    act.wait_ge(s["gn_ms"], 3)
                    act.activation(sc[:, 96:104], sc[:, 96:104], ACT.Sqrt).then_inc(s["gn_root"], 1)
                act.wait_ge(s["qk_turned"], h + 1)
                act.activation(qT[:, h, :] if h < 4 else kT[:, h - 4, :], PS[:, 6 + h % 2, :], ACT.Copy).then_inc(s["qk_ready"], 1)
            att_act(act, 0)
            act.wait_ge(att[0]["o"], 8)
            act.dma_start(GG, gg_dram[0:2].rearrange("a p n -> p a n")).then_inc(s["gg_loaded"], 16)
            split_high(act, N_ABOUT + 3)
            for n in range(N_FIN, N_FIN + 3):
                split_high(act, n)
            res_act(act, 0, ps_rows, (unit_used, N_ABOUT + 4))

            pre_act(act, 1)

            def ffn_silu(f0, it):
                if f0 % 2 == 0:
                    act.wait_ge(s["g_done"], f0 // 2 + 1 + it * 3)
                else:
                    act.wait_ge(unit_used, N_FIN + f0 + it * 6)
                if f0 >= 2:
                    act.wait_ge(s["hid_made"], f0 - 1 + it * 6)
                act.activation(sgf[:, f0 % 2, :], PS[:, 2 * (f0 % 2), :], ACT.Silu).then_inc(s["silu_made"], 1)

            for j in range(6):
                ffn_silu(j, 0)
                split_high(act, N_FIN + j + 3)
            with act.Fori(0, 2) as i:
                for j in range(6):
                    ffn_silu(6 + j, i)
                    split_high(act, N_FIN + 6 + j + 3, i)
            for j in range(18, 22):
                ffn_silu(j, 0)
                split_high(act, N_FIN + j + 3)
            act.wait_ge(unit_used, N_FIN + 22)
            for d in range(11):
                for f in (2 * d, 2 * d + 1):
                    act.wait_ge(s["hid_made"], f + 1)
                    if d and f % 2 == 0:
                        act.wait_ge(s["fd_used"], d)
                    elif d:
                        act.wait_ge(unit_used, N_FOUT + d)
                    act.activation(fh[:, f % 2, :], HID[:, f, :], ACT.Copy).then_inc(s["fd_high"], 1)
                n = N_FOUT + d + 3
                split_high(act, n, 0, UNIT if n < N_MLA else MLA_W[n - N_MLA])
            act.wait_ge(s["fd_ready"], 22)
            act.dma_start(GG, gg_dram[2:4].rearrange("a p n -> p a n")).then_inc(s["gg_loaded"], 16)
            res_act(act, 1, ps_rows, (unit_used, N_FOUT + 11))

            pre_act(act, 2)
            split_high(act, N_MLA + 3, 0, MLA_W[3])
            act.wait_ge(unit_used, N_MLA + 2)
            for b in range(2):
                act.activation(cqn[:, b, :], PS[:, b, 0:CQ], ACT.Copy).then_inc(s["c_copied"], 1)
            act.wait_ge(unit_used, N_MLA + 4)
            for b in range(NB):
                act.activation(ckvn[:, b, :], PS[:, 2 + b, 0:CKV], ACT.Copy).then_inc(s["c_copied"], 1)
                act.activation(kr2[:, b, 0:CROPE], PS[:, 2 + b, CKV:CKV + CROPE], ACT.Copy).then_inc(s["c_copied"], 1)
            for n in range(N_MLA + 4, N_MLA + 7):
                split_high(act, n, 0, MLA_W[n - N_MLA])
            act.wait_ge(s["gn_ms"], 4)
            act.activation(sc[:, 96:102], sc[:, 96:102], ACT.Sqrt).then_inc(s["gn_root"], 1)
            for k in range(5):
                act.wait_ge(s["c_scaled"], k + 1)
                dst = cqh[:, k, :] if k < 3 else ckh[:, k - 3, :]
                act.activation(dst, tmp[:, (k % 2) * 512:(k % 2) * 512 + (256 if k < 3 else 512)], ACT.Copy).then_inc(s["c_high"], 1)
            act.wait_ge(s["kr_turned"], 1)
            act.activation(krT, PS[:, 7, :], ACT.Copy).then_inc(s["kr_copied"], 1)
            for b in range(2):
                act.wait_ge(s["qr_done"], b + 1)
                act.activation(qrt[:, b, :], PS[:, b, :], ACT.Copy).then_inc(s["qr_copied"], 1)
            for h in range(8):
                act.wait_ge(*((s["qn_done"], h + 1) if h < 7 else (unit_used, N_MLA + 7)))
                act.activation(qnT[:, h, :], PS[:, 2 + h % 4, 0:256], ACT.Copy).then_inc(s["qn_moved"], 1)
            for n in range(N_MLA + 7, N_MLA + 9):
                split_high(act, n, 0, MLA_W[n - N_MLA])
            for p in range(4):
                act.wait_ge(s["qr_turned"], p + 1)
                act.activation(qrT[:, p, :], PS[:, 6 + p % 2, 0:256], ACT.Copy).then_inc(s["qr_moved"], 1)
            for j in range(16):
                act.wait_ge(*((s["kv_done"], j + 1) if j < 15 else (unit_used, N_MLA + 9)))
                dst = knT[:, j, :] if j < 8 else V1[:, (j - 8) // 2, ((j - 8) % 2) * 512:((j - 8) % 2 + 1) * 512]
                act.activation(dst, PS[:, j % 6, :], ACT.Copy).then_inc(s["kv_moved"], 1)
            for n in range(N_MLA + 9, N_MLA + 12):
                split_high(act, n)
            att_act(act, 1)
            act.wait_ge(att[1]["o"], 8)
            act.dma_start(GGm, gg_dram[4]).then_inc(s["gg_loaded"], 16)
            split_high(act, N_MLA + 12)
            res_act(act, 2, ps_rows, (unit_used, N_MLA + 13))

            act.dma_start(RT, moe_router[0].rearrange("(k p) e -> p k e", p=P)).then_inc(s["rt_loaded"], 16)
            pre_act(act, 3)
            act.wait_ge(s["resid_done"], 10)
            act.dma_start(GGm, gg_dram[5]).then_inc(s["gg_loaded"], 16)
            act.wait_ge(s["route1"], 1)
            act.activation(rs[:, 32:34], rs[:, 32:34], ACT.Exp).then_inc(s["route_exp"], 1)

            def tokens(g, hf):
                act.wait_ge(s["xg_scaled"], g * 2 + hf + 1)
                act.activation(xgh[:, 4 * hf:4 * hf + 4, :].rearrange("p k t -> p (k t)"),
                               tmp[:, hf * 512:(hf + 1) * 512], ACT.Copy).then_inc(s["xg_high"], 1)

            def visit(v, chained):
                split_high(act, U0 + 3, v * NCH)
                silu(U0 + 2, v * NCH, 0)

                def body(n, it, par):
                    for j in range(3):
                        split_high(act, n + j, it)
                    turned(it + (n - UC) // 6 + 1, 1 - par)
                    for j in range(3, 5):
                        split_high(act, n + j, it)
                    silu(n + 2, it, par)
                    split_high(act, n + 5, it)

                with act.Fori(0, 3) as i:
                    body(UC, v * NCH + i * 2, 1)
                    body(UC + 6, v * NCH + i * 2, 0)
                split_high(act, UC + 36, v * NCH)
                split_high(act, UC + 37, v * NCH)
                if chained:
                    with act.If(v < NE - 1):
                        split_high(act, U0, v * NCH + NCH)
                turned(v * NCH + NCH, 0)
                if chained:
                    for hf in range(2):
                        tokens(v + 1, hf)

            def silu(n, it, par):
                act.wait_ge(unit_used, n + it * 6)
                act.activation(sg[:, par, :], PS[:, 2 * par, :], ACT.Silu).then_inc(s["esilu_made"], 1)

            def turned(count, par):
                act.wait_ge(s["ht_done"], count)
                act.activation(hth[:, par, :], PS[:, 4, :], ACT.Copy).then_inc(s["ht_high"], 1)

            for j in range(3):
                split_high(act, U0 + j)
            for hf in range(2):
                tokens(0, hf)
            with act.Fori(0, NE) as e:
                visit(e, True)
                with act.If(e < NE - 1):
                    for j in range(1, 3):
                        split_high(act, U0 + j, e * NCH + NCH)
            act.wait_ge(s["route_ready"], 1)
            with act.Fori(0, NE) as e:
                n = act.value_load(cnt[0:1, bass.ds(e, 1)], min_val=0, max_val=SEQ)
                v = e + NV
                with act.If(n > P):
                    for j in range(3):
                        split_high(act, U0 + j, v * NCH)
                    for hf in range(2):
                        tokens(v + 1, hf)
                    visit(v, False)
                with act.Else():
                    act.wait_ge(high_made, N_MOE + v * VISIT)
                    act.sem_inc(high_made, VISIT)
                    for name, k, more in (("xg_high", 2, 2), ("esilu_made", NCH, 0), ("ht_high", NCH, 0)):
                        act.wait_ge(s[name], v * k + more)
                        act.sem_inc(s[name], k)
            res_act(act, 3, lambda b: ACC[:, b, :], (s["acc_made"], 2 * NE + 2))

        @block.vector
        def _(dve):
            class Link:
                n = 0

                def __call__(self, ins):
                    ins.then_inc(s["dve_step"], 1)
                    self.n += 1
                    dve.wait_ge(s["dve_step"], self.n)

                resid = 0

                def after_resid(self):
                    self.resid += 1
                    dve.wait_ge(s["resid_done"], self.resid)

            link = Link()

            dve.wait_ge(s["pack_turned"], 1)
            dve.wait_ge(s["silu_ready"], 1)
            dve.tensor_copy(vec[:, 0:57], PS[:, 7, 0:57]).then_inc(s["vec_ready"], 1)
            dve.wait_ge(s["act_high"], 1)
            dve.tensor_tensor(act4[:, :, 2:4], sil[:, :, :].rearrange("p s k -> p k s"),
                              act4[:, :, 0:2].bitcast(F32), ALU.subtract).then_inc(s["act_ready"], 1)

            def ada_chunk(q, units, col):
                dve.wait_ge(unit_used, units)
                dve.tensor_copy(modrows[32 * q:32 * q + 4, bass.ds(col, 512)], PS[0:4, q, :]).then_inc(s["rows_copied"], 1)

            for q in range(3):
                for j in (2 * q, 2 * q + 1):
                    vector_low(dve, j)
                ada_chunk(q, 2 * q + 2, 0)
            with dve.Fori(0, 7) as i:
                for q in range(3):
                    for j in (2 * q, 2 * q + 1):
                        vector_low(dve, 6 + j, i)
                    ada_chunk(q, i * 6 + 8 + 2 * q, i * 512 + 512)
            dve.wait_ge(s["cols_done"], 1)
            for l in range(2):
                for w in range(2):
                    for t in range(2):
                        for kh in range(2):
                            o = 2 * (((l * 2 + w) * 2 + t) * KD + 4 * kh)
                            last = dve.tensor_copy(modc[:, l, w, t, 4 * kh:4 * kh + 4, :].rearrange("p k s -> p (k s)"),
                                                   PS[:, 5 + row(l, 3 * w + t, 4 * kh)[0], o:o + 8])
            last.then_inc(s["cols_ready"], 1)
            dve.wait_ge(s["cols_ready"], 1)
            for l in range(2):
                for w in range(2):
                    g = vec[:, 16 + 16 * w + 8 * l:24 + 16 * w + 8 * l].unsqueeze(2).broadcast_to([P, KD, 2])
                    last = dve.scalar_tensor_tensor(out=scol[:, l, w, :, :], in0=modc[:, l, w, 1, :, :], scalar=1.0,
                                                    in1=g, op0=ALU.add, op1=ALU.mult)
                    if (l, w) != (1, 1):
                        link(last)
            last.then_inc(s["cols_ready"], 1)
            dve.wait_ge(s["gpost_loaded"], 64)
            for i in range(6):
                dve.wait_ge(s["gate_done"], i + 1)
                if i >= 2:
                    dve.wait_ge(s[f"gg_stored{i % 2}"], 16 * (i // 2))
                gp = (0, 0, 2, 2, 1, 3)[i]
                dve.tensor_tensor(ggmake[:, i % 2, :], ps_rows(i % 2), gpost[:, gp, :], ALU.mult).then_inc(s["gate_made"], 1)
            dve.wait_ge(s["ws_turned"], 1)
            dve.tensor_copy(wsT, PS[:, 6, :].rearrange("p (g i) -> p g i", g=4)).then_inc(s["ws_ready"], 1)
            for n in range(N_ABIN, N_ABIN + 3):
                vector_low(dve, n)
            for i in range(2):
                dve.wait_ge(s[f"gg_stored{i}"], 48)

            pre_dve(dve, 0, link)

            def rope(t, heads, width, cc, ss, scr):
                f = width // 4
                v = t.rearrange("p (h a s f) -> p h a s f", a=2, s=2, f=f)
                w = scr.rearrange("p (h a s f) -> p h a s f", a=2, s=2, f=f)
                sv = ss.rearrange("p (a s f) -> p a s f", a=2, s=2)
                for a_ in range(2):
                    for s_ in range(2):
                        sin = sv[:, a_, s_, :].unsqueeze(1).broadcast_to([P, heads, f])
                        link(dve.tensor_tensor(w[:, :, a_, s_, :], v[:, :, a_, 1 - s_, :], sin, ALU.mult))
                th = t.rearrange("p (h w) -> p h w", h=heads)
                link(dve.tensor_tensor(th, th, cc.unsqueeze(1).broadcast_to([P, heads, width]), ALU.mult))
                return dve.tensor_tensor(t, t, scr, ALU.add)

            def mean_squares(v, groups):
                for h0 in range(0, groups, 8):
                    sq = tmp[:, :].rearrange("p (g d) -> p g d", g=8)
                    link(dve.tensor_tensor(sq, v[:, h0:h0 + 8, :], v[:, h0:h0 + 8, :], ALU.mult))
                    link(dve.tensor_reduce(sc[:, 96 + h0:104 + h0], sq, AXX, ALU.add))
                dve.tensor_scalar(sc[:, 96:96 + groups], sc[:, 96:96 + groups], 1.0 / P, EPS, ALU.mult, ALU.add).then_inc(s["gn_ms"], 1)

            for n in range(N_ABIN + 3, N_ABIN + 7):
                vector_low(dve, n)
            dve.wait_ge(s["gelu_made"], 8)
            dve.wait_ge(s["mixc_loaded"], 64)
            vg = V.rearrange("p b (g d) -> p (b g) d", d=P)
            mean_squares(vg, 16)
            vector_low(dve, N_ABIN + 7)
            dve.wait_ge(s["gn_root"], 1)
            link(dve.reciprocal(sc[:, 112:128], sc[:, 96:112]))
            link(dve.tensor_tensor(vg, vg, sc[:, 112:128].unsqueeze(2).broadcast_to([P, 16, P]), ALU.mult))
            dve.tensor_tensor(V, V, anb.unsqueeze(1).broadcast_to([P, NB, 512]), ALU.mult).then_inc(s["vn_ready"], 1)
            dve.wait_ge(s["q_copied"], NB)
            qg = Q.rearrange("p b (g d) -> p (b g) d", d=P)
            mean_squares(qg, 16)
            dve.wait_ge(s["gn_root"], 2)
            link(dve.reciprocal(sc[:, 112:128], sc[:, 96:112]))
            link(dve.tensor_tensor(qg, qg, sc[:, 112:128].unsqueeze(2).broadcast_to([P, 16, P]), ALU.mult))
            link(dve.tensor_tensor(qg, qg, qgb.unsqueeze(1).broadcast_to([P, 16, P]), ALU.mult))
            for b in range(LB):
                last = rope(Q[:, b, :], 4, HD, K[:, C_CB + b * HD:C_CB + (b + 1) * HD],
                            K[:, C_SB + b * HD:C_SB + (b + 1) * HD], tmp[:, 0:512])
                if b < LB - 1:
                    link(last)
            last.then_inc(s["qn_ready"], 1)
            for b in range(NB):
                dve.wait_ge(s["mix_done"], b + 1)
                for g in range(4):
                    last = dve.scalar_tensor_tensor(out=U[:, b, g * P:(g + 1) * P], in0=PS[:, b % 2, g * P:(g + 1) * P],
                                                    scalar=vec[:, 53 + g:54 + g], in1=U[:, b, g * P:(g + 1) * P],
                                                    op0=ALU.add, op1=ALU.mult)
                last.then_inc(s["gated"], 1)
            for g in range(4):
                dve.wait_ge(s["cat_high"], g + 1)
                dve.tensor_tensor(alk[:, g, :], PS[:, 2 + g % 2, :], ahk[:, g, :].bitcast(F32), ALU.subtract).then_inc(s["cat_low"], 1)
            dve.wait_ge(s["kv_copied"], NB)
            dve.wait_ge(s["qn_ready"], 1)
            kv4 = KV.rearrange("p b (g d) -> p b g d", d=P)[:, :, 0:2, :]
            sq = tmp[:, :].rearrange("p (b g d) -> p b g d", b=NB, g=2)
            kss = sc[:, 96:104].rearrange("p (b g) -> p b g", b=NB)
            link(dve.tensor_tensor(sq, kv4, kv4, ALU.mult))
            link(dve.tensor_reduce(kss, sq, AXX, ALU.add))
            dve.tensor_scalar(sc[:, 96:104], sc[:, 96:104], 1.0 / P, EPS, ALU.mult, ALU.add).then_inc(s["gn_ms"], 1)
            dve.wait_ge(s["gn_root"], 3)
            link(dve.reciprocal(sc[:, 112:120], sc[:, 96:104]))
            for b in range(NB):
                kb = kv4[:, b, :, :]
                link(dve.tensor_tensor(kb, kb, sc[:, 112 + 2 * b:114 + 2 * b].unsqueeze(2).broadcast_to([P, 2, P]), ALU.mult))
                last = dve.tensor_tensor(kb, kb, kgb.unsqueeze(1).broadcast_to([P, 2, P]), ALU.mult)
                if b < LB:
                    link(last)
                    last = rope(KV[:, b, 0:256], 2, HD, K[:, C_CB + b * HD:C_CB + (b + 1) * HD],
                                K[:, C_SB + b * HD:C_SB + (b + 1) * HD], tmp[:, 0:256])
                if b < NB - 1:
                    link(last)
            last.then_inc(s["kn_ready"], 1)
            for n in range(N_ABOUT, N_ABOUT + 3):
                vector_low(dve, n)
            att_dve(dve, 0, link)
            vector_low(dve, N_ABOUT + 3)
            for n in range(N_FIN, N_FIN + 3):
                vector_low(dve, n)
            res_dve(dve, 0, ps_rows, lambda b: GG[:, b // LB, :], link)

            pre_dve(dve, 1, link)

            def ffn_hidden(f0, f, it):
                dve.wait_ge(s["silu_made"], f0 + 1 + it * 6)
                if f0 % 2 == 0:
                    dve.wait_ge(s["u_done"], f0 // 2 + 1 + it * 3)
                else:
                    dve.wait_ge(unit_used, N_FIN + f0 + 1 + it * 6)
                dve.tensor_tensor(HID[:, bass.ds(f, 1), :].rearrange("p a t -> p (a t)"), sgf[:, f0 % 2, :],
                                  PS[:, 2 * (f0 % 2) + 1, :], ALU.mult).then_inc(s["hid_made"], 1)

            for j in range(6):
                ffn_hidden(j, j, 0)
                vector_low(dve, N_FIN + j + 3)
            with dve.Fori(0, 2) as i:
                for j in range(6):
                    ffn_hidden(6 + j, i * 6 + 6 + j, i)
                    vector_low(dve, N_FIN + 6 + j + 3, i)
            for j in range(18, 22):
                ffn_hidden(j, j, 0)
                vector_low(dve, N_FIN + j + 3)
            for d in range(11):
                for f in (2 * d, 2 * d + 1):
                    dve.wait_ge(s["fd_high"], f + 1)
                    dve.tensor_tensor(fl[:, f % 2, :], HID[:, f, :], fh[:, f % 2, :].bitcast(F32), ALU.subtract).then_inc(s["fd_ready"], 1)
                n = N_FOUT + d + 3
                vector_low(dve, n, 0, UNIT if n < N_MLA else MLA_W[n - N_MLA])
            res_dve(dve, 1, ps_rows, lambda b: GG[:, b // LB, :], link)

            pre_dve(dve, 2, link)
            vector_low(dve, N_MLA + 3, 0, MLA_W[3])
            dve.wait_ge(s["c_copied"], 10)
            link(dve.tensor_tensor(tmp[:, 0:768].rearrange("p (b n) -> p b n", b=2), cqn, cqn, ALU.mult))
            link(dve.tensor_reduce(sc[:, 96:98], tmp[:, 0:768].rearrange("p (b n) -> p b n", b=2), AXX, ALU.add))
            link(dve.tensor_tensor(tmp[:, :].rearrange("p (b n) -> p b n", b=NB), ckvn, ckvn, ALU.mult))
            link(dve.tensor_reduce(sc[:, 98:102], tmp[:, :].rearrange("p (b n) -> p b n", b=NB), AXX, ALU.add))
            link(dve.tensor_scalar(sc[:, 96:98], sc[:, 96:98], 1.0 / CQ, EPS, ALU.mult, ALU.add))
            dve.tensor_scalar(sc[:, 98:102], sc[:, 98:102], 1.0 / CKV, EPS, ALU.mult, ALU.add).then_inc(s["gn_ms"], 1)
            for n in range(N_MLA + 4, N_MLA + 7):
                vector_low(dve, n, 0, MLA_W[n - N_MLA])
            for b in range(LB):
                link(rope(kr2[:, b, 0:CROPE], 1, CROPE, K[:, C_CC + b * CROPE:C_CC + (b + 1) * CROPE],
                          K[:, C_SC + b * CROPE:C_SC + (b + 1) * CROPE], tmp[:, 0:CROPE]))
            dve.tensor_copy(kr2[:, :, CROPE:2 * CROPE], kr2[:, :, 0:CROPE]).then_inc(s["kr_ready"], 1)
            dve.wait_ge(s["gn_root"], 4)
            link(dve.reciprocal(sc[:, 112:118], sc[:, 96:102]))
            for b in range(2):
                link(dve.tensor_scalar(cqn[:, b, :], cqn[:, b, :], sc[:, 112 + b:113 + b], None, ALU.mult))
            for b in range(NB):
                last = dve.tensor_scalar(ckvn[:, b, :], ckvn[:, b, :], sc[:, 114 + b:115 + b], None, ALU.mult)
                if b < NB - 1:
                    link(last)
            last.then_inc(s["c_copied"], 1)

            def c_lower(k):
                w = 256 if k < 3 else 512
                d, u = (cql[:, k, :], cqh[:, k, :]) if k < 3 else (ckl[:, k - 3, :], ckh[:, k - 3, :])
                dve.wait_ge(s["c_high"], k + 1)
                dve.tensor_tensor(d, tmp[:, (k % 2) * 512:(k % 2) * 512 + w], u.bitcast(F32), ALU.subtract).then_inc(s["c_ready"], 1)

            for k in range(5):
                w = 256 if k < 3 else 512
                dve.wait_ge(s["c_turned"], k + 1)
                if k >= 2:
                    dve.wait_ge(s["c_ready"], k - 1)
                dve.tensor_scalar(tmp[:, (k % 2) * 512:(k % 2) * 512 + w], PS[:, 6 + k % 2, 0:w], vec[:, 48 + k:49 + k], None,
                                  ALU.mult).then_inc(s["c_scaled"], 1)
                if k:
                    c_lower(k - 1)
            c_lower(4)
            for b in range(LB):
                dve.wait_ge(s["qr_copied"], b + 1)
                last = rope(qrt[:, b, :], 8, CROPE, K[:, C_CC + b * CROPE:C_CC + (b + 1) * CROPE],
                            K[:, C_SC + b * CROPE:C_SC + (b + 1) * CROPE], rot[:, b * 512:(b + 1) * 512])
                last.then_inc(s["qr_ready"], 1)
            for n in range(N_MLA + 7, N_MLA + 12):
                vector_low(dve, n)
            att_dve(dve, 1, link)
            vector_low(dve, N_MLA + 12)
            res_dve(dve, 2, ps_rows, lambda b: GGm, link)

            pre_dve(dve, 3, link)
            link(dve.memset(zero16, 0.0))
            link(dve.memset(rs[:, 64:192], 1.0))
            link(dve.memset(tab, 0.0))
            dve.memset(SELT, 0.0)
            dve.memset(yg, 0.0).then_inc(s["y_gated"], 1)
            dve.memset(ACC, 0.0).then_inc(s["acc_made"], 1)
            LOG, TOP, IDX, OH, POS = 0, 16, 192, 208, 34
            dve.wait_ge(s["logits_done"], 1)
            link(dve.tensor_copy(rs[:, LOG:LOG + 16], PS[:, 0, 0:16]))
            for b in range(LB):
                lg = rs[:, LOG + 8 * b:LOG + 8 * b + 8]
                top = rs[:, TOP + 8 * b:TOP + 8 * b + 8]
                link(dve.max(top, lg))
                link(dve.max_index(rs[:, IDX + 8 * b:IDX + 8 * b + 8].bitcast(U32), top, lg))
                link(dve.tensor_tensor(rs[:, 32 + b:33 + b], top[:, 1:2], top[:, 0:1], ALU.subtract))
            idxf = sc[:, 128:144]
            dve.tensor_copy(idxf, rs[:, IDX:IDX + 16].bitcast(U32)).then_inc(s["route1"], 1)
            dve.wait_ge(s["route_exp"], 1)
            link(dve.tensor_scalar(rs[:, POS:POS + 2], rs[:, 32:34], 1.0, None, ALU.add))
            link(dve.reciprocal(sc[:, 146:148], rs[:, POS:POS + 2]))
            link(dve.tensor_tensor(sc[:, 148:150], sc[:, 146:148], rs[:, 32:34], ALU.mult))
            i8 = K[:, C_I8:C_I8 + NE]
            for b in range(LB):
                g, mk, oh = tab[:, 2, b, 0:NE], tab[:, 1, b, 0:NE], rs[:, OH:OH + 8]
                link(dve.tensor_scalar(g, i8, idxf[:, 8 * b:8 * b + 1], sc[:, 146 + b:147 + b], ALU.is_equal, ALU.mult))
                link(dve.tensor_scalar(oh, i8, idxf[:, 8 * b + 1:8 * b + 2], sc[:, 148 + b:149 + b], ALU.is_equal, ALU.mult))
                link(dve.tensor_tensor(g, g, oh, ALU.add))
                link(dve.tensor_scalar(mk, i8, idxf[:, 8 * b:8 * b + 1], None, ALU.is_equal))
                link(dve.tensor_scalar(oh, i8, idxf[:, 8 * b + 1:8 * b + 2], None, ALU.is_equal))
                last = dve.tensor_tensor(mk, mk, oh, ALU.add)
                if b < LB - 1:
                    link(last)
            last.then_inc(s["mask_made"], 1)
            gsel = sc[:, 152:154]
            gslot = sc[:, 154:155]
            dve.wait_ge(s["pos_done"], 1)
            link(dve.tensor_copy(tab[:, 0, :, 0:NE], PS[:, 1, 0:16].rearrange("p (b e) -> p b e", b=LB)))
            dve.tensor_copy(cnt[:, :], PS[:, 1, 16:24]).then_inc(s["route_ready"], 1)

            def low_units(n, it, js):
                for j in js:
                    vector_low(dve, n + j, it)

            def hidden(count, n, it, par):
                dve.wait_ge(s["esilu_made"], count)
                dve.wait_ge(unit_used, n + it * 6)
                dve.tensor_tensor(hh[:, par, :], sg[:, par, :], PS[:, 2 * par + 1, :], ALU.mult).then_inc(s["h_made"], 1)

            def turned(count, par):
                dve.wait_ge(s["ht_high"], count)
                dve.tensor_tensor(htl[:, par, :], PS[:, 4, :], hth[:, par, :].bitcast(F32), ALU.subtract).then_inc(s["ht_ready"], 1)

            def select(g, e, base):
                for b in range(LB):
                    dve.tensor_scalar(SEL[:, b, :], K[:, C_IOTA + base:C_IOTA + base + P],
                                      tab[:, 0, b, bass.ds(e, 1)], tab[:, 1, b, bass.ds(e, 1)], ALU.is_equal, ALU.mult)
                    last = dve.tensor_copy(gsel[:, b:b + 1], tab[:, 2, b, bass.ds(e, 1)])
                last.then_inc(s["sel_made"], 1)

            def scaled(g, hf):
                dve.wait_ge(s["gathered"], g * 2 + hf + 1)
                for k in range(4 * hf, 4 * hf + 4):
                    last = dve.tensor_scalar(tmp[:, k * P:(k + 1) * P], PS[:, 2 + hf, (k % 4) * P:(k % 4 + 1) * P],
                                             scol[:, 1, 1, k, 0:1], modc[:, 1, 1, 0, k, 0:1], ALU.mult, ALU.add)
                last.then_inc(s["xg_scaled"], 1)

            def tokens(g, hf):
                dve.wait_ge(s["xg_high"], g * 2 + hf + 1)
                dve.tensor_tensor(xgl[:, 4 * hf:4 * hf + 4, :].rearrange("p k t -> p (k t)"), tmp[:, hf * 512:(hf + 1) * 512],
                                  xgh[:, 4 * hf:4 * hf + 4, :].rearrange("p k t -> p (k t)").bitcast(F32),
                                  ALU.subtract).then_inc(s["xg_ready"], 1)

            def accumulate(w):
                dve.wait_ge(s["scattered"], w + 2)
                dve.wait_ge(s["acc_made"], w + 2)
                dve.tensor_tensor(ACC.rearrange("p b n -> p (b n)"), ACC.rearrange("p b n -> p (b n)"),
                                  PS[:, 2:6, :].rearrange("p a n -> p (a n)"), ALU.add).then_inc(s["acc_made"], 1)

            def visit(v, e, chained):
                low_units(U0, v * NCH, (3,))
                if chained:
                    accumulate(v - 1)
                hidden(v * NCH + 1, U0 + 4, v * NCH, 0)
                dve.wait_ge(s["selt_done"], v + 1)
                dve.tensor_copy(SELT, PS[:, 5, 0:256])
                dve.tensor_copy(gslot, PS[:, 5, 256:257]).then_inc(s["selt_copied"], 1)
                if chained:
                    select(v + 1, e + 1, 0)

                def body(n, it, par):
                    count = it + (n - UC) // 6 + 1
                    low_units(n, it, (0, 1, 2))
                    turned(count, 1 - par)
                    low_units(n, it, (3, 4, 5))
                    hidden(count + 1, n + 4, it, par)

                with dve.Fori(0, 3) as i:
                    body(UC, v * NCH + i * 2, 1)
                    body(UC + 6, v * NCH + i * 2, 0)
                low_units(UC + 36, v * NCH, (0, 1))
                if chained:
                    scaled(v + 1, 0)
                turned(v * NCH + NCH, 0)
                if chained:
                    scaled(v + 1, 1)
                    for hf in range(2):
                        tokens(v + 1, hf)
                    with dve.If(e < NE - 1):
                        low_units(U0, v * NCH + NCH, (0,))
                dve.wait_ge(unit_used, N_MOE + VISIT + v * VISIT)
                dve.wait_ge(s["selt_copied"], v + 1)
                dve.tensor_scalar(yg, PS[:, 6:8, :].rearrange("p a n -> p (a n)"), gslot, None, ALU.mult).then_inc(s["y_gated"], 1)
                if chained:
                    with dve.If(e < NE - 1):
                        low_units(U0, v * NCH + NCH, (1, 2))
                else:
                    accumulate(v)

            def gather_first(g, e, base, it):
                select(g, e, base)
                low_units(U0, it, (0,))
                for hf in range(2):
                    scaled(g, hf)
                for hf in range(2):
                    tokens(g, hf)
                low_units(U0, it, (1, 2))

            gather_first(0, 0, 0, 0)
            with dve.Fori(0, NE) as e:
                visit(e, e, True)
            accumulate(NE - 1)
            dve.wait_ge(s["route_ready"], 1)
            with dve.Fori(0, NE) as e:
                n = dve.value_load(cnt[0:1, bass.ds(e, 1)], min_val=0, max_val=SEQ)
                v = e + NV
                with dve.If(n > P):
                    gather_first(v + 1, e, P, v * NCH)
                    visit(v, e, False)
                with dve.Else():
                    for sl in range(SPL):
                        m = makers(sl)
                        before = m * len([n for n in range(N_MOE) if n % SPL == sl])
                        dve.wait_ge(low_made[sl], before + v * (2 * NCH * m))
                        dve.sem_inc(low_made[sl], 2 * NCH)
                    for name, k, more in (("sel_made", 1, 1), ("xg_scaled", 2, 2), ("xg_ready", 2, 2), ("selt_copied", 1, 0),
                                          ("h_made", NCH, 0), ("ht_ready", NCH, 0), ("y_gated", 1, 1), ("acc_made", 1, 2)):
                        dve.wait_ge(s[name], v * k + more)
                        dve.sem_inc(s[name], k)
            dve.wait_ge(s["acc_made"], 2 * NE + 2)
            res_dve(dve, 3, lambda b: ACC[:, b, :], lambda b: GGm, link)

        @block.tensor
        def _(pe):
            pe.wait_ge(s["consts_loaded"], 16)
            pe.wait_ge(s["pack_loaded"], 16 * 7)
            pe.transpose(PS[:, 7, 0:57], tmp[0:57, 0:P], K[0:57, C_ID:C_ID + 57]).then_inc(s["pack_turned"], 1)
            pe.wait_ge(s["act_ready"], 1)

            def ada(n, it, before):
                for q in range(3):
                    if before is not None:
                        pe.wait_ge(s["rows_copied"], before + q)
                    for kh in range(2):
                        u = n + 2 * q + kh
                        unit_ready(pe, u, it)
                        wh, wl = halves(u, 4)
                        for k in range(4):
                            a = act4[:, 4 * kh + k, :]
                            pe.matmul(PS[0:4, q, :], a, wh[:, k, :], start=(kh == 0 and k == 0), stop=False)
                            last = pe.matmul(PS[0:4, q, :], a, wl[:, k, :], start=False, stop=(kh == 1 and k == 3))
                        last.then_inc(unit_used, 1)

            ada(0, 0, None)
            with pe.Fori(0, 7) as i:
                ada(6, i, i * 3 + 1)

            pe.wait_ge(s["rows_copied"], 24)
            pe.wait_ge(s["bias_loaded"], 48)
            for l in range(2):
                for w in range(2):
                    for t in range(2):
                        for k in range(KD):
                            q, col = row(l, 3 * w + t, k)
                            o = 2 * (((l * 2 + w) * 2 + t) * KD + k)
                            last = pe.matmul(PS[:, 5 + q, o:o + 2], modrows[32 * q:32 * q + 5, col:col + P],
                                             K[32 * q:32 * q + 5, C_SEL:C_SEL + 2], start=True, stop=True)
            last.then_inc(s["cols_done"], 1)
            for i, (l, part, st) in enumerate(((0, 2, 0), (0, 2, 1), (0, 5, 0), (0, 5, 1), (1, 2, 0), (1, 5, 0))):
                if i >= 2:
                    pe.wait_ge(s["gate_made"], i - 1)
                for hf in range(2):
                    q, col = row(l, part, 4 * hf)
                    last = pe.matmul(PS[:, 2 * (i % 2) + hf, :], K[32 * q:32 * q + 5, C_BC + st * P:C_BC + (st + 1) * P],
                                     modrows[32 * q:32 * q + 5, col:col + 512], start=True, stop=True)
                last.then_inc(s["gate_done"], 1)
            pe.wait_ge(s["mixc_loaded"], 64)
            pe.wait_ge(s["cols_ready"], 1)
            for g in range(4):
                last = pe.transpose(PS[:, 6, g * P:(g + 1) * P], work[:, 10240 + g * P:10240 + (g + 1) * P], ident)
            last.then_inc(s["ws_turned"], 1)

            pe.wait_ge(s["gate_made"], 6)
            pre_pe(pe, 0)
            pe.wait_ge(s["ws_ready"], 1)
            pe.wait_ge(pre[0]["low"], KD)
            for ch in range(4):
                for kh in range(2):
                    u = N_ABIN + 2 * ch + kh
                    unit_ready(pe, u)
                    wh, wl = halves(u, 4)
                    for b in range(NB):
                        if kh == 0 and ch >= 2:
                            pe.wait_ge(s["gelu_made"], (ch - 2) * NB + b + 1)
                        for k in range(4):
                            kk = 4 * kh + k
                            last = product(pe, PS[:, (ch % 2) * 4 + b, :], ahk[:, kk, b * P:(b + 1) * P],
                                           alk[:, kk, b * P:(b + 1) * P], wh[:, k, :], wl[:, k, :],
                                           kk == 0, kk == KD - 1)
                    last.then_inc(unit_used, 1)
            pe.wait_ge(s["vn_ready"], 1)
            pe.wait_ge(s["q_copied"], NB)
            for b in range(NB):
                if b >= 2:
                    pe.wait_ge(s["gated"], b - 1)
                for g in range(4):
                    last = pe.matmul(PS[:, b % 2, g * P:(g + 1) * P], wsT[:, g, :], V[:, b, g * P:(g + 1) * P],
                                     start=True, stop=True)
                last.then_inc(s["mix_done"], 1)
            pe.wait_ge(s["gated"], NB)
            for g in range(4):
                if g >= 2:
                    pe.wait_ge(s["cat_low"], g - 1)
                for b in range(NB):
                    last = pe.transpose(PS[:, 2 + g % 2, b * P:(b + 1) * P], U[:, b, g * P:(g + 1) * P], ident)
                last.then_inc(s["cat_turned"], 1)
            pe.wait_ge(s["qn_ready"], 1)
            pe.wait_ge(s["kv_copied"], NB)
            for h in range(6):
                if h == 4:
                    pe.wait_ge(s["kn_ready"], 1)
                if h >= 2:
                    pe.wait_ge(s["qk_ready"], h - 1)
                for b in range(NB):
                    t = Q[:, b, h * P:(h + 1) * P] if h < 4 else KV[:, b, (h - 4) * P:(h - 3) * P]
                    last = pe.transpose(PS[:, 6 + h % 2, b * P:(b + 1) * P], t, ident)
                last.then_inc(s["qk_turned"], 1)
            pe.wait_ge(s["qk_ready"], 6)
            pe.wait_ge(s["cat_low"], 4)
            att_pe(pe, 0)
            pe.wait_ge(att[0]["low"], 8)
            for j in range(4):
                u = N_ABOUT + j
                unit_ready(pe, u)
                wh, wl = halves(u, 2)
                for b in range(NB):
                    for k in range(2):
                        kk = 2 * j + k
                        for hf in range(2):
                            last = product(pe, PS[:, 2 * b + hf, :], ahk[:, kk, b * P:(b + 1) * P], alk[:, kk, b * P:(b + 1) * P],
                                           wh[:, k, hf * 512:(hf + 1) * 512], wl[:, k, hf * 512:(hf + 1) * 512],
                                           kk == 0, kk == KD - 1)
                last.then_inc(unit_used, 1)

            pre_pe(pe, 1)
            pe.wait_ge(pre[1]["low"], KD)

            def ffn_pair(f0, n, it):
                for j in range(2):
                    f = f0 + j
                    for gu in range(2):
                        if j == 0:
                            unit_ready(pe, n + gu, it)
                        if gu == 0 and f >= 2:
                            pe.wait_ge(s["hid_made"], f - 1 + it * 6)
                        wh, wl = (t[:, :, j * P:(j + 1) * P] for t in halves(n + gu, KD))
                        for k in range(KD):
                            last = product(pe, PS[:, 2 * (f % 2) + gu, :], wh[:, k, :], wl[:, k, :], ahk[:, k, :], alk[:, k, :],
                                           k == 0, k == KD - 1)
                        last.then_inc(s[("g_done", "u_done")[gu]] if j == 0 else unit_used, 1)

            for j in range(3):
                ffn_pair(2 * j, N_FIN + 2 * j, 0)
            with pe.Fori(0, 2) as i:
                for j in range(3):
                    ffn_pair(6 + 2 * j, N_FIN + 6 + 2 * j, i)
            for j in range(9, 11):
                ffn_pair(2 * j, N_FIN + 2 * j, 0)
            pe.wait_ge(s["hid_made"], 22)
            for d in range(11):
                u = N_FOUT + d
                unit_ready(pe, u)
                wh, wl = halves(u, 2)
                for k in range(2):
                    f = 2 * d + k
                    pe.wait_ge(s["fd_ready"], f + 1)
                    for b in range(NB):
                        for hf in range(2):
                            last = product(pe, PS[:, 2 * b + hf, :], fh[:, f % 2, b * P:(b + 1) * P], fl[:, f % 2, b * P:(b + 1) * P],
                                           wh[:, k, hf * 512:(hf + 1) * 512], wl[:, k, hf * 512:(hf + 1) * 512],
                                           f == 0, f == 21)
                    if k == 0:
                        last.then_inc(s["fd_used"], 1)
                last.then_inc(unit_used, 1)

            pre_pe(pe, 2)
            pe.wait_ge(pre[2]["low"], KD)
            for j in range(4):
                u = N_MLA + j
                unit_ready(pe, u)
                wh, wl = halves(u, 4, MLA_W[j])
                w = CQ if j < 2 else CKV + CROPE
                for b in range(LB if j < 2 else NB):
                    for k in range(4):
                        kk = 4 * (j % 2) + k
                        last = product(pe, PS[:, b if j < 2 else 2 + b, 0:w], ahk[:, kk, b * P:(b + 1) * P],
                                       alk[:, kk, b * P:(b + 1) * P], wh[:, k, :], wl[:, k, :], kk == 0, kk == KD - 1)
                last.then_inc(unit_used, 1)
            pe.wait_ge(s["kr_ready"], 1)
            pe.wait_ge(s["c_copied"], 11)
            for k in range(5):
                if k >= 2:
                    pe.wait_ge(s["c_scaled"], k - 1)
                for b in range(LB if k < 3 else NB):
                    t = cqn[:, b, k * P:(k + 1) * P] if k < 3 else ckvn[:, b, (k - 3) * P:(k - 2) * P]
                    last = pe.transpose(PS[:, 6 + k % 2, b * P:(b + 1) * P], t, ident)
                last.then_inc(s["c_turned"], 1)
            pe.wait_ge(s["c_scaled"], 4)
            for b in range(NB):
                last = pe.transpose(PS[:, 7, b * P:(b + 1) * P], kr2[:, b, :], ident)
            last.then_inc(s["kr_turned"], 1)
            for j in range(3):
                unit_ready(pe, N_MLA + 4 + j)
            pe.wait_ge(s["c_ready"], 3)
            uq = [[t.rearrange("p a (h d) -> p (a h) d", h=8) for t in halves(N_MLA + 4 + k, 1, 1536)] for k in range(3)]
            for b in range(LB):
                for k in range(3):
                    wh, wl = (t[:, :, HD:HD + CROPE] for t in uq[k])
                    last = product(pe, PS[:, b, :], cqh[:, k, b * P:(b + 1) * P], cql[:, k, b * P:(b + 1) * P], wh, wl, k == 0, k == 2)
                last.then_inc(s["qr_done"], 1)
            for h in range(8):
                if h >= 4:
                    pe.wait_ge(s["qn_moved"], h - 3)
                for k in range(3):
                    wh, wl = (t[:, h, 0:HD] for t in uq[k])
                    last = product(pe, PS[:, 2 + h % 4, 0:256], wh, wl, cqh[:, k, :], cql[:, k, :], k == 0, k == 2)
                if h < 7:
                    last.then_inc(s["qn_done"], 1)
            last.then_inc(unit_used, 3)
            pe.wait_ge(s["kr_copied"], 1)
            pe.wait_ge(s["qr_ready"], LB)
            for p in range(4):
                if p >= 2:
                    pe.wait_ge(s["qr_moved"], p - 1)
                for b in range(LB):
                    last = pe.transpose(PS[:, 6 + p % 2, b * P:(b + 1) * P], qrt[:, b, p * P:(p + 1) * P], ident)
                last.then_inc(s["qr_turned"], 1)
            for j in range(2):
                unit_ready(pe, N_MLA + 7 + j)
            pe.wait_ge(s["c_ready"], 5)
            pe.wait_ge(s["qn_moved"], 8)
            ukv = [[t.rearrange("p a (h d) -> p (a h) d", h=8) for t in halves(N_MLA + 7 + k, 1)] for k in range(2)]
            for j in range(16):
                if j >= 6:
                    pe.wait_ge(s["kv_moved"], j - 5)
                for k in range(2):
                    if j < 8:
                        wh, wl = (t[:, j, 0:HD] for t in ukv[k])
                        last = product(pe, PS[:, j % 6, :], wh, wl, ckh[:, k, :], ckl[:, k, :], k == 0, k == 1)
                    else:
                        b, hf = (j - 8) // 2, (j - 8) % 2
                        wh, wl = (t[:, 4 * hf:4 * hf + 4, HD:2 * HD] for t in ukv[k])
                        last = product(pe, PS[:, j % 6, :], ckh[:, k, b * P:(b + 1) * P], ckl[:, k, b * P:(b + 1) * P], wh, wl, k == 0, k == 1)
                if j < 15:
                    last.then_inc(s["kv_done"], 1)
            last.then_inc(unit_used, 2)
            pe.wait_ge(s["kv_moved"], 16)
            pe.wait_ge(s["qr_moved"], 4)
            att_pe(pe, 1)
            pe.wait_ge(att[1]["low"], 8)
            for j in range(4):
                u = N_MLA + 9 + j
                unit_ready(pe, u)
                wh, wl = halves(u, 2)
                for b in range(LB):
                    for k in range(2):
                        kk = 2 * j + k
                        for hf in range(2):
                            last = product(pe, PS[:, 2 * b + hf, :], och[:, kk, b * P:(b + 1) * P], ocl[:, kk, b * P:(b + 1) * P],
                                           wh[:, k, hf * 512:(hf + 1) * 512], wl[:, k, hf * 512:(hf + 1) * 512],
                                           kk == 0, kk == KD - 1)
                last.then_inc(unit_used, 1)

            pre_pe(pe, 3)
            pe.wait_ge(pre[3]["low"], KD)
            pe.wait_ge(s["rt_loaded"], 16)
            for b in range(LB):
                for k in range(KD):
                    for t in (ahk, alk):
                        last = pe.matmul(PS[:, 0, 8 * b:8 * b + 8], t[:, k, b * P:(b + 1) * P].bitcast(F32), RT[:, k, :],
                                         start=(k == 0 and t is ahk), stop=(k == KD - 1 and t is alk))
            last.then_inc(s["logits_done"], 1)
            pe.wait_ge(s["mask_made"], 1)
            mk = [tab[:, 1, b, 0:NE] for b in range(LB)]
            ones = rs[:, 64:192]
            tri = K[:, C_TRI:C_TRI + P]
            pe.matmul(PS[:, 1, 0:8], tri, mk[0], start=True, stop=True)
            pe.matmul(PS[:, 1, 8:16], tri, mk[1], start=True, stop=False)
            pe.matmul(PS[:, 1, 8:16], ones, mk[0], start=False, stop=True)
            pe.matmul(PS[:, 1, 16:24], ones, mk[0], start=True, stop=False)
            pe.matmul(PS[:, 1, 16:24], ones, mk[1], start=False, stop=True).then_inc(s["pos_done"], 1)

            gsel = sc[:, 152:154]

            def turn(count, par):
                pe.wait_ge(s["h_made"], count)
                for j in range(4):
                    last = pe.transpose(PS[:, 4, j * P:(j + 1) * P], hh[:, par, j * P:(j + 1) * P], ident)
                last.then_inc(s["ht_done"], 1)

            def up(n, it, par, parts=(0, 1)):
                for gu in parts:
                    for kh in range(2):
                        u = n + 2 * gu + kh
                        unit_ready(pe, u, it)
                        wh, wl = halves(u, 4)
                        for k in range(4):
                            kk = 4 * kh + k
                            last = product(pe, PS[:, 2 * par + gu, :], xgh[:, kk, :], xgl[:, kk, :], wh[:, k, :], wl[:, k, :],
                                           kk == 0, kk == KD - 1)
                        last.then_inc(unit_used, 1)

            def down(n, it, count, par):
                pe.wait_ge(s["ht_ready"], count)
                for j in range(2):
                    unit_ready(pe, n + j, it)
                    wh, wl = halves(n + j, 2)
                    for k in range(2):
                        f = 2 * j + k
                        for hf in range(2):
                            o = PS[:, 6 + hf, :]
                            a_h, a_l = hth[:, par, f * P:(f + 1) * P], htl[:, par, f * P:(f + 1) * P]
                            mh, ml = wh[:, k, hf * 512:(hf + 1) * 512], wl[:, k, hf * 512:(hf + 1) * 512]
                            pe.matmul(o, a_h, mh, start=False, stop=True, skip_group_check=True)
                            pe.matmul(o, a_h, ml, start=False, stop=True, skip_group_check=True)
                            last = pe.matmul(o, a_l, mh, start=False, stop=True, skip_group_check=True)
                    last.then_inc(unit_used, 1)

            def gather(g):
                pe.wait_ge(s["sel_made"], g + 1)
                for hf in range(2):
                    for k in range(4 * hf, 4 * hf + 4):
                        for b in range(LB):
                            last = pe.matmul(PS[:, 2 + hf, (k % 4) * P:(k % 4 + 1) * P], xn[:, b, k * P:(k + 1) * P],
                                             SEL[:, b, :], start=(b == 0), stop=(b == LB - 1))
                    last.then_inc(s["gathered"], 1)

            def scatter(w):
                pe.wait_ge(s["y_gated"], w + 2)
                for b in range(LB):
                    for hf in range(2):
                        last = pe.matmul(PS[:, 2 + 2 * b + hf, :], SELT[:, b * P:(b + 1) * P], yg[:, hf * 512:(hf + 1) * 512],
                                         start=True, stop=True)
                last.then_inc(s["scattered"], 1)

            def visit(v, chained):
                pe.wait_ge(s["xg_ready"], v * 2 + (2 if chained else 4))
                up(U0, v * NCH, 0, (0,))
                if chained:
                    scatter(v - 1)
                for hf in range(2):
                    pe.matmul(PS[:, 6 + hf, :], zero16[:, 0:P], zero16[:, 0:512], start=True, stop=True)
                up(U0, v * NCH, 0, (1,))
                pe.wait_ge(s["acc_made"], v + 2)
                for b in range(LB):
                    pe.transpose(PS[:, 5, b * P:(b + 1) * P], SEL[:, b, :], ident)
                for b in range(LB):
                    last = pe.matmul(PS[:, 5, 256:257], SEL[:, b, :], gsel[:, b:b + 1], start=(b == 0), stop=(b == LB - 1))
                last.then_inc(s["selt_done"], 1)
                with pe.Fori(0, 3) as i:
                    for j in range(2):
                        it = v * NCH + i * 2
                        turn(it + j + 1, j)
                        up(UC + 6 * j, it, 1 - j)
                        down(UC + 6 * j + 4, it, it + j + 1, j)
                if chained:
                    gather(v + 1)
                turn(v * NCH + NCH, 0)
                down(UC + 36, v * NCH, v * NCH + NCH, 0)
                if not chained:
                    scatter(v)

            gather(0)
            with pe.Fori(0, NE) as e:
                visit(e, True)
            scatter(NE - 1)
            pe.wait_ge(s["route_ready"], 1)
            with pe.Fori(0, NE) as e:
                n = pe.value_load(cnt[0:1, bass.ds(e, 1)], min_val=0, max_val=SEQ)
                v = e + NV
                with pe.If(n > P):
                    gather(v + 1)
                    visit(v, False)
                with pe.Else():
                    pe.wait_ge(unit_used, N_MOE + v * VISIT)
                    pe.sem_inc(unit_used, VISIT)
                    for name, k, more in (("gathered", 2, 2), ("selt_done", 1, 0), ("ht_done", NCH, 0), ("scattered", 1, 1)):
                        pe.wait_ge(s[name], v * k + more)
                        pe.sem_inc(s[name], k)


_INS = ['x', 'c', 'ctx', 'c_ctx', 'ada_w', 'ada_b', 'g_pre_mix', 'g_post_mix', 'g_pre_ffn', 'g_post_ffn',
        'ab_w_in', 'a_norm_g', 'a_ws', 'a_bs', 'b_qnorm_g', 'b_knorm_g', 'ab_w_out', 'ffn_w_in', 'ffn_w_out',
        'mla_w_dq', 'mla_qnorm_g', 'mla_w_uq', 'mla_w_dkv', 'mla_kvnorm_g', 'mla_w_ukv', 'mla_w_o',
        'moe_router', 'moe_w_in', 'moe_w_out']


def kernel(**inputs):
    import concourse.bacc as _bacc
    from concourse.bass_utils import run_bass_kernel_spmd as _run

    nc = _bacc.Bacc("TRN2", target_bir_lowering=False, num_devices=1)
    arrays, args = {}, []
    for name in _INS + ["consts"]:
        a = np.ascontiguousarray(constants() if name == "consts" else inputs[name])
        arrays[f"in_{name}_dram"] = a
        args.append(nc.dram_tensor(f"in_{name}_dram", a.shape, mybir.dt.from_np(a.dtype), kind="ExternalInput").ap())
    args.append(nc.dram_tensor("out_0_dram", (1, SEQ, D), F32, kind="ExternalOutput").ap())
    trunk(nc, *args)
    r = _run(nc, [arrays], core_ids=[0])
    return r.results[0]["out_0_dram"]
```

```python
from contextlib import ExitStack

import numpy as np

import concourse.bass as bass
from concourse import mybir

ALU = mybir.AluOpType
ACT = mybir.ActivationFunctionType
AXX = mybir.AxisListType.X
F32 = mybir.dt.float32
F32R = mybir.dt.float32r
BF16 = mybir.dt.bfloat16
I32 = mybir.dt.int32
U32 = mybir.dt.uint32

P = 128
D = 1024
KD = D // P
SEQ = 256
CTX = 256
NTOK = SEQ + CTX
NB = NTOK // P
LB = SEQ // P
GRID_W = 64
EPS = 1e-6
HD = 128
CROPE = 64
CQ, CKV = 384, 256
D_FF = 2816
NE = 8
D_FFE = 3584

UNIT = 2048
RAW = 6
SPL = 3
FCH = 512
NCH = D_FFE // FCH
VISIT = NCH * 6

N_ABIN = [12, 20, 28, 30]
N_ADA = [0, 6, 14, 22]
N_ABOUT = 32
N_FIN = 36
N_FOUT = 82
N_MLA = N_FOUT + 11
N_MOE = N_MLA + 13

C_ID, C_TRI, C_IOTA = 0, 128, 256
C_CB, C_SB = 512, 768
C_CC, C_SC = 1024, 1152
C_EPS, C_I8 = 1280, 1281
C_N = 1296



def constants():
    k = np.zeros((P, C_N), np.float32)
    k[:, C_ID:C_ID + P] = np.eye(P)
    k[:, C_TRI:C_TRI + P] = np.triu(np.ones((P, P)), 1)
    k[:, C_IOTA:C_IOTA + 256] = np.arange(256)
    tok = np.arange(SEQ)
    row, col = (tok // GRID_W).astype(np.float32), (tok % GRID_W).astype(np.float32)
    for width, c0, s0 in ((HD, C_CB, C_SB), (CROPE, C_CC, C_SC)):
        nf = width // 4
        inv = np.float32(10000.0) ** (-np.arange(nf, dtype=np.float32) / np.float32(nf))
        ang = np.stack([row[:, None] * inv, col[:, None] * inv], axis=1).astype(np.float32)
        ang = np.broadcast_to(ang[:, :, None, :], (SEQ, 2, 2, nf))
        sign = np.array([-1.0, 1.0], np.float32)[None, None, :, None]
        for b in range(LB):
            t = slice(b * P, b * P + P)
            k[:, c0 + b * width:c0 + (b + 1) * width] = np.cos(ang[t]).reshape(P, width)
            k[:, s0 + b * width:s0 + (b + 1) * width] = (np.sin(ang[t]) * sign).reshape(P, width)
    k[:, C_EPS] = EPS
    k[:, C_I8:C_I8 + NE] = np.arange(NE)
    return k


def trunk(nc, x, c, ctx, c_ctx, ada_w, ada_b, g_pre_mix, g_post_mix, g_pre_ffn, g_post_ffn,
          ab_w_in, a_norm_g, a_ws, a_bs, b_qnorm_g, b_knorm_g, ab_w_out, ffn_w_in, ffn_w_out,
          mla_w_dq, mla_qnorm_g, mla_w_uq, mla_w_dkv, mla_kvnorm_g, mla_w_ukv, mla_w_o,
          moe_router, moe_w_in, moe_w_out, consts, out):
    es = ExitStack()
    with es:
        def sb(name, shape, dt=F32):
            return es.enter_context(nc.sbuf_tensor(name, shape, dt))

        def sem(name):
            return es.enter_context(nc.semaphore(name))

        raw = [sb(f"raw{i}", [P, UNIT]) for i in range(RAW)]
        high = [sb(f"high{i}", [P, UNIT], F32R) for i in range(SPL)]
        low = [sb(f"low{i}", [P, UNIT], F32R) for i in range(SPL)]
        X = sb("X", [P, NB, D])
        ah = sb("ah", [P, KD * NTOK], F32R)
        al = sb("al", [P, KD * NTOK], F32R)
        tmp = sb("tmp", [P, 2 * 512])
        K = sb("K", [P, C_N])
        mixc = sb("mixc", [P, 1280])
        vec = sb("vec", [P, 192])
        modall = sb("modall", [P, 96, 2])
        gcol = sb("gcol", [P, 32])
        grow = sb("grow", [32, P])
        scol = sb("scol", [P, 2, 2, KD, 2])
        sc = sb("sc", [P, 160])
        sil = sb("sil", [P, 2, KD])
        act4 = sb("act4", [P, KD, 4], F32R)
        cnt = sb("cnt", [P, NE], I32)
        work = sb("work", [P, 11 * 1024])
        PS = es.enter_context(nc.psum_tensor("PS", [P, 8, 512], F32))
        gg_dram = nc.dram_tensor("gg_scratch", [6, D], F32).ap()

        ident = K[:, C_ID:C_ID + P]
        xn = work[:, 0:NB * D].rearrange("p (b d) -> p b d", b=NB)
        raw_loaded = [sem(f"raw_loaded{i}") for i in range(RAW)]
        high_made = sem("high_made")
        low_made = [sem(f"low_made{i}") for i in range(SPL)]
        unit_used = sem("unit_used")

        def load_unit(sp, n, src, it=0):
            if n >= RAW:
                m = makers(n)
                sp.wait_ge(low_made[n % SPL], m * ((n - RAW) // SPL + 1) + it * (2 * m))
            dst = raw[n % RAW][:, 0:src.shape[1] * src.shape[2]].rearrange("p (a n) -> p a n", a=src.shape[1])
            sp.dma_start(dst, src).then_inc(raw_loaded[n % RAW], 16)

        def split_high(act, n, it=0, width=UNIT):
            act.wait_ge(raw_loaded[n % RAW], 16 * (n // RAW + 1) + it * 16)
            if n >= SPL:
                act.wait_ge(unit_used, n - SPL + 1 + it * 6)
            act.activation(high[n % SPL][:, 0:width], raw[n % RAW][:, 0:width], ACT.Copy).then_inc(high_made, 1)

        def makers(n):
            return 2 if n % SPL == SPL - 1 else 1

        def split_low(eng, n, it, c0, c1):
            eng.wait_ge(high_made, n + 1 + it * 6)
            eng.tensor_tensor(low[n % SPL][:, c0:c1], raw[n % RAW][:, c0:c1],
                              high[n % SPL][:, c0:c1].bitcast(F32), ALU.subtract).then_inc(low_made[n % SPL], 1)

        def vector_low(dve, n, it=0, width=UNIT):
            split_low(dve, n, it, 0 if makers(n) == 1 else width // 2, width)

        def pool_low(pool, n, it=0, width=UNIT):
            split_low(pool, n, it, 0, width // 2)

        def unit_ready(pe, n, it=0):
            m = makers(n)
            pe.wait_ge(low_made[n % SPL], m * (n // SPL + 1) + it * (2 * m))

        def halves(n, a, width=UNIT):
            return [t[n % SPL][:, 0:width].rearrange("p (a n) -> p a n", a=a) for t in (high, low)]

        def product(pe, o, sh, sl, mh, ml, start, stop):
            pe.matmul(o, sh, mh, start=start, stop=False)
            pe.matmul(o, sh, ml, start=False, stop=False)
            return pe.matmul(o, sl, mh, start=False, stop=stop)

        ahk = ah[:, :].rearrange("p (k t) -> p k t", k=KD)
        alk = al[:, :].rearrange("p (k t) -> p k t", k=KD)

        modv = modall[:, :, :].rearrange("p (l a k) s -> p l a k s", l=2, a=6)
        modc = modv.rearrange("p l (w t) k s -> p l w t k s", w=2)
        rows = [work[:, 8192:8704], mixc[:, 0:512]]
        U = work[:, 4096:6144].rearrange("p (b n) -> p b n", b=NB)
        V = work[:, 6144:8192].rearrange("p (b n) -> p b n", b=NB)
        Q = work[:, 0:2048].rearrange("p (b n) -> p b n", b=NB)
        KV = work[:, 2048:4096].rearrange("p (b n) -> p b n", b=NB)
        qT = work[:, 8192:10240].rearrange("p (h t) -> p h t", h=4)
        kT = work[:, 10240:11264].rearrange("p (h t) -> p h t", h=2)
        HID = work[:, 0:22 * 512].rearrange("p (f t) -> p f t", f=22)
        knT = work[:, 4096:8192].rearrange("p (h t) -> p h t", h=8)
        qnT = work[:, 8192:10240].rearrange("p (h t) -> p h t", h=8)
        krT = work[:, 10240:10752]
        V1 = work[:, 0:4096].rearrange("p (b n) -> p b n", b=NB)
        cqn = work[:, 0:768].rearrange("p (b n) -> p b n", b=2)
        ckvn = work[:, 768:1792].rearrange("p (b n) -> p b n", b=NB)
        kr2 = work[:, 1792:2304].rearrange("p (b n) -> p b n", b=NB)
        qrt = work[:, 2304:3328].rearrange("p (b n) -> p b n", b=2)
        rot = work[:, 4096:5120]
        GG = work[:, 4096:6144].rearrange("p (a n) -> p a n", a=2)
        ACC = work[:, 2048:4096].rearrange("p (b n) -> p b n", b=2)
        GGm = work[:, 4096:5120]
        sg = work[:, 5120:6144].rearrange("p (a n) -> p a n", a=2)
        hh = work[:, 6144:7168].rearrange("p (a n) -> p a n", a=2)
        yg = work[:, 7168:8192]
        SEL = work[:, 8192:8448].rearrange("p (b n) -> p b n", b=2)
        SELT = work[:, 8448:8704]
        RT = work[:, 8704:8768].rearrange("p (k n) -> p k n", k=KD)
        rs = work[:, 8768:9024]
        tab = work[:, 9024:9024 + 6 * (NE + 1)].rearrange("p (t b e) -> p t b e", t=3, b=LB)
        zero16 = work[:, 9216:9472].bitcast(BF16)
        anb, qgb, kgb = mixc[:, 0:512], mixc[:, 512:640], mixc[:, 640:768]
        g_post = [vec[:, 57 + 16 * w:73 + 16 * w].rearrange("p (l k) -> p l k", l=2) for w in range(2)]
        wsT = mixc[:, 768:1280].rearrange("p (g i) -> p g i", g=4)
        XC = X[:, 2:4, :].rearrange("p b d -> p (b d)")
        sgf = tmp[:, :].rearrange("p (a n) -> p a n", a=2)
        fh = ah[:, 0:2048].rearrange("p (a t) -> p a t", a=4)
        fl = al[:, 0:2048].rearrange("p (a t) -> p a t", a=4)
        cqh, cql = (t[:, 0:768].rearrange("p (k t) -> p k t", k=3) for t in (ah, al))
        ckh, ckl = (t[:, 768:1792].rearrange("p (k t) -> p k t", k=2) for t in (ah, al))
        och, ocl = (t[:, 2048:4096].rearrange("p (k t) -> p k t", k=8) for t in (ah, al))
        xgh, xgl = (t[:, 0:1024].rearrange("p (k t) -> p k t", k=KD) for t in (ah, al))
        hth, htl = (t[:, 1024:2048].rearrange("p (a t) -> p a t", a=2) for t in (ah, al))

        s = {}
        for name in """consts_loaded pack_loaded x_loaded mixc_loaded gg_loaded gg_stored
                rt_loaded out_stored
                pack_turned vec_ready silu_ready act_high act_ready rows_copied cols_turned cols_taken cols_ready
                gate_cols gate_turned gate_rows ws_turned ws_ready dve_step
                gelu_made q_copied kv_copied gn_ms gn_root vn_ready mix_done gated cat_turned
                cat_high cat_low qk_turned qk_ready qn_ready kn_ready
                g_done u_done silu_made hid_made fd_high fd_ready
                c_copied c_turned c_scaled c_high c_ready kr_ready kr_turned kr_copied
                qr_done qr_copied qr_ready qr_turned qr_moved qn_done qn_moved kv_done kv_moved
                logits_done route1 route_exp mask_made pos_done route_ready
                sel_made gathered selt_done xg_scaled xg_high xg_ready selt_copied
                esilu_made h_made ht_done ht_high ht_ready y_gated scattered acc_made
                resid_done resid_pool y_scaled y_done squared mean_made root_made""".split():
            s[name] = sem(name)

        PRE = [(NB, 0, 0), (NB, 0, 1), (NB, 1, 0), (LB, 1, 1)]
        pre = [{n: sem(f"pre{i}_{n}") for n in "xn turned scaled act_scaled high low pool_low".split()} for i in range(4)]
        RES = [(NB, 0), (NB, 2), (LB, 4), (LB, 5)]
        squares = [0]
        for i in range(4):
            squares += [squares[-1] + PRE[i][0], squares[-1] + PRE[i][0] + RES[i][0]]
        att = [{n: sem(f"att{i}_{n}") for n in "scored bias exp p turned pt o high low".split()} for i in range(2)]

        SS, MS, RSTD = 0, 4, 8

        junk = ah[:, 3072:4096]
        SCR = [tmp[:, 0:512], tmp[:, 512:1024], work[:, 6144:6656], work[:, 6656:7168]]
        OLD = [0, 2, 4, 5]
        RDONE = [0, 2, 4, 5]
        YDONE = [0, 3, 6]

        def x_ready(eng, i, b):
            eng.wait_ge(s["resid_done" if b % 2 else "resid_pool"], OLD[i - 1] + b // 2 + 1)

        def act_warm(act, col):
            act.activation(sc[:, col:col + 1], K[:, C_EPS:C_EPS + 1], ACT.Sqrt)

        def pre_act(act, i):
            nb, layer, place = PRE[i]
            m = pre[i]
            if i == 0:
                act_warm(act, 155)
                act.wait_ge(s["x_loaded"], 32)
            for b in range(nb):
                if i:
                    x_ready(act, i, b)
                if b:
                    act.wait_ge(s["squared"], squares[2 * i] + b)
                act.activation(junk, X[:, b, :], ACT.Square, accum_out=sc[:, SS + b:SS + b + 1]).then_inc(s["squared"], 1)
            act.wait_ge(s["mean_made"], 2 * i + 1)
            act.activation(sc[:, MS:MS + nb], sc[:, MS:MS + nb], ACT.Sqrt).then_inc(s["root_made"], 1)

        def pre_act_chunks(act, i):
            nb, layer, place = PRE[i]
            m = pre[i]

            def upper(k):
                act.wait_ge(m["scaled"], k + 1)
                if nb > LB:
                    act.wait_ge(m["act_scaled"], k + 1)
                act.activation(ahk[:, k, 0:nb * P], SCR[k % 4][:, 0:nb * P], ACT.Copy).then_inc(m["high"], 1)

            act.wait_ge(s["cols_ready"], [1, 2, 3, 3][i])
            for k in range(KD):
                if nb > LB:
                    act.wait_ge(m["turned"], k + 1)
                    if k >= 4:
                        low_ready(act, i, k - 4)
                    act.activation(SCR[k % 4][:, SEQ:], PS[:, 2 + k % 2, 0:SEQ], ACT.Identity,
                                   bias=modc[:, layer, place, 0, k, 1:2], scale=scol[:, layer, place, k, 1:2]).then_inc(m["act_scaled"], 1)
                if k:
                    upper(k - 1)
            upper(KD - 1)

        def low_ready(eng, i, k):
            eng.wait_ge(pre[i]["pool_low" if k % 2 else "low"], k // 2 + 1)

        def pre_low(eng, i, k):
            nb = PRE[i][0]
            m = pre[i]
            eng.wait_ge(m["high"], k + 1)
            eng.tensor_tensor(alk[:, k, 0:nb * P], SCR[k % 4][:, 0:nb * P],
                              ahk[:, k, 0:nb * P].bitcast(F32), ALU.subtract).then_inc(m["pool_low" if k % 2 else "low"], 1)

        def pre_pool(pool, i):
            for k in range(1, KD, 2):
                pre_low(pool, i, k)

        def pre_dve(dve, i, link):
            nb, layer, place = PRE[i]
            m = pre[i]
            dve.wait_ge(s["squared"], squares[2 * i] + nb)
            dve.tensor_scalar(sc[:, MS:MS + nb], sc[:, SS:SS + nb], 1.0 / D, EPS, ALU.mult, ALU.add).then_inc(s["mean_made"], 1)
            dve.wait_ge(s["root_made"], 2 * i + 1)
            link(dve.reciprocal(sc[:, RSTD:RSTD + nb], sc[:, MS:MS + nb]))
            for b in range(nb):
                if i:
                    x_ready(dve, i, b)
                dve.tensor_scalar(xn[:, b, :], X[:, b, :], sc[:, RSTD + b:RSTD + b + 1], None, ALU.mult).then_inc(m["xn"], 1)

        def pre_dve_chunks(dve, i):
            nb, layer, place = PRE[i]
            m = pre[i]
            for k in range(KD):
                dve.wait_ge(m["turned"], k + 1)
                if k >= 4:
                    low_ready(dve, i, k - 4)
                dve.tensor_scalar(SCR[k % 4][:, 0:SEQ], PS[:, k % 2, 0:SEQ], scol[:, layer, place, k, 0:1],
                                  modc[:, layer, place, 0, k, 0:1], ALU.mult, ALU.add).then_inc(m["scaled"], 1)
                if k % 2:
                    pre_low(dve, i, k - 1)

        def pre_pe(pe, i):
            nb = PRE[i][0]
            m = pre[i]
            pe.wait_ge(m["xn"], nb)
            for k in range(KD):
                if k >= 2:
                    pe.wait_ge(m["scaled"], k - 1)
                    if nb > LB:
                        pe.wait_ge(m["act_scaled"], k - 1)
                for b in range(nb):
                    last = pe.transpose(PS[:, 2 * (b // LB) + k % 2, (b % LB) * P:(b % LB + 1) * P], xn[:, b, k * P:(k + 1) * P], ident)
                last.then_inc(m["turned"], 1)

        def pre_done(pe, i):
            for k in (KD - 2, KD - 1):
                low_ready(pe, i, k)

        def res_act(act, i, y, done):
            nb = RES[i][0]
            act_warm(act, 156 + i)
            for b in range(nb):
                if i == 3 or b == nb - 1:
                    act.wait_ge(*done)
                else:
                    act.wait_ge(s["y_done"], YDONE[i] + b + 1)
                if b:
                    act.wait_ge(s["squared"], squares[2 * i + 1] + b)
                act.activation(tmp[:, :], y(b), ACT.Square, accum_out=sc[:, SS + b:SS + b + 1]).then_inc(s["squared"], 1)
            act.wait_ge(s["mean_made"], 2 * i + 1 + 1)
            act.activation(sc[:, MS:MS + nb], sc[:, MS:MS + nb], ACT.Sqrt).then_inc(s["root_made"], 1)

        YG = [tmp[:, :], work[:, 6144:7168]]

        def res_pool(pool, i):
            for b in range(0, RES[i][0], 2):
                pool.wait_ge(s["y_scaled"], RDONE[i] + b // 2 + 1)
                pool.tensor_tensor(X[:, b, :], X[:, b, :], YG[0], ALU.add).then_inc(s["resid_pool"], 1)

        def res_dve(dve, i, y, gate, link):
            nb = RES[i][0]
            dve.wait_ge(s["squared"], squares[2 * i + 1] + nb)
            dve.tensor_scalar(sc[:, MS:MS + nb], sc[:, SS:SS + nb], 1.0 / D, EPS, ALU.mult, ALU.add).then_inc(s["mean_made"], 1)
            dve.wait_ge(s["root_made"], 2 * i + 1 + 1)
            link(dve.reciprocal(sc[:, RSTD:RSTD + nb], sc[:, MS:MS + nb]))
            dve.wait_ge(s["gg_loaded"], 16 * (i + 1))
            for b in range(nb):
                if b >= 2 and b % 2 == 0:
                    dve.wait_ge(s["resid_pool"], RDONE[i] + b // 2)
                ins = dve.scalar_tensor_tensor(out=YG[b % 2], in0=y(b), scalar=sc[:, RSTD + b:RSTD + b + 1],
                                               in1=gate(b), op0=ALU.mult, op1=ALU.mult)
                if b % 2 == 0:
                    ins.then_inc(s["y_scaled"], 1)
                else:
                    link(ins)
                    dve.tensor_tensor(X[:, b, :], X[:, b, :], YG[1], ALU.add).then_inc(s["resid_done"], 1)
                    dve.wait_ge(s["resid_done"], RDONE[i] + b // 2 + 1)

        def ps_rows(b):
            return PS[:, 2 * b:2 * b + 2, :].rearrange("p a n -> p (a n)")

        PB = [work[:, 4096:5120], XC[:, 0:1024]]
        PT = [[work[:, 6144:7168], work[:, 7168:8192]], [tmp[:, :], mixc[:, 0:1024]]]
        qrT = XC[:, 1024:2048].rearrange("p (h t) -> p h t", h=4)
        ATT = [dict(n=16, scale=HD ** -0.5), dict(n=16, scale=(HD + CROPE) ** -0.5)]
        MX, NBI, SUM, REC = 16, 32, 48, 64

        def att_keys(a, i):
            return (0, NTOK) if a == 1 or i < 8 else (SEQ, CTX)

        def att_pe(pe, a):
            m = att[a]
            n = ATT[a]["n"]

            def scores(i):
                k0, nk = att_keys(a, i)
                if i >= 2:
                    pe.wait_ge(m["exp"], i - 1)
                o = PS[:, i % 2, 0:nk]
                if a == 0:
                    h, t0 = (i // 2) % 4, (SEQ if i >= 8 else 0) + (i % 2) * P
                    last = pe.matmul(o, qT[:, h, t0:t0 + P], kT[:, h // 2, k0:k0 + nk], start=True, stop=True)
                else:
                    h, t0, r = i // 2, (i % 2) * P, 64 * ((i // 2) % 2)
                    pe.matmul(o, qnT[:, h, t0:t0 + P], knT[:, h, :], start=True, stop=False)
                    last = pe.matmul(o, qrT[r:r + 64, h // 2, t0:t0 + P], krT[r:r + 64, :], start=False, stop=True)
                last.then_inc(m["scored"], 1)

            def turn(i):
                k0, nk = att_keys(a, i)
                pe.wait_ge(m["p"], i + 1)
                if i >= 2:
                    pe.wait_ge(m["pt"], i - 1)
                for k in range(nk // P):
                    last = pe.transpose(PS[:, 2 + i % 2, k * P:(k + 1) * P],
                                        PB[a][:, (i % 2) * 512 + k * P:(i % 2) * 512 + (k + 1) * P], ident)
                last.then_inc(m["turned"], 1)

            def values(h):
                k0, nk = att_keys(a, 2 * h)
                pe.wait_ge(m["pt"], 2 * h + 2)
                if h >= 2:
                    pe.wait_ge(m["low"], h - 1)
                pt = PT[a][h % 2].rearrange("p (k q) -> p k q", k=4)
                for k in range(nk // P):
                    kb = k0 // P + k
                    v = KV[:, kb, 256 + ((h % 4) // 2) * P:256 + ((h % 4) // 2 + 1) * P] if a == 0 else V1[:, kb, h * P:(h + 1) * P]
                    last = pe.matmul(PS[:, 4 + h % 2, 0:256], v, pt[:, k, :], start=(k == 0), stop=(k == nk // P - 1))
                last.then_inc(m["o"], 1)

            for i in range(n + 3):
                if i < n:
                    scores(i)
                if 2 <= i < n + 2:
                    turn(i - 2)
                if i >= 3 and (i - 3) % 2 == 1:
                    values((i - 3) // 2)

        def att_out(a, h, t):
            if a == 0:
                return t[0][:, 4 + h % 4, (h // 4) * SEQ:(h // 4 + 1) * SEQ]
            return t[1][:, h, :]

        def att_act(act, a):
            m = att[a]
            n = ATT[a]["n"]

            def exp(i):
                nk = att_keys(a, i)[1]
                act.wait_ge(m["bias"], i + 1)
                if i >= 2:
                    act.wait_ge(m["turned"], i - 1)
                act.activation(PB[a][:, (i % 2) * 512:(i % 2) * 512 + nk], PS[:, i % 2, 0:nk], ACT.Exp,
                               bias=sc[:, NBI + i:NBI + i + 1], scale=ATT[a]["scale"],
                               accum_out=sc[:, SUM + i:SUM + i + 1]).then_inc(m["exp"], 1)

            def copy(i):
                nk = att_keys(a, i)[1]
                h = i // 2
                act.wait_ge(m["turned"], i + 1)
                if h >= 2:
                    act.wait_ge(m["o"], h - 1)
                pt = PT[a][h % 2].rearrange("p (k q) -> p k q", k=4)
                act.activation(pt[:, 0:nk // P, (i % 2) * P:(i % 2 + 1) * P],
                               PS[:, 2 + i % 2, 0:nk].rearrange("p (k q) -> p k q", q=P), ACT.Copy).then_inc(m["pt"], 1)

            def upper(h):
                act.wait_ge(m["o"], h + 1)
                act.activation(att_out(a, h, (ahk, och)), PS[:, 4 + h % 2, 0:256], ACT.Copy).then_inc(m["high"], 1)

            for i in range(n + 3):
                if i < n:
                    exp(i)
                if 2 <= i < n + 2:
                    copy(i - 2)
                if i >= 3 and (i - 3) % 2 == 1:
                    upper((i - 3) // 2)

        def att_dve(dve, a, link):
            m = att[a]
            n = ATT[a]["n"]

            def peak(i):
                nk = att_keys(a, i)[1]
                dve.wait_ge(m["scored"], i + 1)
                link(dve.tensor_reduce(sc[:, MX + i:MX + i + 1], PS[:, i % 2, 0:nk], AXX, ALU.max))
                dve.tensor_scalar(sc[:, NBI + i:NBI + i + 1], sc[:, MX + i:MX + i + 1], -ATT[a]["scale"], None,
                                  ALU.mult).then_inc(m["bias"], 1)

            def norm(i):
                nk = att_keys(a, i)[1]
                dve.wait_ge(m["exp"], i + 1)
                link(dve.reciprocal(sc[:, REC + i:REC + i + 1], sc[:, SUM + i:SUM + i + 1]))
                p = PB[a][:, (i % 2) * 512:(i % 2) * 512 + nk]
                dve.tensor_scalar(p, p, sc[:, REC + i:REC + i + 1], None, ALU.mult).then_inc(m["p"], 1)

            def lower(h):
                dve.wait_ge(m["high"], h + 1)
                dve.tensor_tensor(att_out(a, h, (alk, ocl)), PS[:, 4 + h % 2, 0:256],
                                  att_out(a, h, (ahk, och)).bitcast(F32), ALU.subtract).then_inc(m["low"], 1)

            for i in range(n + 3):
                if i < n:
                    peak(i)
                if 1 <= i < n + 1:
                    norm(i - 1)
                if i >= 3 and (i - 3) % 2 == 1:
                    lower((i - 3) // 2)

        def ada_low(dve, g, lows, it, n, buf, bank):
            for q in range(3):
                for j in (2 * q, 2 * q + 1):
                    if lows:
                        vector_low(dve, n + j + 3, it)
                dve.wait_ge(unit_used, n + 2 * q + 2 + it * 6)
                if q == 0:
                    dve.wait_ge(s["cols_turned"], g)
                dve.tensor_copy(rows[buf][32 * q:32 * q + 4, :], PS[0:4, bank + q, :]).then_inc(s["rows_copied"], 1)

        def cols_take(dve, g, bank):
            dve.wait_ge(s["cols_turned"], g + 1)
            t = PS[:, bank, 0:384].rearrange("p (k q r) -> p q k r", k=4, q=3)
            dst = modall[:, bass.ds(g * 12, 12), :].rearrange("p (q k) s -> p q k s", q=3)
            dve.tensor_copy(dst, t[:, :, :, 0:2]).then_inc(s["cols_taken"], 1)
            dve.wait_ge(s["cols_taken"], g * 2 + 1)
            dve.tensor_tensor(dst, dst, t[:, :, :, 2:4], ALU.add).then_inc(s["cols_taken"], 1)

        def rows_of(w):
            return w.rearrange("(k p) n -> p k n", p=P)

        abin, about = rows_of(ab_w_in[0]), rows_of(ab_w_out[0])
        fin, fout = rows_of(ffn_w_in[0]), rows_of(ffn_w_out[0])
        wdq, wdkv, wuq, wukv, wo = (rows_of(w[0]) for w in (mla_w_dq, mla_w_dkv, mla_w_uq, mla_w_ukv, mla_w_o))
        MLA_W = [4 * CQ] * 2 + [4 * (CKV + CROPE)] * 2 + [1536] * 3 + [2048] * 2 + [2048] * 4

        def mla_src(j):
            if j < 2:
                return wdq[:, 4 * j:4 * j + 4, :]
            if j < 4:
                return wdkv[:, 4 * (j - 2):4 * (j - 2) + 4, :]
            if j < 7:
                return wuq[:, j - 4:j - 3, :]
            if j < 9:
                return wukv[:, j - 7:j - 6, :]
            return wo[:, 2 * (j - 9):2 * (j - 9) + 2, :]

        NV = NE

        U0 = N_MOE
        UC = N_MOE + 4

        block = es.enter_context(nc.Block())

        @block.sync
        def _(sp):
            sp.dma_start(K[:, :], consts).then_inc(s["consts_loaded"], 16)
            pk, pb = tmp[:, 0:P], tmp[:, P:2 * P]
            for r, n, src in ((0, 8, c[0].rearrange("(k p) -> k p", p=P)), (8, 8, c_ctx.rearrange("(k p) -> k p", p=P)),
                              (16, 16, g_pre_mix.rearrange("l (k p) -> (l k) p", p=P)),
                              (32, 16, g_pre_ffn.rearrange("l (k p) -> (l k) p", p=P)),
                              (48, 3, mla_qnorm_g[0].rearrange("(k p) -> k p", p=P)),
                              (51, 2, mla_kvnorm_g[0].rearrange("(k p) -> k p", p=P)), (53, 4, a_bs[0]),
                              (57, 16, g_post_mix.rearrange("l (k p) -> (l k) p", p=P)),
                              (73, 16, g_post_ffn.rearrange("l (k p) -> (l k) p", p=P))):
                sp.dma_start(pk[r:r + n, :], src).then_inc(s["pack_loaded"], 16)
            sp.dma_start(pb[0:96, :], ada_b.rearrange("l (k p) -> (l k) p", p=P)).then_inc(s["pack_loaded"], 16)

            def ada_group(layer, n, it, col):
                w = rows_of(ada_w[layer])
                for q in range(3):
                    for kh in range(2):
                        load_unit(sp, n + 2 * q + kh, w[:, 4 * kh:4 * kh + 4, bass.ds(col + q * 512, 512)], it)

            def abin_chunk(ch):
                for kh in range(2):
                    load_unit(sp, N_ABIN[ch] + kh, abin[:, 4 * kh:4 * kh + 4, ch * 512:(ch + 1) * 512])

            ada_group(0, N_ADA[0], 0, 0)
            ada_group(0, N_ADA[1], 0, 1536)
            abin_chunk(0)
            ada_group(0, N_ADA[2], 0, 2 * 1536)
            abin_chunk(1)
            ada_group(0, N_ADA[3], 0, 3 * 1536)
            abin_chunk(2)
            abin_chunk(3)
            for j in range(4):
                load_unit(sp, N_ABOUT + j, about[:, 2 * j:2 * j + 2, :])

            def fin_pair(n, it, col):
                load_unit(sp, n, fin[:, :, bass.ds(col, 256)], it)
                load_unit(sp, n + 1, fin[:, :, bass.ds(col + D_FF, 256)], it)

            def fin_part(n, it, col, ada_col, pairs):
                fin_pair(n, it, col)
                ada_group(1, n + 2, it, ada_col)
                for j in range(1, pairs):
                    fin_pair(n + 6 + 2 * j, it, col + j * 256)

            fin_part(N_FIN, 0, 0, 0, 3)
            with sp.Fori(0, 2) as i:
                fin_part(N_FIN + 12, i * 2, i * 768 + 768, i * 1536 + 1536, 3)
            fin_part(N_FIN + 36, 0, 9 * 256, 3 * 1536, 2)
            for j in range(11):
                load_unit(sp, N_FOUT + j, fout[:, 2 * j:2 * j + 2, :])
            for j in range(13):
                load_unit(sp, N_MLA + j, mla_src(j))

            def visit(v, e):
                wi, wo_ = rows_of(moe_w_in[0, e]), rows_of(moe_w_out[0, e])

                def up(n, it, col):
                    for j in range(4):
                        load_unit(sp, n + j, wi[:, 4 * (j % 2):4 * (j % 2) + 4, bass.ds(col + (j // 2) * D_FFE, FCH)], it)

                def down(n, it, blk):
                    for j in range(2):
                        load_unit(sp, n + j, wo_[:, bass.ds(blk + 2 * j, 2), :], it)

                up(U0, v * NCH, 0)
                with sp.Fori(0, 3) as i:
                    for j in range(2):
                        up(UC + 6 * j, v * NCH + i * 2, i * 1024 + (j + 1) * FCH)
                        down(UC + 4 + 6 * j, v * NCH + i * 2, i * 8 + j * 4)
                down(UC + 36, v * NCH, 24)

            with sp.Fori(0, NE) as e:
                visit(e, e)
            sp.wait_ge(s["route_ready"], 1)
            with sp.Fori(0, NE) as e:
                n = sp.value_load(cnt[0:1, bass.ds(e, 1)], min_val=0, max_val=SEQ)
                with sp.If(n > P):
                    visit(e + NV, e)
                with sp.Else():
                    for j in range(6):
                        r = (N_MOE + j) % RAW
                        sp.wait_ge(raw_loaded[r], 16 * ((N_MOE + j) // RAW) + (e + NV) * (16 * NCH))
                        sp.sem_inc(raw_loaded[r], 16 * NCH)
            for b in range(LB):
                sp.wait_ge(s["resid_done" if b % 2 else "resid_pool"], 6)
                sp.dma_start(out[0, b * P:(b + 1) * P, :], X[:, b, :]).then_inc(s["out_stored"], 16)
            sp.wait_ge(s["out_stored"], 16 * LB)

        @block.gpsimd
        def _(pool):

            def unit(n):
                if n % SPL == SPL - 1:
                    pool_low(pool, n, 0, MLA_W[n - N_MLA] if N_MLA <= n < N_MOE else UNIT)

            for n in range(12):
                unit(n)
            pre_pool(pool, 0)
            for n in range(12, N_FIN + 3):
                unit(n)
            res_pool(pool, 0)
            pre_pool(pool, 1)
            for n in range(N_FIN + 3, N_FIN + 12):
                unit(n)
            with pool.Fori(0, 2) as i:
                for n in range(N_FIN + 12, N_FIN + 24):
                    if n % SPL == SPL - 1:
                        pool_low(pool, n, i * 2)
            for n in range(N_FIN + 36, N_MLA + 3):
                unit(n)
            res_pool(pool, 1)
            pre_pool(pool, 2)
            for n in range(N_MLA + 3, N_MOE):
                unit(n)
            res_pool(pool, 2)
            pre_pool(pool, 3)
            first = next(n for n in range(N_MOE, N_MOE + 3) if n % SPL == SPL - 1)
            with pool.Fori(0, NE) as e:
                with pool.Fori(0, NCH) as i:
                    pool_low(pool, first, e * NCH + i)
                    pool_low(pool, first + 3, e * NCH + i)
            pool.wait_ge(s["route_ready"], 1)
            with pool.Fori(0, NE) as e:
                n = pool.value_load(cnt[0:1, bass.ds(e, 1)], min_val=0, max_val=SEQ)
                with pool.If(n > P):
                    with pool.Fori(0, NCH) as i:
                        pool_low(pool, first, (e + NV) * NCH + i)
                        pool_low(pool, first + 3, (e + NV) * NCH + i)
                with pool.Else():
                    pool.wait_ge(low_made[SPL - 1], 2 * (first // SPL) + (e + NV) * (4 * NCH))
                    pool.sem_inc(low_made[SPL - 1], 2 * NCH)
            res_pool(pool, 3)

        @block.scalar
        def _(act):
            for b, src in enumerate((x[0], ctx[0])):
                act.dma_start(X[:, 2 * b:2 * b + 2, :], src.rearrange("(b p) d -> p b d", p=P)).then_inc(s["x_loaded"], 16)
            act.dma_start(anb, a_norm_g[0].partition_broadcast(P)).then_inc(s["mixc_loaded"], 16)
            act.dma_start(qgb, b_qnorm_g[0].partition_broadcast(P)).then_inc(s["mixc_loaded"], 16)
            act.dma_start(kgb, b_knorm_g[0].partition_broadcast(P)).then_inc(s["mixc_loaded"], 16)
            act.dma_start(work[:, 10240:10752].rearrange("p (g i) -> p g i", g=4),
                          a_ws[0].rearrange("g i j -> i g j")).then_inc(s["mixc_loaded"], 16)

            act.wait_ge(s["pack_turned"], 1)
            act.activation(sil[:, :, :].rearrange("p s k -> p (s k)"), PS[:, 7, 0:16], ACT.Silu).then_inc(s["silu_ready"], 1)
            act.wait_ge(s["silu_ready"], 1)
            act.activation(act4[:, :, 0:2], sil[:, :, :].rearrange("p s k -> p k s"), ACT.Copy).then_inc(s["act_high"], 1)
            pre_act(act, 0)
            for n in range(12):
                split_high(act, n)

            pre_act_chunks(act, 0)
            for n in range(12, 15):
                split_high(act, n)
            ahead = 15
            for ch in range(4):
                end = N_ABIN[ch] + 2
                for n in range(ahead, min(end + 3, N_ABOUT)):
                    split_high(act, n)
                ahead = max(ahead, min(end + 3, N_ABOUT))
                act.wait_ge(unit_used, end)
                for b in range(NB):
                    src = PS[:, (ch % 2) * 4 + b, :]
                    if ch < 2:
                        act.activation((U, V)[ch][:, b, :], src, ACT.Gelu_apprx_tanh).then_inc(s["gelu_made"], 1)
                    else:
                        act.activation((Q, KV)[ch - 2][:, b, :], src, ACT.Copy).then_inc(s[("q_copied", "kv_copied")[ch - 2]], 1)
                if ch >= 2:
                    act.wait_ge(s["gn_ms"], ch - 1)
                    act.activation(sc[:, 96:112], sc[:, 96:112], ACT.Sqrt).then_inc(s["gn_root"], 1)

            def gates_out(i, n):
                act.wait_ge(s["gate_turned"], i + 1)
                act.activation(grow[0:8 * n, :], PS[0:8 * n, 5, 0:P], ACT.Copy).then_inc(s["gate_rows"], 1)
                act.wait_ge(s["gate_rows"], i + 1)
                act.dma_start(gg_dram[4 * i:4 * i + n].rearrange("g (k p) -> (g k) p", p=P), grow[0:8 * n, :]).then_inc(s["gg_stored"], 16)

            for g in range(4):
                act.wait_ge(s["cat_turned"], g + 1)
                act.activation(ahk[:, g, :], PS[:, 2 + g % 2, :], ACT.Copy).then_inc(s["cat_high"], 1)
            for n in range(N_ABOUT, N_ABOUT + 3):
                split_high(act, n)
            gates_out(0, 4)
            for h in range(6):
                if h == 4:
                    act.wait_ge(s["gn_ms"], 3)
                    act.activation(sc[:, 96:104], sc[:, 96:104], ACT.Sqrt).then_inc(s["gn_root"], 1)
                act.wait_ge(s["qk_turned"], h + 1)
                act.activation(qT[:, h, :] if h < 4 else kT[:, h - 4, :], PS[:, 6 + h % 2, :], ACT.Copy).then_inc(s["qk_ready"], 1)
            att_act(act, 0)
            act.wait_ge(att[0]["o"], 8)
            act.wait_ge(s["gg_stored"], 16)
            act.dma_start(GG, gg_dram[0:2].partition_broadcast(P)).then_inc(s["gg_loaded"], 16)
            split_high(act, N_ABOUT + 3)
            for n in range(N_FIN, N_FIN + 3):
                split_high(act, n)
            res_act(act, 0, ps_rows, (unit_used, N_ABOUT + 4))

            pre_act(act, 1)
            pre_act_chunks(act, 1)

            def ffn_silu(f0, n, it, i):
                if f0 % 2 == 0:
                    act.wait_ge(s["g_done"], f0 // 2 + 1 + i * 3)
                else:
                    act.wait_ge(unit_used, n + it * 6)
                if f0 >= 2:
                    act.wait_ge(s["hid_made"], f0 - 1 + i * 6)
                act.activation(sgf[:, f0 % 2, :], PS[:, 2 * (f0 % 2), :], ACT.Silu).then_inc(s["silu_made"], 1)

            def ffn_part(n, it, f0, i, pairs):
                for p in range(pairs):
                    m = n + (2 * p + 6 if p else 0)
                    for j in range(2):
                        ffn_silu(f0 + 2 * p + j, m + j, it, i)
                        split_high(act, m + j + 3, it)
                    if p == 0:
                        for j in range(2, 8):
                            split_high(act, m + j + 3, it)

            ffn_part(N_FIN, 0, 0, 0, 3)
            with act.Fori(0, 2) as i:
                ffn_part(N_FIN + 12, i * 2, 6, i, 3)
            ffn_part(N_FIN + 36, 0, 18, 0, 2)
            act.wait_ge(unit_used, N_FOUT)
            def hidden_high(f):
                act.wait_ge(s["hid_made"], f + 1)
                act.activation(fh[:, f % 4, :], HID[:, f, :], ACT.Copy).then_inc(s["fd_high"], 1)

            for f in range(4):
                hidden_high(f)
            for d in range(11):
                act.wait_ge(unit_used, N_FOUT + d + 1)
                for f in range(2 * d + 4, min(2 * d + 6, 22)):
                    hidden_high(f)
                n = N_FOUT + d + 3
                split_high(act, n, 0, UNIT if n < N_MLA else MLA_W[n - N_MLA])
            act.wait_ge(s["fd_ready"], 22)
            act.dma_start(GG, gg_dram[2:4].partition_broadcast(P)).then_inc(s["gg_loaded"], 16)
            res_act(act, 1, ps_rows, (unit_used, N_FOUT + 11))

            pre_act(act, 2)
            pre_act_chunks(act, 2)
            gates_out(1, 2)
            split_high(act, N_MLA + 3, 0, MLA_W[3])
            act.wait_ge(unit_used, N_MLA + 2)
            for b in range(2):
                act.activation(cqn[:, b, :], PS[:, b, 0:CQ], ACT.Copy).then_inc(s["c_copied"], 1)
            act.wait_ge(unit_used, N_MLA + 4)
            for b in range(NB):
                act.activation(ckvn[:, b, :], PS[:, 2 + b, 0:CKV], ACT.Copy).then_inc(s["c_copied"], 1)
                act.activation(kr2[:, b, 0:CROPE], PS[:, 2 + b, CKV:CKV + CROPE], ACT.Copy).then_inc(s["c_copied"], 1)
            for n in range(N_MLA + 4, N_MLA + 7):
                split_high(act, n, 0, MLA_W[n - N_MLA])
            act.wait_ge(s["gn_ms"], 4)
            act.activation(sc[:, 96:102], sc[:, 96:102], ACT.Sqrt).then_inc(s["gn_root"], 1)
            for k in range(5):
                act.wait_ge(s["c_scaled"], k + 1)
                dst = cqh[:, k, :] if k < 3 else ckh[:, k - 3, :]
                act.activation(dst, tmp[:, (k % 2) * 512:(k % 2) * 512 + (256 if k < 3 else 512)], ACT.Copy).then_inc(s["c_high"], 1)
            act.wait_ge(s["kr_turned"], 1)
            act.activation(krT, PS[:, 7, :], ACT.Copy).then_inc(s["kr_copied"], 1)
            for b in range(2):
                act.wait_ge(s["qr_done"], b + 1)
                act.activation(qrt[:, b, :], PS[:, b, :], ACT.Copy).then_inc(s["qr_copied"], 1)
            for h in range(8):
                act.wait_ge(*((s["qn_done"], h + 1) if h < 7 else (unit_used, N_MLA + 7)))
                act.activation(qnT[:, h, :], PS[:, 2 + h % 4, 0:256], ACT.Copy).then_inc(s["qn_moved"], 1)
            for n in range(N_MLA + 7, N_MLA + 9):
                split_high(act, n, 0, MLA_W[n - N_MLA])
            for p in range(4):
                act.wait_ge(s["qr_turned"], p + 1)
                act.activation(qrT[:, p, :], PS[:, 6 + p % 2, 0:256], ACT.Copy).then_inc(s["qr_moved"], 1)
            for j in range(16):
                act.wait_ge(*((s["kv_done"], j + 1) if j < 15 else (unit_used, N_MLA + 9)))
                dst = knT[:, j, :] if j < 8 else V1[:, (j - 8) // 2, ((j - 8) % 2) * 512:((j - 8) % 2 + 1) * 512]
                act.activation(dst, PS[:, j % 6, :], ACT.Copy).then_inc(s["kv_moved"], 1)
            for n in range(N_MLA + 9, N_MLA + 12):
                split_high(act, n)
            att_act(act, 1)
            act.wait_ge(att[1]["o"], 8)
            act.wait_ge(s["gg_stored"], 32)
            act.dma_start(GGm, gg_dram[4].partition_broadcast(P)).then_inc(s["gg_loaded"], 16)
            split_high(act, N_MLA + 12)
            res_act(act, 2, ps_rows, (unit_used, N_MLA + 13))

            act.dma_start(RT, moe_router[0].rearrange("(k p) e -> p k e", p=P)).then_inc(s["rt_loaded"], 16)
            pre_act(act, 3)
            pre_act_chunks(act, 3)
            act.wait_ge(s["resid_done"], 5)
            act.dma_start(GGm, gg_dram[5].partition_broadcast(P)).then_inc(s["gg_loaded"], 16)
            act.wait_ge(s["route1"], 1)
            act.activation(rs[:, 32:34], rs[:, 32:34], ACT.Exp).then_inc(s["route_exp"], 1)

            def tokens(g, hf):
                act.wait_ge(s["xg_scaled"], g * 2 + hf + 1)
                act.activation(xgh[:, 4 * hf:4 * hf + 4, :].rearrange("p k t -> p (k t)"),
                               tmp[:, hf * 512:(hf + 1) * 512], ACT.Copy).then_inc(s["xg_high"], 1)

            def visit(v, chained):
                split_high(act, U0 + 3, v * NCH)
                silu(U0 + 2, v * NCH, 0)

                def body(n, it, par):
                    for j in range(3):
                        split_high(act, n + j, it)
                    turned(it + (n - UC) // 6 + 1, 1 - par)
                    for j in range(3, 5):
                        split_high(act, n + j, it)
                    silu(n + 2, it, par)
                    split_high(act, n + 5, it)

                with act.Fori(0, 3) as i:
                    body(UC, v * NCH + i * 2, 1)
                    body(UC + 6, v * NCH + i * 2, 0)
                split_high(act, UC + 36, v * NCH)
                split_high(act, UC + 37, v * NCH)
                if chained:
                    with act.If(v < NE - 1):
                        split_high(act, U0, v * NCH + NCH)
                turned(v * NCH + NCH, 0)
                if chained:
                    for hf in range(2):
                        tokens(v + 1, hf)

            def silu(n, it, par):
                act.wait_ge(unit_used, n + it * 6)
                act.activation(sg[:, par, :], PS[:, 2 * par, :], ACT.Silu).then_inc(s["esilu_made"], 1)

            def turned(count, par):
                act.wait_ge(s["ht_done"], count)
                act.activation(hth[:, par, :], PS[:, 4, :], ACT.Copy).then_inc(s["ht_high"], 1)

            for j in range(3):
                split_high(act, U0 + j)
            for hf in range(2):
                tokens(0, hf)
            with act.Fori(0, NE) as e:
                visit(e, True)
                with act.If(e < NE - 1):
                    for j in range(1, 3):
                        split_high(act, U0 + j, e * NCH + NCH)
            act.wait_ge(s["route_ready"], 1)
            with act.Fori(0, NE) as e:
                n = act.value_load(cnt[0:1, bass.ds(e, 1)], min_val=0, max_val=SEQ)
                v = e + NV
                with act.If(n > P):
                    for j in range(3):
                        split_high(act, U0 + j, v * NCH)
                    for hf in range(2):
                        tokens(v + 1, hf)
                    visit(v, False)
                with act.Else():
                    act.wait_ge(high_made, N_MOE + v * VISIT)
                    act.sem_inc(high_made, VISIT)
                    for name, k, more in (("xg_high", 2, 2), ("esilu_made", NCH, 0), ("ht_high", NCH, 0)):
                        act.wait_ge(s[name], v * k + more)
                        act.sem_inc(s[name], k)
            res_act(act, 3, lambda b: ACC[:, b, :], (s["acc_made"], 2 * NE + 2))

        @block.vector
        def _(dve):
            class Link:
                n = 0

                def __call__(self, ins):
                    ins.then_inc(s["dve_step"], 1)
                    self.n += 1
                    dve.wait_ge(s["dve_step"], self.n)

            link = Link()

            dve.wait_ge(s["pack_turned"], 1)
            dve.wait_ge(s["silu_ready"], 1)
            dve.tensor_copy(vec[:, 0:89], PS[:, 7, 0:89])
            dve.tensor_copy(vec[:, 96:192], PS[:, 7, 96:192]).then_inc(s["vec_ready"], 1)
            dve.wait_ge(s["act_high"], 1)
            dve.tensor_tensor(act4[:, :, 2:4], sil[:, :, :].rearrange("p s k -> p k s"),
                              act4[:, :, 0:2].bitcast(F32), ALU.subtract).then_inc(s["act_ready"], 1)

            def mod_ready(l, a0, a1):
                v = modv[:, l, a0:a1].rearrange("p a k s -> p (a k) s")
                bias = vec[:, 96 + 48 * l + 8 * a0:96 + 48 * l + 8 * a1].unsqueeze(2).broadcast_to([P, 8 * (a1 - a0), 2])
                link(dve.tensor_tensor(v, v, bias, ALU.add))

            def gain_scale(l, w):
                g = vec[:, 16 + 16 * w + 8 * l:24 + 16 * w + 8 * l].unsqueeze(2).broadcast_to([P, KD, 2])
                return dve.scalar_tensor_tensor(out=scol[:, l, w, :, :], in0=modc[:, l, w, 1, :, :], scalar=1.0,
                                                in1=g, op0=ALU.add, op1=ALU.mult)

            def gates(l, streams):
                for w in range(2):
                    for st in range(streams):
                        o = 8 * (w * streams + st)
                        last = dve.tensor_tensor(gcol[:, o:o + 8], modc[:, l, w, 2, :, st], g_post[w][:, l, :], ALU.mult)
                last.then_inc(s["gate_cols"], 1)

            link(dve.memset(rows[0][0:96, :], 0.0))
            pre_dve(dve, 0, link)
            for n in range(3):
                vector_low(dve, n)
            ada_low(dve, 0, True, 0, N_ADA[0], 0, 4)
            cols_take(dve, 0, 7)
            dve.wait_ge(s["ws_turned"], 1)
            dve.tensor_copy(wsT, PS[:, 3, :].rearrange("p (g i) -> p g i", g=4)).then_inc(s["ws_ready"], 1)
            for n in range(9, 12):
                vector_low(dve, n)
            ada_low(dve, 1, False, 0, N_ADA[1], 0, 4)
            cols_take(dve, 1, 7)
            dve.wait_ge(s["cols_taken"], 4)
            mod_ready(0, 0, 3)
            gain_scale(0, 0).then_inc(s["cols_ready"], 1)

            dve.wait_ge(s["cols_ready"], 1)
            pre_dve_chunks(dve, 0)

            def rope(t, heads, width, cc, ss, scr):
                f = width // 4
                v = t.rearrange("p (h a s f) -> p h a s f", a=2, s=2, f=f)
                w = scr.rearrange("p (h a s f) -> p h a s f", a=2, s=2, f=f)
                sv = ss.rearrange("p (a s f) -> p a s f", a=2, s=2)
                for a_ in range(2):
                    for s_ in range(2):
                        sin = sv[:, a_, s_, :].unsqueeze(1).broadcast_to([P, heads, f])
                        link(dve.tensor_tensor(w[:, :, a_, s_, :], v[:, :, a_, 1 - s_, :], sin, ALU.mult))
                th = t.rearrange("p (h w) -> p h w", h=heads)
                link(dve.tensor_tensor(th, th, cc.unsqueeze(1).broadcast_to([P, heads, width]), ALU.mult))
                return dve.tensor_tensor(t, t, scr, ALU.add)

            def mean_squares(v, groups):
                for h0 in range(0, groups, 8):
                    sq = tmp[:, :].rearrange("p (g d) -> p g d", g=8)
                    link(dve.tensor_tensor(sq, v[:, h0:h0 + 8, :], v[:, h0:h0 + 8, :], ALU.mult))
                    link(dve.tensor_reduce(sc[:, 96 + h0:104 + h0], sq, AXX, ALU.add))
                dve.tensor_scalar(sc[:, 96:96 + groups], sc[:, 96:96 + groups], 1.0 / P, EPS, ALU.mult, ALU.add).then_inc(s["gn_ms"], 1)

            for n in range(12, 17):
                vector_low(dve, n)
            ada_low(dve, 2, True, 0, N_ADA[2], 0, 4)
            cols_take(dve, 2, 7)
            for n in range(23, 25):
                vector_low(dve, n)
            ada_low(dve, 3, True, 0, N_ADA[3], 0, 0)
            cols_take(dve, 3, 3)
            dve.wait_ge(s["cols_taken"], 8)
            mod_ready(0, 3, 6)
            gates(0, 2)
            gain_scale(0, 1).then_inc(s["cols_ready"], 1)
            dve.wait_ge(s["gelu_made"], 8)
            dve.wait_ge(s["mixc_loaded"], 64)
            vg = V.rearrange("p b (g d) -> p (b g) d", d=P)
            mean_squares(vg, 16)
            vector_low(dve, 31)
            dve.wait_ge(s["gn_root"], 1)
            link(dve.reciprocal(sc[:, 112:128], sc[:, 96:112]))
            link(dve.tensor_tensor(vg, vg, sc[:, 112:128].unsqueeze(2).broadcast_to([P, 16, P]), ALU.mult))
            dve.tensor_tensor(V, V, anb.unsqueeze(1).broadcast_to([P, NB, 512]), ALU.mult).then_inc(s["vn_ready"], 1)
            dve.wait_ge(s["q_copied"], NB)
            qg = Q.rearrange("p b (g d) -> p (b g) d", d=P)
            mean_squares(qg, 16)
            dve.wait_ge(s["gn_root"], 2)
            link(dve.reciprocal(sc[:, 112:128], sc[:, 96:112]))
            link(dve.tensor_tensor(qg, qg, sc[:, 112:128].unsqueeze(2).broadcast_to([P, 16, P]), ALU.mult))
            link(dve.tensor_tensor(qg, qg, qgb.unsqueeze(1).broadcast_to([P, 16, P]), ALU.mult))
            for b in range(LB):
                last = rope(Q[:, b, :], 4, HD, K[:, C_CB + b * HD:C_CB + (b + 1) * HD],
                            K[:, C_SB + b * HD:C_SB + (b + 1) * HD], tmp[:, 0:512])
                if b < LB - 1:
                    link(last)
            last.then_inc(s["qn_ready"], 1)
            for b in range(NB):
                dve.wait_ge(s["mix_done"], b + 1)
                for g in range(4):
                    last = dve.scalar_tensor_tensor(out=U[:, b, g * P:(g + 1) * P], in0=PS[:, b % 2, g * P:(g + 1) * P],
                                                    scalar=vec[:, 53 + g:54 + g], in1=U[:, b, g * P:(g + 1) * P],
                                                    op0=ALU.add, op1=ALU.mult)
                last.then_inc(s["gated"], 1)
            for g in range(4):
                dve.wait_ge(s["cat_high"], g + 1)
                dve.tensor_tensor(alk[:, g, :], PS[:, 2 + g % 2, :], ahk[:, g, :].bitcast(F32), ALU.subtract).then_inc(s["cat_low"], 1)
            dve.wait_ge(s["kv_copied"], NB)
            dve.wait_ge(s["qn_ready"], 1)
            kv4 = KV.rearrange("p b (g d) -> p b g d", d=P)[:, :, 0:2, :]
            sq = tmp[:, :].rearrange("p (b g d) -> p b g d", b=NB, g=2)
            kss = sc[:, 96:104].rearrange("p (b g) -> p b g", b=NB)
            link(dve.tensor_tensor(sq, kv4, kv4, ALU.mult))
            link(dve.tensor_reduce(kss, sq, AXX, ALU.add))
            dve.tensor_scalar(sc[:, 96:104], sc[:, 96:104], 1.0 / P, EPS, ALU.mult, ALU.add).then_inc(s["gn_ms"], 1)
            dve.wait_ge(s["gn_root"], 3)
            link(dve.reciprocal(sc[:, 112:120], sc[:, 96:104]))
            for b in range(NB):
                kb = kv4[:, b, :, :]
                link(dve.tensor_tensor(kb, kb, sc[:, 112 + 2 * b:114 + 2 * b].unsqueeze(2).broadcast_to([P, 2, P]), ALU.mult))
                last = dve.tensor_tensor(kb, kb, kgb.unsqueeze(1).broadcast_to([P, 2, P]), ALU.mult)
                if b < LB:
                    link(last)
                    last = rope(KV[:, b, 0:256], 2, HD, K[:, C_CB + b * HD:C_CB + (b + 1) * HD],
                                K[:, C_SB + b * HD:C_SB + (b + 1) * HD], tmp[:, 0:256])
                if b < NB - 1:
                    link(last)
            last.then_inc(s["kn_ready"], 1)
            for n in range(N_ABOUT, N_ABOUT + 3):
                vector_low(dve, n)
            att_dve(dve, 0, link)
            vector_low(dve, N_ABOUT + 3)
            for n in range(N_FIN, N_FIN + 3):
                vector_low(dve, n)
            res_dve(dve, 0, ps_rows, lambda b: GG[:, b // LB, :], link)

            pre_dve(dve, 1, link)
            pre_dve_chunks(dve, 1)

            def ffn_hidden(f0, f, n, it, i):
                dve.wait_ge(s["silu_made"], f0 + 1 + i * 6)
                if f0 % 2 == 0:
                    dve.wait_ge(s["u_done"], f0 // 2 + 1 + i * 3)
                else:
                    dve.wait_ge(unit_used, n + 1 + it * 6)
                dve.tensor_tensor(HID[:, bass.ds(f, 1), :].rearrange("p a t -> p (a t)"), sgf[:, f0 % 2, :],
                                  PS[:, 2 * (f0 % 2) + 1, :], ALU.mult).then_inc(s["hid_made"], 1)

            def ffn_part(n, it, f0, i, f, g, pairs):
                for p in range(pairs):
                    m = n + (2 * p + 6 if p else 0)
                    for j in range(2):
                        ffn_hidden(f0 + 2 * p + j, f + (2 * p + j), m + j, it, i)
                        vector_low(dve, m + j + 3, it)
                    if p == 0:
                        ada_low(dve, g, True, it, m + 2, 1, 4)
                    if p == 1:
                        cols_take(dve, g, 7)

            ffn_part(N_FIN, 0, 0, 0, 0, 4, 3)
            with dve.Fori(0, 2) as i:
                ffn_part(N_FIN + 12, i * 2, 6, i, i * 6 + 6, i + 5, 3)
            ffn_part(N_FIN + 36, 0, 18, 0, 18, 7, 2)
            dve.wait_ge(s["cols_taken"], 16)
            mod_ready(1, 0, 6)
            dve.wait_ge(s["gate_rows"], 1)
            gates(1, 1)
            link(gain_scale(1, 0))
            gain_scale(1, 1).then_inc(s["cols_ready"], 1)

            def hidden_low(f):
                dve.wait_ge(s["fd_high"], f + 1)
                dve.tensor_tensor(fl[:, f % 4, :], HID[:, f, :], fh[:, f % 4, :].bitcast(F32), ALU.subtract).then_inc(s["fd_ready"], 1)

            for f in range(4):
                hidden_low(f)
            for d in range(11):
                for f in range(2 * d + 4, min(2 * d + 6, 22)):
                    hidden_low(f)
                n = N_FOUT + d + 3
                vector_low(dve, n, 0, UNIT if n < N_MLA else MLA_W[n - N_MLA])
            res_dve(dve, 1, ps_rows, lambda b: GG[:, b // LB, :], link)

            pre_dve(dve, 2, link)
            pre_dve_chunks(dve, 2)
            vector_low(dve, N_MLA + 3, 0, MLA_W[3])
            dve.wait_ge(s["c_copied"], 10)
            link(dve.tensor_tensor(tmp[:, 0:768].rearrange("p (b n) -> p b n", b=2), cqn, cqn, ALU.mult))
            link(dve.tensor_reduce(sc[:, 96:98], tmp[:, 0:768].rearrange("p (b n) -> p b n", b=2), AXX, ALU.add))
            link(dve.tensor_tensor(tmp[:, :].rearrange("p (b n) -> p b n", b=NB), ckvn, ckvn, ALU.mult))
            link(dve.tensor_reduce(sc[:, 98:102], tmp[:, :].rearrange("p (b n) -> p b n", b=NB), AXX, ALU.add))
            link(dve.tensor_scalar(sc[:, 96:98], sc[:, 96:98], 1.0 / CQ, EPS, ALU.mult, ALU.add))
            dve.tensor_scalar(sc[:, 98:102], sc[:, 98:102], 1.0 / CKV, EPS, ALU.mult, ALU.add).then_inc(s["gn_ms"], 1)
            for n in range(N_MLA + 4, N_MLA + 7):
                vector_low(dve, n, 0, MLA_W[n - N_MLA])
            for b in range(LB):
                link(rope(kr2[:, b, 0:CROPE], 1, CROPE, K[:, C_CC + b * CROPE:C_CC + (b + 1) * CROPE],
                          K[:, C_SC + b * CROPE:C_SC + (b + 1) * CROPE], tmp[:, 0:CROPE]))
            dve.tensor_copy(kr2[:, :, CROPE:2 * CROPE], kr2[:, :, 0:CROPE]).then_inc(s["kr_ready"], 1)
            dve.wait_ge(s["gn_root"], 4)
            link(dve.reciprocal(sc[:, 112:118], sc[:, 96:102]))
            for b in range(2):
                link(dve.tensor_scalar(cqn[:, b, :], cqn[:, b, :], sc[:, 112 + b:113 + b], None, ALU.mult))
            for b in range(NB):
                last = dve.tensor_scalar(ckvn[:, b, :], ckvn[:, b, :], sc[:, 114 + b:115 + b], None, ALU.mult)
                if b < NB - 1:
                    link(last)
            last.then_inc(s["c_copied"], 1)

            def c_lower(k):
                w = 256 if k < 3 else 512
                d, u = (cql[:, k, :], cqh[:, k, :]) if k < 3 else (ckl[:, k - 3, :], ckh[:, k - 3, :])
                dve.wait_ge(s["c_high"], k + 1)
                dve.tensor_tensor(d, tmp[:, (k % 2) * 512:(k % 2) * 512 + w], u.bitcast(F32), ALU.subtract).then_inc(s["c_ready"], 1)

            for k in range(5):
                w = 256 if k < 3 else 512
                dve.wait_ge(s["c_turned"], k + 1)
                if k >= 2:
                    dve.wait_ge(s["c_ready"], k - 1)
                dve.tensor_scalar(tmp[:, (k % 2) * 512:(k % 2) * 512 + w], PS[:, 6 + k % 2, 0:w], vec[:, 48 + k:49 + k], None,
                                  ALU.mult).then_inc(s["c_scaled"], 1)
                if k:
                    c_lower(k - 1)
            c_lower(4)
            for b in range(LB):
                dve.wait_ge(s["qr_copied"], b + 1)
                last = rope(qrt[:, b, :], 8, CROPE, K[:, C_CC + b * CROPE:C_CC + (b + 1) * CROPE],
                            K[:, C_SC + b * CROPE:C_SC + (b + 1) * CROPE], rot[:, b * 512:(b + 1) * 512])
                last.then_inc(s["qr_ready"], 1)
            for n in range(N_MLA + 7, N_MLA + 12):
                vector_low(dve, n)
            att_dve(dve, 1, link)
            vector_low(dve, N_MLA + 12)
            res_dve(dve, 2, ps_rows, lambda b: GGm, link)

            pre_dve(dve, 3, link)
            pre_dve_chunks(dve, 3)
            link(dve.memset(zero16, 0.0))
            link(dve.memset(rs[:, 64:192], 1.0))
            link(dve.memset(tab, 0.0))
            dve.memset(SELT, 0.0)
            dve.memset(yg, 0.0).then_inc(s["y_gated"], 1)
            dve.memset(ACC, 0.0).then_inc(s["acc_made"], 1)
            LOG, TOP, IDX, OH, POS = 0, 16, 192, 208, 34
            dve.wait_ge(s["logits_done"], 1)
            link(dve.tensor_copy(rs[:, LOG:LOG + 16], PS[:, 0, 0:16]))
            for b in range(LB):
                lg = rs[:, LOG + 8 * b:LOG + 8 * b + 8]
                top = rs[:, TOP + 8 * b:TOP + 8 * b + 8]
                link(dve.max(top, lg))
                link(dve.max_index(rs[:, IDX + 8 * b:IDX + 8 * b + 8].bitcast(U32), top, lg))
                link(dve.tensor_tensor(rs[:, 32 + b:33 + b], top[:, 1:2], top[:, 0:1], ALU.subtract))
            idxf = sc[:, 128:144]
            dve.tensor_copy(idxf, rs[:, IDX:IDX + 16].bitcast(U32)).then_inc(s["route1"], 1)
            dve.wait_ge(s["route_exp"], 1)
            link(dve.tensor_scalar(rs[:, POS:POS + 2], rs[:, 32:34], 1.0, None, ALU.add))
            link(dve.reciprocal(sc[:, 146:148], rs[:, POS:POS + 2]))
            link(dve.tensor_tensor(sc[:, 148:150], sc[:, 146:148], rs[:, 32:34], ALU.mult))
            i8 = K[:, C_I8:C_I8 + NE]
            for b in range(LB):
                g, mk, oh = tab[:, 2, b, 0:NE], tab[:, 1, b, 0:NE], rs[:, OH:OH + 8]
                link(dve.tensor_scalar(g, i8, idxf[:, 8 * b:8 * b + 1], sc[:, 146 + b:147 + b], ALU.is_equal, ALU.mult))
                link(dve.tensor_scalar(oh, i8, idxf[:, 8 * b + 1:8 * b + 2], sc[:, 148 + b:149 + b], ALU.is_equal, ALU.mult))
                link(dve.tensor_tensor(g, g, oh, ALU.add))
                link(dve.tensor_scalar(mk, i8, idxf[:, 8 * b:8 * b + 1], None, ALU.is_equal))
                link(dve.tensor_scalar(oh, i8, idxf[:, 8 * b + 1:8 * b + 2], None, ALU.is_equal))
                last = dve.tensor_tensor(mk, mk, oh, ALU.add)
                if b < LB - 1:
                    link(last)
            last.then_inc(s["mask_made"], 1)
            gsel = sc[:, 152:154]
            gslot = sc[:, 154:155]
            dve.wait_ge(s["pos_done"], 1)
            link(dve.tensor_copy(tab[:, 0, :, 0:NE], PS[:, 1, 0:16].rearrange("p (b e) -> p b e", b=LB)))
            dve.tensor_copy(cnt[:, :], PS[:, 1, 16:24]).then_inc(s["route_ready"], 1)

            def low_units(n, it, js):
                for j in js:
                    vector_low(dve, n + j, it)

            def hidden(count, n, it, par):
                dve.wait_ge(s["esilu_made"], count)
                dve.wait_ge(unit_used, n + it * 6)
                dve.tensor_tensor(hh[:, par, :], sg[:, par, :], PS[:, 2 * par + 1, :], ALU.mult).then_inc(s["h_made"], 1)

            def turned(count, par):
                dve.wait_ge(s["ht_high"], count)
                dve.tensor_tensor(htl[:, par, :], PS[:, 4, :], hth[:, par, :].bitcast(F32), ALU.subtract).then_inc(s["ht_ready"], 1)

            def select(g, e, base):
                for b in range(LB):
                    dve.tensor_scalar(SEL[:, b, :], K[:, C_IOTA + base:C_IOTA + base + P],
                                      tab[:, 0, b, bass.ds(e, 1)], tab[:, 1, b, bass.ds(e, 1)], ALU.is_equal, ALU.mult)
                    last = dve.tensor_copy(gsel[:, b:b + 1], tab[:, 2, b, bass.ds(e, 1)])
                last.then_inc(s["sel_made"], 1)

            def scaled(g, hf):
                dve.wait_ge(s["gathered"], g * 2 + hf + 1)
                for k in range(4 * hf, 4 * hf + 4):
                    last = dve.tensor_scalar(tmp[:, k * P:(k + 1) * P], PS[:, 2 + hf, (k % 4) * P:(k % 4 + 1) * P],
                                             scol[:, 1, 1, k, 0:1], modc[:, 1, 1, 0, k, 0:1], ALU.mult, ALU.add)
                last.then_inc(s["xg_scaled"], 1)

            def tokens(g, hf):
                dve.wait_ge(s["xg_high"], g * 2 + hf + 1)
                dve.tensor_tensor(xgl[:, 4 * hf:4 * hf + 4, :].rearrange("p k t -> p (k t)"), tmp[:, hf * 512:(hf + 1) * 512],
                                  xgh[:, 4 * hf:4 * hf + 4, :].rearrange("p k t -> p (k t)").bitcast(F32),
                                  ALU.subtract).then_inc(s["xg_ready"], 1)

            def accumulate(w):
                dve.wait_ge(s["scattered"], w + 2)
                dve.wait_ge(s["acc_made"], w + 2)
                dve.tensor_tensor(ACC.rearrange("p b n -> p (b n)"), ACC.rearrange("p b n -> p (b n)"),
                                  PS[:, 2:6, :].rearrange("p a n -> p (a n)"), ALU.add).then_inc(s["acc_made"], 1)

            def visit(v, e, chained):
                low_units(U0, v * NCH, (3,))
                if chained:
                    accumulate(v - 1)
                hidden(v * NCH + 1, U0 + 4, v * NCH, 0)
                dve.wait_ge(s["selt_done"], v + 1)
                dve.tensor_copy(SELT, PS[:, 5, 0:256])
                dve.tensor_copy(gslot, PS[:, 5, 256:257]).then_inc(s["selt_copied"], 1)
                if chained:
                    select(v + 1, e + 1, 0)

                def body(n, it, par):
                    count = it + (n - UC) // 6 + 1
                    low_units(n, it, (0, 1, 2))
                    turned(count, 1 - par)
                    low_units(n, it, (3, 4, 5))
                    hidden(count + 1, n + 4, it, par)

                with dve.Fori(0, 3) as i:
                    body(UC, v * NCH + i * 2, 1)
                    body(UC + 6, v * NCH + i * 2, 0)
                low_units(UC + 36, v * NCH, (0, 1))
                if chained:
                    scaled(v + 1, 0)
                turned(v * NCH + NCH, 0)
                if chained:
                    scaled(v + 1, 1)
                    for hf in range(2):
                        tokens(v + 1, hf)
                    with dve.If(e < NE - 1):
                        low_units(U0, v * NCH + NCH, (0,))
                dve.wait_ge(unit_used, N_MOE + VISIT + v * VISIT)
                dve.wait_ge(s["selt_copied"], v + 1)
                dve.tensor_scalar(yg, PS[:, 6:8, :].rearrange("p a n -> p (a n)"), gslot, None, ALU.mult).then_inc(s["y_gated"], 1)
                if chained:
                    with dve.If(e < NE - 1):
                        low_units(U0, v * NCH + NCH, (1, 2))
                else:
                    accumulate(v)

            def gather_first(g, e, base, it):
                select(g, e, base)
                low_units(U0, it, (0,))
                for hf in range(2):
                    scaled(g, hf)
                for hf in range(2):
                    tokens(g, hf)
                low_units(U0, it, (1, 2))

            gather_first(0, 0, 0, 0)
            with dve.Fori(0, NE) as e:
                visit(e, e, True)
            accumulate(NE - 1)
            dve.wait_ge(s["route_ready"], 1)
            with dve.Fori(0, NE) as e:
                n = dve.value_load(cnt[0:1, bass.ds(e, 1)], min_val=0, max_val=SEQ)
                v = e + NV
                with dve.If(n > P):
                    gather_first(v + 1, e, P, v * NCH)
                    visit(v, e, False)
                with dve.Else():
                    for sl in range(SPL):
                        m = makers(sl)
                        before = m * len([n for n in range(N_MOE) if n % SPL == sl])
                        dve.wait_ge(low_made[sl], before + v * (2 * NCH * m))
                        dve.sem_inc(low_made[sl], 2 * NCH)
                    for name, k, more in (("sel_made", 1, 1), ("xg_scaled", 2, 2), ("xg_ready", 2, 2), ("selt_copied", 1, 0),
                                          ("h_made", NCH, 0), ("ht_ready", NCH, 0), ("y_gated", 1, 1), ("acc_made", 1, 2)):
                        dve.wait_ge(s[name], v * k + more)
                        dve.sem_inc(s[name], k)
            dve.wait_ge(s["acc_made"], 2 * NE + 2)
            res_dve(dve, 3, lambda b: ACC[:, b, :], lambda b: GGm, link)

        @block.tensor
        def _(pe):
            pe.wait_ge(s["consts_loaded"], 16)
            pe.wait_ge(s["pack_loaded"], 16 * 10)
            pe.transpose(PS[:, 7, 0:89], tmp[0:89, 0:P], K[0:89, C_ID:C_ID + 89])
            pe.transpose(PS[:, 7, 96:192], tmp[0:96, P:2 * P], K[0:96, C_ID:C_ID + 96]).then_inc(s["pack_turned"], 1)
            pe.wait_ge(s["act_ready"], 1)

            def ada(n, it, g, bank):
                for q in range(3):
                    if type(g) is not int or g > 0:
                        pe.wait_ge(s["rows_copied"], (g - 1) * 3 + (q + 1))
                    for kh in range(2):
                        u = n + 2 * q + kh
                        unit_ready(pe, u, it)
                        wh, wl = halves(u, 4)
                        for k in range(4):
                            a = act4[:, 4 * kh + k, :]
                            pe.matmul(PS[0:4, bank + q, :], a, wh[:, k, :], start=(kh == 0 and k == 0), stop=False)
                            last = pe.matmul(PS[0:4, bank + q, :], a, wl[:, k, :], start=False, stop=(kh == 1 and k == 3))
                        last.then_inc(unit_used, 1)

            def ada_turn(g, buf, bank):
                pe.wait_ge(s["rows_copied"], g * 3 + 3)
                if type(g) is not int or g > 0:
                    pe.wait_ge(s["cols_taken"], g * 2)
                for k in range(4):
                    last = pe.transpose(PS[:, bank, k * 96:(k + 1) * 96], rows[buf][0:96, k * P:(k + 1) * P],
                                        K[0:96, C_ID:C_ID + 96])
                last.then_inc(s["cols_turned"], 1)

            pe.wait_ge(s["vec_ready"], 1)
            ada(N_ADA[0], 0, 0, 4)
            ada_turn(0, 0, 7)
            pe.wait_ge(s["mixc_loaded"], 64)
            for g in range(4):
                last = pe.transpose(PS[:, 3, g * P:(g + 1) * P], work[:, 10240 + g * P:10240 + (g + 1) * P], ident)
            last.then_inc(s["ws_turned"], 1)
            ada(N_ADA[1], 0, 1, 4)
            ada_turn(1, 0, 7)

            pe.wait_ge(s["ws_ready"], 1)
            pre_pe(pe, 0)
            pre_done(pe, 0)
            for ch in range(4):
                if ch in (1, 2):
                    bank = 4 * (ch % 2)
                    if ch == 2:
                        pe.wait_ge(s["gelu_made"], NB)
                    ada(N_ADA[ch + 1], 0, ch + 1, bank)
                    ada_turn(ch + 1, 0, bank + 3)
                    pe.wait_ge(s["rows_copied"], 3 * (ch + 2))
                for kh in range(2):
                    u = N_ABIN[ch] + kh
                    unit_ready(pe, u)
                    wh, wl = halves(u, 4)
                    for b in range(NB):
                        if kh == 0 and ch >= 2:
                            pe.wait_ge(s["gelu_made"], (ch - 2) * NB + b + 1)
                        if kh == 0 and ch in (1, 2) and b == 3:
                            pe.wait_ge(s["cols_taken"], 2 * (ch + 2))
                        for k in range(4):
                            kk = 4 * kh + k
                            last = product(pe, PS[:, (ch % 2) * 4 + b, :], ahk[:, kk, b * P:(b + 1) * P],
                                           alk[:, kk, b * P:(b + 1) * P], wh[:, k, :], wl[:, k, :],
                                           kk == 0, kk == KD - 1)
                    last.then_inc(unit_used, 1)
            pe.wait_ge(s["vn_ready"], 1)
            pe.wait_ge(s["q_copied"], NB)
            for b in range(NB):
                if b >= 2:
                    pe.wait_ge(s["gated"], b - 1)
                for g in range(4):
                    last = pe.matmul(PS[:, b % 2, g * P:(g + 1) * P], wsT[:, g, :], V[:, b, g * P:(g + 1) * P],
                                     start=True, stop=True)
                last.then_inc(s["mix_done"], 1)
            pe.wait_ge(s["gated"], NB)
            for g in range(4):
                if g >= 2:
                    pe.wait_ge(s["cat_low"], g - 1)
                for b in range(NB):
                    last = pe.transpose(PS[:, 2 + g % 2, b * P:(b + 1) * P], U[:, b, g * P:(g + 1) * P], ident)
                last.then_inc(s["cat_turned"], 1)
            pe.wait_ge(s["qn_ready"], 1)
            pe.wait_ge(s["kv_copied"], NB)
            pe.wait_ge(s["gate_cols"], 1)
            pe.transpose(PS[0:32, 5, 0:P], gcol[:, 0:32], ident).then_inc(s["gate_turned"], 1)
            for h in range(6):
                if h == 4:
                    pe.wait_ge(s["kn_ready"], 1)
                if h >= 2:
                    pe.wait_ge(s["qk_ready"], h - 1)
                for b in range(NB):
                    t = Q[:, b, h * P:(h + 1) * P] if h < 4 else KV[:, b, (h - 4) * P:(h - 3) * P]
                    last = pe.transpose(PS[:, 6 + h % 2, b * P:(b + 1) * P], t, ident)
                last.then_inc(s["qk_turned"], 1)
            pe.wait_ge(s["qk_ready"], 6)
            pe.wait_ge(s["cat_low"], 4)
            att_pe(pe, 0)
            pe.wait_ge(att[0]["low"], 8)
            for j in range(4):
                u = N_ABOUT + j
                unit_ready(pe, u)
                wh, wl = halves(u, 2)
                for b in range(NB):
                    for k in range(2):
                        kk = 2 * j + k
                        for hf in range(2):
                            last = product(pe, PS[:, 2 * b + hf, :], ahk[:, kk, b * P:(b + 1) * P], alk[:, kk, b * P:(b + 1) * P],
                                           wh[:, k, hf * 512:(hf + 1) * 512], wl[:, k, hf * 512:(hf + 1) * 512],
                                           kk == 0, kk == KD - 1)
                    if j == 3 and b < NB - 1:
                        last.then_inc(s["y_done"], 1)
                last.then_inc(unit_used, 1)

            pre_pe(pe, 1)
            pre_done(pe, 1)

            def ffn_pair(f0, n, it, i):
                for j in range(2):
                    f = f0 + j
                    for gu in range(2):
                        if j == 0:
                            unit_ready(pe, n + gu, it)
                        if gu == 0 and f >= 2:
                            pe.wait_ge(s["hid_made"], f - 1 + i * 6)
                        wh, wl = (t[:, :, j * P:(j + 1) * P] for t in halves(n + gu, KD))
                        for k in range(KD):
                            last = product(pe, PS[:, 2 * (f % 2) + gu, :], wh[:, k, :], wl[:, k, :], ahk[:, k, :], alk[:, k, :],
                                           k == 0, k == KD - 1)
                        last.then_inc(s[("g_done", "u_done")[gu]] if j == 0 else unit_used, 1)

            def ffn_part(n, it, f0, i, g, pairs):
                for p in range(pairs):
                    ffn_pair(f0 + 2 * p, n + (2 * p + 6 if p else 0), it, i)
                    if p == 0:
                        ada(n + 2, it, g, 4)
                    if p == 1:
                        ada_turn(g, 1, 7)

            ffn_part(N_FIN, 0, 0, 0, 4, 3)
            with pe.Fori(0, 2) as i:
                ffn_part(N_FIN + 12, i * 2, 6, i, i + 5, 3)
            ffn_part(N_FIN + 36, 0, 18, 0, 7, 2)
            pe.wait_ge(s["cols_taken"], 16)
            pe.wait_ge(s["hid_made"], 22)
            for d in range(11):
                u = N_FOUT + d
                unit_ready(pe, u)
                wh, wl = halves(u, 2)
                for k in range(2):
                    f = 2 * d + k
                    pe.wait_ge(s["fd_ready"], f + 1)
                    for b in range(NB):
                        for hf in range(2):
                            last = product(pe, PS[:, 2 * b + hf, :], fh[:, f % 4, b * P:(b + 1) * P], fl[:, f % 4, b * P:(b + 1) * P],
                                           wh[:, k, hf * 512:(hf + 1) * 512], wl[:, k, hf * 512:(hf + 1) * 512],
                                           f == 0, f == 21)
                        if f == 21 and b < NB - 1:
                            last.then_inc(s["y_done"], 1)
                last.then_inc(unit_used, 1)

            pre_pe(pe, 2)
            pe.wait_ge(s["gate_cols"], 2)
            pe.transpose(PS[0:16, 5, 0:P], gcol[:, 0:16], ident).then_inc(s["gate_turned"], 1)
            pre_done(pe, 2)
            for j in range(4):
                if j == 2:
                    pe.wait_ge(s["gate_rows"], 2)
                u = N_MLA + j
                unit_ready(pe, u)
                wh, wl = halves(u, 4, MLA_W[j])
                w = CQ if j < 2 else CKV + CROPE
                for b in range(LB if j < 2 else NB):
                    for k in range(4):
                        kk = 4 * (j % 2) + k
                        last = product(pe, PS[:, b if j < 2 else 2 + b, 0:w], ahk[:, kk, b * P:(b + 1) * P],
                                       alk[:, kk, b * P:(b + 1) * P], wh[:, k, :], wl[:, k, :], kk == 0, kk == KD - 1)
                last.then_inc(unit_used, 1)
            pe.wait_ge(s["kr_ready"], 1)
            pe.wait_ge(s["c_copied"], 11)
            for k in range(5):
                if k >= 2:
                    pe.wait_ge(s["c_scaled"], k - 1)
                for b in range(LB if k < 3 else NB):
                    t = cqn[:, b, k * P:(k + 1) * P] if k < 3 else ckvn[:, b, (k - 3) * P:(k - 2) * P]
                    last = pe.transpose(PS[:, 6 + k % 2, b * P:(b + 1) * P], t, ident)
                last.then_inc(s["c_turned"], 1)
            pe.wait_ge(s["c_scaled"], 4)
            for b in range(NB):
                last = pe.transpose(PS[:, 7, b * P:(b + 1) * P], kr2[:, b, :], ident)
            last.then_inc(s["kr_turned"], 1)
            for j in range(3):
                unit_ready(pe, N_MLA + 4 + j)
            pe.wait_ge(s["c_ready"], 3)
            uq = [[t.rearrange("p a (h d) -> p (a h) d", h=8) for t in halves(N_MLA + 4 + k, 1, 1536)] for k in range(3)]
            for b in range(LB):
                for k in range(3):
                    wh, wl = (t[:, :, HD:HD + CROPE] for t in uq[k])
                    last = product(pe, PS[:, b, :], cqh[:, k, b * P:(b + 1) * P], cql[:, k, b * P:(b + 1) * P], wh, wl, k == 0, k == 2)
                last.then_inc(s["qr_done"], 1)
            for h in range(8):
                if h >= 4:
                    pe.wait_ge(s["qn_moved"], h - 3)
                for k in range(3):
                    wh, wl = (t[:, h, 0:HD] for t in uq[k])
                    last = product(pe, PS[:, 2 + h % 4, 0:256], wh, wl, cqh[:, k, :], cql[:, k, :], k == 0, k == 2)
                if h < 7:
                    last.then_inc(s["qn_done"], 1)
            last.then_inc(unit_used, 3)
            pe.wait_ge(s["kr_copied"], 1)
            pe.wait_ge(s["qr_ready"], LB)
            for p in range(4):
                if p >= 2:
                    pe.wait_ge(s["qr_moved"], p - 1)
                for b in range(LB):
                    last = pe.transpose(PS[:, 6 + p % 2, b * P:(b + 1) * P], qrt[:, b, p * P:(p + 1) * P], ident)
                last.then_inc(s["qr_turned"], 1)
            for j in range(2):
                unit_ready(pe, N_MLA + 7 + j)
            pe.wait_ge(s["c_ready"], 5)
            pe.wait_ge(s["qn_moved"], 8)
            ukv = [[t.rearrange("p a (h d) -> p (a h) d", h=8) for t in halves(N_MLA + 7 + k, 1)] for k in range(2)]
            for j in range(16):
                if j >= 6:
                    pe.wait_ge(s["kv_moved"], j - 5)
                for k in range(2):
                    if j < 8:
                        wh, wl = (t[:, j, 0:HD] for t in ukv[k])
                        last = product(pe, PS[:, j % 6, :], wh, wl, ckh[:, k, :], ckl[:, k, :], k == 0, k == 1)
                    else:
                        b, hf = (j - 8) // 2, (j - 8) % 2
                        wh, wl = (t[:, 4 * hf:4 * hf + 4, HD:2 * HD] for t in ukv[k])
                        last = product(pe, PS[:, j % 6, :], ckh[:, k, b * P:(b + 1) * P], ckl[:, k, b * P:(b + 1) * P], wh, wl, k == 0, k == 1)
                if j < 15:
                    last.then_inc(s["kv_done"], 1)
            last.then_inc(unit_used, 2)
            pe.wait_ge(s["kv_moved"], 16)
            pe.wait_ge(s["qr_moved"], 4)
            att_pe(pe, 1)
            pe.wait_ge(att[1]["low"], 8)
            for j in range(4):
                u = N_MLA + 9 + j
                unit_ready(pe, u)
                wh, wl = halves(u, 2)
                for b in range(LB):
                    for k in range(2):
                        kk = 2 * j + k
                        for hf in range(2):
                            last = product(pe, PS[:, 2 * b + hf, :], och[:, kk, b * P:(b + 1) * P], ocl[:, kk, b * P:(b + 1) * P],
                                           wh[:, k, hf * 512:(hf + 1) * 512], wl[:, k, hf * 512:(hf + 1) * 512],
                                           kk == 0, kk == KD - 1)
                    if j == 3 and b < LB - 1:
                        last.then_inc(s["y_done"], 1)
                last.then_inc(unit_used, 1)

            pre_pe(pe, 3)
            pre_done(pe, 3)
            pe.wait_ge(s["rt_loaded"], 16)
            for b in range(LB):
                for k in range(KD):
                    for t in (ahk, alk):
                        last = pe.matmul(PS[:, 0, 8 * b:8 * b + 8], t[:, k, b * P:(b + 1) * P].bitcast(F32), RT[:, k, :],
                                         start=(k == 0 and t is ahk), stop=(k == KD - 1 and t is alk))
            last.then_inc(s["logits_done"], 1)
            pe.wait_ge(s["mask_made"], 1)
            mk = [tab[:, 1, b, 0:NE] for b in range(LB)]
            ones = rs[:, 64:192]
            tri = K[:, C_TRI:C_TRI + P]
            pe.matmul(PS[:, 1, 0:8], tri, mk[0], start=True, stop=True)
            pe.matmul(PS[:, 1, 8:16], tri, mk[1], start=True, stop=False)
            pe.matmul(PS[:, 1, 8:16], ones, mk[0], start=False, stop=True)
            pe.matmul(PS[:, 1, 16:24], ones, mk[0], start=True, stop=False)
            pe.matmul(PS[:, 1, 16:24], ones, mk[1], start=False, stop=True).then_inc(s["pos_done"], 1)

            gsel = sc[:, 152:154]

            def turn(count, par):
                pe.wait_ge(s["h_made"], count)
                for j in range(4):
                    last = pe.transpose(PS[:, 4, j * P:(j + 1) * P], hh[:, par, j * P:(j + 1) * P], ident)
                last.then_inc(s["ht_done"], 1)

            def up(n, it, par, parts=(0, 1)):
                for gu in parts:
                    for kh in range(2):
                        u = n + 2 * gu + kh
                        unit_ready(pe, u, it)
                        wh, wl = halves(u, 4)
                        for k in range(4):
                            kk = 4 * kh + k
                            last = product(pe, PS[:, 2 * par + gu, :], xgh[:, kk, :], xgl[:, kk, :], wh[:, k, :], wl[:, k, :],
                                           kk == 0, kk == KD - 1)
                        last.then_inc(unit_used, 1)

            def down(n, it, count, par):
                pe.wait_ge(s["ht_ready"], count)
                for j in range(2):
                    unit_ready(pe, n + j, it)
                    wh, wl = halves(n + j, 2)
                    for k in range(2):
                        f = 2 * j + k
                        for hf in range(2):
                            o = PS[:, 6 + hf, :]
                            a_h, a_l = hth[:, par, f * P:(f + 1) * P], htl[:, par, f * P:(f + 1) * P]
                            mh, ml = wh[:, k, hf * 512:(hf + 1) * 512], wl[:, k, hf * 512:(hf + 1) * 512]
                            pe.matmul(o, a_h, mh, start=False, stop=True, skip_group_check=True)
                            pe.matmul(o, a_h, ml, start=False, stop=True, skip_group_check=True)
                            last = pe.matmul(o, a_l, mh, start=False, stop=True, skip_group_check=True)
                    last.then_inc(unit_used, 1)

            def gather(g):
                pe.wait_ge(s["sel_made"], g + 1)
                for hf in range(2):
                    for k in range(4 * hf, 4 * hf + 4):
                        for b in range(LB):
                            last = pe.matmul(PS[:, 2 + hf, (k % 4) * P:(k % 4 + 1) * P], xn[:, b, k * P:(k + 1) * P],
                                             SEL[:, b, :], start=(b == 0), stop=(b == LB - 1))
                    last.then_inc(s["gathered"], 1)

            def scatter(w):
                pe.wait_ge(s["y_gated"], w + 2)
                for b in range(LB):
                    for hf in range(2):
                        last = pe.matmul(PS[:, 2 + 2 * b + hf, :], SELT[:, b * P:(b + 1) * P], yg[:, hf * 512:(hf + 1) * 512],
                                         start=True, stop=True)
                last.then_inc(s["scattered"], 1)

            def visit(v, chained):
                pe.wait_ge(s["xg_ready"], v * 2 + (2 if chained else 4))
                up(U0, v * NCH, 0, (0,))
                if chained:
                    scatter(v - 1)
                for hf in range(2):
                    pe.matmul(PS[:, 6 + hf, :], zero16[:, 0:P], zero16[:, 0:512], start=True, stop=True)
                up(U0, v * NCH, 0, (1,))
                pe.wait_ge(s["acc_made"], v + 2)
                for b in range(LB):
                    pe.transpose(PS[:, 5, b * P:(b + 1) * P], SEL[:, b, :], ident)
                for b in range(LB):
                    last = pe.matmul(PS[:, 5, 256:257], SEL[:, b, :], gsel[:, b:b + 1], start=(b == 0), stop=(b == LB - 1))
                last.then_inc(s["selt_done"], 1)
                with pe.Fori(0, 3) as i:
                    for j in range(2):
                        it = v * NCH + i * 2
                        turn(it + j + 1, j)
                        up(UC + 6 * j, it, 1 - j)
                        down(UC + 6 * j + 4, it, it + j + 1, j)
                if chained:
                    gather(v + 1)
                turn(v * NCH + NCH, 0)
                down(UC + 36, v * NCH, v * NCH + NCH, 0)
                if not chained:
                    scatter(v)

            gather(0)
            with pe.Fori(0, NE) as e:
                visit(e, True)
            scatter(NE - 1)
            pe.wait_ge(s["route_ready"], 1)
            with pe.Fori(0, NE) as e:
                n = pe.value_load(cnt[0:1, bass.ds(e, 1)], min_val=0, max_val=SEQ)
                v = e + NV
                with pe.If(n > P):
                    gather(v + 1)
                    visit(v, False)
                with pe.Else():
                    pe.wait_ge(unit_used, N_MOE + v * VISIT)
                    pe.sem_inc(unit_used, VISIT)
                    for name, k, more in (("gathered", 2, 2), ("selt_done", 1, 0), ("ht_done", NCH, 0), ("scattered", 1, 1)):
                        pe.wait_ge(s[name], v * k + more)
                        pe.sem_inc(s[name], k)


_INS = ['x', 'c', 'ctx', 'c_ctx', 'ada_w', 'ada_b', 'g_pre_mix', 'g_post_mix', 'g_pre_ffn', 'g_post_ffn',
        'ab_w_in', 'a_norm_g', 'a_ws', 'a_bs', 'b_qnorm_g', 'b_knorm_g', 'ab_w_out', 'ffn_w_in', 'ffn_w_out',
        'mla_w_dq', 'mla_qnorm_g', 'mla_w_uq', 'mla_w_dkv', 'mla_kvnorm_g', 'mla_w_ukv', 'mla_w_o',
        'moe_router', 'moe_w_in', 'moe_w_out']


def kernel(**inputs):
    import concourse.bacc as _bacc
    from concourse.bass_utils import run_bass_kernel_spmd as _run

    nc = _bacc.Bacc("TRN2", target_bir_lowering=False, num_devices=1)
    arrays, args = {}, []
    for name in _INS + ["consts"]:
        a = np.ascontiguousarray(constants() if name == "consts" else inputs[name])
        arrays[f"in_{name}_dram"] = a
        args.append(nc.dram_tensor(f"in_{name}_dram", a.shape, mybir.dt.from_np(a.dtype), kind="ExternalInput").ap())
    args.append(nc.dram_tensor("out_0_dram", (1, SEQ, D), F32, kind="ExternalOutput").ap())
    trunk(nc, *args)
    r = _run(nc, [arrays], core_ids=[0])
    return r.results[0]["out_0_dram"]
```

```python
from contextlib import ExitStack

import numpy as np

import concourse.bass as bass
from concourse import mybir

ALU = mybir.AluOpType
ACT = mybir.ActivationFunctionType
AXX = mybir.AxisListType.X
F32 = mybir.dt.float32
F32R = mybir.dt.float32r
BF16 = mybir.dt.bfloat16
I32 = mybir.dt.int32
U32 = mybir.dt.uint32

P = 128
D = 1024
KD = D // P
SEQ = 256
CTX = 256
NTOK = SEQ + CTX
NB = NTOK // P
LB = SEQ // P
GRID_W = 64
EPS = 1e-6
HD = 128
CROPE = 64
CQ, CKV = 384, 256
D_FF = 2816
NE = 8
D_FFE = 3584

UNIT = 2048
RAW = 6
SPL = 3
FCH = 512
NCH = D_FFE // FCH
TOP = 2
NLATE = TOP * SEQ // (P + 1)
VISIT = NCH * 6

N_ABIN = [8, 18, 28, 30]
N_ADA = [0, 10, 20]
N_ABOUT = 32
N_FIN = 36
N_FOUT = 82
N_MLA = N_FOUT + 11
N_MOE = N_MLA + 13

C_ID, C_TRI, C_IOTA = 0, 128, 256
C_CB, C_SB = 512, 768
C_CC, C_SC = 1024, 1152
C_EPS, C_I8 = 1280, 1281
C_D8 = 1289
C_N = 1298



def constants():
    k = np.zeros((P, C_N), np.float32)
    k[:, C_ID:C_ID + P] = np.eye(P)
    k[:, C_TRI:C_TRI + P] = np.triu(np.ones((P, P)), 1)
    k[:, C_IOTA:C_IOTA + 256] = np.arange(256)
    tok = np.arange(SEQ)
    row, col = (tok // GRID_W).astype(np.float32), (tok % GRID_W).astype(np.float32)
    for width, c0, s0 in ((HD, C_CB, C_SB), (CROPE, C_CC, C_SC)):
        nf = width // 4
        inv = np.float32(10000.0) ** (-np.arange(nf, dtype=np.float32) / np.float32(nf))
        ang = np.stack([row[:, None] * inv, col[:, None] * inv], axis=1).astype(np.float32)
        ang = np.broadcast_to(ang[:, :, None, :], (SEQ, 2, 2, nf))
        sign = np.array([-1.0, 1.0], np.float32)[None, None, :, None]
        for b in range(LB):
            t = slice(b * P, b * P + P)
            k[:, c0 + b * width:c0 + (b + 1) * width] = np.cos(ang[t]).reshape(P, width)
            k[:, s0 + b * width:s0 + (b + 1) * width] = (np.sin(ang[t]) * sign).reshape(P, width)
    k[:, C_EPS] = EPS
    k[:, C_I8:C_I8 + NE] = np.arange(NE)
    k[:, C_D8:C_D8 + NE] = NE - np.arange(NE)
    return k


def trunk(nc, x, c, ctx, c_ctx, ada_w, ada_b, g_pre_mix, g_post_mix, g_pre_ffn, g_post_ffn,
          ab_w_in, a_norm_g, a_ws, a_bs, b_qnorm_g, b_knorm_g, ab_w_out, ffn_w_in, ffn_w_out,
          mla_w_dq, mla_qnorm_g, mla_w_uq, mla_w_dkv, mla_kvnorm_g, mla_w_ukv, mla_w_o,
          moe_router, moe_w_in, moe_w_out, consts, out):
    es = ExitStack()
    with es:
        def sb(name, shape, dt=F32):
            return es.enter_context(nc.sbuf_tensor(name, shape, dt))

        def sem(name):
            return es.enter_context(nc.semaphore(name))

        raw = [sb(f"raw{i}", [P, UNIT]) for i in range(RAW)]
        high = [sb(f"high{i}", [P, UNIT], F32R) for i in range(SPL)]
        low = [sb(f"low{i}", [P, UNIT], F32R) for i in range(SPL)]
        X = sb("X", [P, NB, D])
        ah = sb("ah", [P, KD * NTOK], F32R)
        al = sb("al", [P, KD * NTOK], F32R)
        tmp = sb("tmp", [P, 2 * 512])
        K = sb("K", [P, C_N])
        mixc = sb("mixc", [P, 1280])
        vec = sb("vec", [P, 192])
        modall = sb("modall", [P, 96, 2])
        gcol = sb("gcol", [P, 32])
        grow = sb("grow", [32, P])
        scol = sb("scol", [P, 2, 2, KD, 2])
        sc = sb("sc", [P, 160])
        sil = sb("sil", [P, 2, KD])
        act4 = sb("act4", [P, KD, 4], F32R)
        late = sb("late", [P, 2, NE], I32)
        work = sb("work", [P, 11 * 1024])
        PS = es.enter_context(nc.psum_tensor("PS", [P, 8, 512], F32))
        gg_dram = nc.dram_tensor("gg_scratch", [6, D], F32).ap()

        ident = K[:, C_ID:C_ID + P]
        xn = work[:, 0:LB * D].rearrange("p (b d) -> p b d", b=LB)
        raw_loaded = [sem(f"raw_loaded{i}") for i in range(RAW)]
        high_made = sem("high_made")
        low_made = [sem(f"low_made{i}") for i in range(SPL)]
        unit_used = sem("unit_used")

        def load_unit(sp, n, src, it=0):
            if n >= RAW:
                m = makers(n)
                sp.wait_ge(low_made[n % SPL], m * ((n - RAW) // SPL + 1) + it * (2 * m))
            dst = raw[n % RAW][:, 0:src.shape[1] * src.shape[2]].rearrange("p (a n) -> p a n", a=src.shape[1])
            sp.dma_start(dst, src).then_inc(raw_loaded[n % RAW], 16)

        def split_high(act, n, it=0, width=UNIT):
            act.wait_ge(raw_loaded[n % RAW], 16 * (n // RAW + 1) + it * 16)
            if n >= SPL:
                act.wait_ge(unit_used, n - SPL + 1 + it * 6)
            act.activation(high[n % SPL][:, 0:width], raw[n % RAW][:, 0:width], ACT.Copy).then_inc(high_made, 1)

        def makers(n):
            return 2 if n % SPL == SPL - 1 else 1

        def split_low(eng, n, it, c0, c1):
            eng.wait_ge(high_made, n + 1 + it * 6)
            eng.tensor_tensor(low[n % SPL][:, c0:c1], raw[n % RAW][:, c0:c1],
                              high[n % SPL][:, c0:c1].bitcast(F32), ALU.subtract).then_inc(low_made[n % SPL], 1)

        def vector_low(dve, n, it=0, width=UNIT):
            split_low(dve, n, it, 0 if makers(n) == 1 else width // 2, width)

        def pool_low(pool, n, it=0, width=UNIT):
            split_low(pool, n, it, 0, width // 2)

        def unit_ready(pe, n, it=0):
            m = makers(n)
            pe.wait_ge(low_made[n % SPL], m * (n // SPL + 1) + it * (2 * m))

        def halves(n, a, width=UNIT):
            return [t[n % SPL][:, 0:width].rearrange("p (a n) -> p a n", a=a) for t in (high, low)]

        def product(pe, o, sh, sl, mh, ml, start, stop):
            pe.matmul(o, sh, mh, start=start, stop=False)
            pe.matmul(o, sh, ml, start=False, stop=False)
            return pe.matmul(o, sl, mh, start=False, stop=stop)

        ahk = ah[:, :].rearrange("p (k t) -> p k t", k=KD)
        alk = al[:, :].rearrange("p (k t) -> p k t", k=KD)

        modv = modall[:, :, :].rearrange("p (l a k) s -> p l a k s", l=2, a=6)
        modc = modv.rearrange("p l (w t) k s -> p l w t k s", w=2)
        rows = [work[:, 8192:8704], mixc[:, 0:512]]
        U = work[:, 4096:6144].rearrange("p (b n) -> p b n", b=NB)
        V = work[:, 6144:8192].rearrange("p (b n) -> p b n", b=NB)
        Q = work[:, 0:2048].rearrange("p (b n) -> p b n", b=NB)
        KV = work[:, 2048:4096].rearrange("p (b n) -> p b n", b=NB)
        qT = work[:, 8192:10240].rearrange("p (h t) -> p h t", h=4)
        kT = work[:, 10240:11264].rearrange("p (h t) -> p h t", h=2)
        HID = work[:, 0:22 * 512].rearrange("p (f t) -> p f t", f=22)
        knT = work[:, 4096:8192].rearrange("p (h t) -> p h t", h=8)
        qnT = work[:, 8192:10240].rearrange("p (h t) -> p h t", h=8)
        krT = work[:, 10240:10752]
        V1 = work[:, 0:4096].rearrange("p (b n) -> p b n", b=NB)
        cqn = work[:, 0:768].rearrange("p (b n) -> p b n", b=2)
        ckvn = work[:, 768:1792].rearrange("p (b n) -> p b n", b=NB)
        kr2 = work[:, 1792:2304].rearrange("p (b n) -> p b n", b=NB)
        qrt = work[:, 2304:3328].rearrange("p (b n) -> p b n", b=2)
        rot = work[:, 4096:5120]
        GG = work[:, 4096:6144].rearrange("p (a n) -> p a n", a=2)
        ACC = work[:, 2048:4096].rearrange("p (b n) -> p b n", b=2)
        GGm = work[:, 4096:5120]
        sg = work[:, 5120:6144].rearrange("p (a n) -> p a n", a=2)
        hh = work[:, 6144:7168].rearrange("p (a n) -> p a n", a=2)
        yg = work[:, 7168:8192]
        SEL = work[:, 8192:8448].rearrange("p (b n) -> p b n", b=2)
        SELT = work[:, 8448:8704]
        RT = work[:, 8704:8768].rearrange("p (k n) -> p k n", k=KD)
        RTh, RTl = (t[:, 256:320].rearrange("p (k n) -> p k n", k=KD) for t in (ah, al))
        lT = work[0:NE, 5120:5376]
        rs = work[:, 8768:9024]
        tab = work[:, 9024:9024 + 6 * (NE + 1)].rearrange("p (t b e) -> p t b e", t=3, b=LB)
        zero16 = work[:, 9216:9472].bitcast(BF16)
        anb, qgb, kgb = mixc[:, 0:512], mixc[:, 512:640], mixc[:, 640:768]
        g_post = [vec[:, 57 + 16 * w:73 + 16 * w].rearrange("p (l k) -> p l k", l=2) for w in range(2)]
        wsT = mixc[:, 768:1280].rearrange("p (g i) -> p g i", g=4)
        XC = X[:, 2:4, :].rearrange("p b d -> p (b d)")
        sgf = tmp[:, :].rearrange("p (a n) -> p a n", a=2)
        fh = ah[:, 0:2048].rearrange("p (a t) -> p a t", a=4)
        fl = al[:, 0:2048].rearrange("p (a t) -> p a t", a=4)
        cqh, cql = (t[:, 0:768].rearrange("p (k t) -> p k t", k=3) for t in (ah, al))
        ckh, ckl = (t[:, 768:1792].rearrange("p (k t) -> p k t", k=2) for t in (ah, al))
        och, ocl = (t[:, 2048:4096].rearrange("p (k t) -> p k t", k=8) for t in (ah, al))
        xgh, xgl = (t[:, 0:1024].rearrange("p (k t) -> p k t", k=KD) for t in (ah, al))
        hth, htl = (t[:, 1024:2048].rearrange("p (a t) -> p a t", a=2) for t in (ah, al))

        s = {}
        for name in """consts_loaded pack_loaded x_loaded mixc_loaded gg_loaded gg_stored
                rt_loaded rt_high rt_ready lt_copied logits_turned out_stored
                pack_turned vec_ready silu_ready act_high act_ready rows_copied cols_turned cols_taken cols_ready
                gate_cols gate_turned gate_rows ws_turned ws_ready dve_step
                gelu_made q_copied kv_copied gn_ms gn_root vn_ready mix_done gated cat_turned
                cat_high cat_low qk_turned qk_ready qn_ready kn_ready
                g_done u_done silu_made hid_made fd_high fd_ready
                c_copied c_turned c_scaled c_high c_ready kr_ready kr_turned kr_copied
                qr_done qr_copied qr_ready qr_turned qr_moved qn_done qn_moved kv_done kv_moved
                logits_done route1 route_exp mask_made pos_done route_ready
                sel_made gathered selt_done xg_scaled xg_high xg_ready selt_copied
                esilu_made h_made ht_done ht_high ht_ready y_gated scattered acc_made
                resid_done resid_pool y_scaled y_done squared mean_made root_made""".split():
            s[name] = sem(name)

        PRE = [(NB, 0, 0), (NB, 0, 1), (NB, 1, 0), (LB, 1, 1)]
        pre = [{n: sem(f"pre{i}_{n}") for n in "diag turned scaled act_scaled high low pool_low".split()} for i in range(4)]
        RES = [(NB, 0), (NB, 2), (LB, 4), (LB, 5)]
        squares = [0]
        for i in range(4):
            squares += [squares[-1] + PRE[i][0], squares[-1] + PRE[i][0] + RES[i][0]]
        att = [{n: sem(f"att{i}_{n}") for n in "scored bias exp p turned pt o high low".split()} for i in range(2)]

        SS, MS, RSTD = 0, 4, 8

        junk = ah[:, 3072:4096]
        diag = work[:, 7168:7168 + NB * P]
        SCR = [tmp[:, 0:512], tmp[:, 512:1024], work[:, 6144:6656], work[:, 6656:7168]]
        RDONE = [0, 2, 4, 5]
        YDONE = [0, 3, 6]

        def x_ready(eng, i, b):
            eng.wait_ge(s["resid_done" if b % 2 else "resid_pool"], RDONE[i - 1] + b // 2 + 1)

        def act_warm(act, col):
            act.activation(sc[:, col:col + 1], K[:, C_EPS:C_EPS + 1], ACT.Sqrt)

        def pre_act(act, i):
            nb, layer, place = PRE[i]
            m = pre[i]
            if i == 0:
                act_warm(act, 155)
                act.wait_ge(s["x_loaded"], 32)
            for b in range(nb):
                if i:
                    x_ready(act, i, b)
                if b:
                    act.wait_ge(s["squared"], squares[2 * i] + b)
                act.activation(junk, X[:, b, :], ACT.Square, accum_out=sc[:, SS + b:SS + b + 1]).then_inc(s["squared"], 1)
            act.wait_ge(s["mean_made"], 2 * i + 1)
            act.activation(sc[:, MS:MS + nb], sc[:, MS:MS + nb], ACT.Sqrt).then_inc(s["root_made"], 1)

        def pre_act_chunks(act, i):
            nb, layer, place = PRE[i]
            m = pre[i]

            def upper(k):
                act.wait_ge(m["scaled"], k + 1)
                if nb > LB:
                    act.wait_ge(m["act_scaled"], k + 1)
                act.activation(ahk[:, k, 0:nb * P], SCR[k % 4][:, 0:nb * P], ACT.Copy).then_inc(m["high"], 1)

            act.wait_ge(s["cols_ready"], [1, 2, 3, 3][i])
            for k in range(KD):
                if nb > LB:
                    act.wait_ge(m["turned"], k + 1)
                    if k >= 4:
                        low_ready(act, i, k - 4)
                    act.activation(SCR[k % 4][:, SEQ:], PS[:, 6 + k % 2, 0:SEQ], ACT.Identity,
                                   bias=modc[:, layer, place, 0, k, 1:2], scale=scol[:, layer, place, k, 1:2]).then_inc(m["act_scaled"], 1)
                if k:
                    upper(k - 1)
            upper(KD - 1)

        def low_ready(eng, i, k):
            eng.wait_ge(pre[i]["pool_low" if k % 2 else "low"], k // 2 + 1)

        def pre_low(eng, i, k):
            nb = PRE[i][0]
            m = pre[i]
            eng.wait_ge(m["high"], k + 1)
            eng.tensor_tensor(alk[:, k, 0:nb * P], SCR[k % 4][:, 0:nb * P],
                              ahk[:, k, 0:nb * P].bitcast(F32), ALU.subtract).then_inc(m["pool_low" if k % 2 else "low"], 1)

        def pre_pool(pool, i):
            for k in range(1, KD, 2):
                pre_low(pool, i, k)

        def pre_dve(dve, i, link):
            nb, layer, place = PRE[i]
            m = pre[i]
            dve.wait_ge(s["squared"], squares[2 * i] + nb)
            dve.tensor_scalar(sc[:, MS:MS + nb], sc[:, SS:SS + nb], 1.0 / D, EPS, ALU.mult, ALU.add).then_inc(s["mean_made"], 1)
            dve.wait_ge(s["root_made"], 2 * i + 1)
            link(dve.reciprocal(sc[:, RSTD:RSTD + nb], sc[:, MS:MS + nb]))
            for b in range(nb):
                dve.tensor_scalar(diag[:, b * P:(b + 1) * P], ident, sc[:, RSTD + b:RSTD + b + 1], None,
                                  ALU.mult).then_inc(m["diag"], 1)

        def pre_dve_chunks(dve, i):
            nb, layer, place = PRE[i]
            m = pre[i]
            for k in range(KD):
                dve.wait_ge(m["turned"], k + 1)
                if k >= 4:
                    low_ready(dve, i, k - 4)
                dve.tensor_scalar(SCR[k % 4][:, 0:SEQ], PS[:, 4 + k % 2, 0:SEQ], scol[:, layer, place, k, 0:1],
                                  modc[:, layer, place, 0, k, 0:1], ALU.mult, ALU.add).then_inc(m["scaled"], 1)
                if k % 2:
                    pre_low(dve, i, k - 1)

        def pre_pe(pe, i):
            nb = PRE[i][0]
            m = pre[i]
            for b in range(nb if i else 0):
                x_ready(pe, i, b)
            pe.wait_ge(m["diag"], nb)
            for k in range(KD):
                if k >= 2:
                    pe.wait_ge(m["scaled"], k - 1)
                    if nb > LB:
                        pe.wait_ge(m["act_scaled"], k - 1)
                for b in range(nb):
                    last = pe.matmul(PS[:, 4 + 2 * (b // LB) + k % 2, (b % LB) * P:(b % LB + 1) * P], X[:, b, k * P:(k + 1) * P],
                                     diag[:, b * P:(b + 1) * P], start=True, stop=True)
                last.then_inc(m["turned"], 1)

        def res_act(act, i, y, done):
            nb = RES[i][0]
            act_warm(act, 156 + i)
            for b in range(nb):
                if i == 3 or b == nb - 1:
                    act.wait_ge(*done)
                else:
                    act.wait_ge(s["y_done"], YDONE[i] + b + 1)
                if b:
                    act.wait_ge(s["squared"], squares[2 * i + 1] + b)
                act.activation(tmp[:, :], y(b), ACT.Square, accum_out=sc[:, SS + b:SS + b + 1]).then_inc(s["squared"], 1)
            act.wait_ge(s["mean_made"], 2 * i + 1 + 1)
            act.activation(sc[:, MS:MS + nb], sc[:, MS:MS + nb], ACT.Sqrt).then_inc(s["root_made"], 1)

        YG = [tmp[:, :], work[:, 6144:7168], work[:, 0:1024]]

        def res_pool(pool, i):
            for b in range(0, RES[i][0], 2):
                pool.wait_ge(s["y_scaled"], RDONE[i] + b // 2 + 1)
                pool.tensor_tensor(X[:, b, :], X[:, b, :], YG[b], ALU.add).then_inc(s["resid_pool"], 1)

        def res_dve(dve, i, y, gate, link):
            nb = RES[i][0]
            dve.wait_ge(s["squared"], squares[2 * i + 1] + nb)
            dve.tensor_scalar(sc[:, MS:MS + nb], sc[:, SS:SS + nb], 1.0 / D, EPS, ALU.mult, ALU.add).then_inc(s["mean_made"], 1)
            dve.wait_ge(s["root_made"], 2 * i + 1 + 1)
            link(dve.reciprocal(sc[:, RSTD:RSTD + nb], sc[:, MS:MS + nb]))
            dve.wait_ge(s["gg_loaded"], 16 * (i + 1))
            for b in [b for b in (0, 2, 1, 3) if b < nb]:
                ins = dve.scalar_tensor_tensor(out=YG[1 if b % 2 else b], in0=y(b), scalar=sc[:, RSTD + b:RSTD + b + 1],
                                               in1=gate(b), op0=ALU.mult, op1=ALU.mult)
                if b % 2 == 0:
                    ins.then_inc(s["y_scaled"], 1)
                else:
                    link(ins)
                    dve.tensor_tensor(X[:, b, :], X[:, b, :], YG[1], ALU.add).then_inc(s["resid_done"], 1)
                    dve.wait_ge(s["resid_done"], RDONE[i] + b // 2 + 1)

        def ps_rows(b):
            return PS[:, 2 * b:2 * b + 2, :].rearrange("p a n -> p (a n)")

        PB = [work[:, 4096:5120], XC[:, 0:1024]]
        PT = [[work[:, 6144:7168], work[:, 7168:8192]], [tmp[:, :], mixc[:, 0:1024]]]
        qrT = XC[:, 1024:2048].rearrange("p (h t) -> p h t", h=4)
        ATT = [dict(n=16, scale=HD ** -0.5), dict(n=16, scale=(HD + CROPE) ** -0.5)]
        MX, NBI, SUM, REC = 16, 32, 48, 64

        BETWEEN = [9, 11, 13]

        def att_keys(a, i):
            return (0, NTOK) if a == 1 or i < 8 else (SEQ, CTX)

        def att_pe(pe, a):
            m = att[a]
            n = ATT[a]["n"]

            def scores(i):
                k0, nk = att_keys(a, i)
                if i >= 2:
                    pe.wait_ge(m["exp"], i - 1)
                o = PS[:, i % 2, 0:nk]
                if a == 0:
                    h, t0 = (i // 2) % 4, (SEQ if i >= 8 else 0) + (i % 2) * P
                    last = pe.matmul(o, qT[:, h, t0:t0 + P], kT[:, h // 2, k0:k0 + nk], start=True, stop=True)
                else:
                    h, t0, r = i // 2, (i % 2) * P, 64 * ((i // 2) % 2)
                    pe.matmul(o, qnT[:, h, t0:t0 + P], knT[:, h, :], start=True, stop=False)
                    last = pe.matmul(o, qrT[r:r + 64, h // 2, t0:t0 + P], krT[r:r + 64, :], start=False, stop=True)
                last.then_inc(m["scored"], 1)

            def turn(i):
                k0, nk = att_keys(a, i)
                pe.wait_ge(m["p"], i + 1)
                if i >= 2:
                    pe.wait_ge(m["pt"], i - 1)
                for k in range(nk // P):
                    last = pe.transpose(PS[:, 2 + i % 2, k * P:(k + 1) * P],
                                        PB[a][:, (i % 2) * 512 + k * P:(i % 2) * 512 + (k + 1) * P], ident)
                last.then_inc(m["turned"], 1)

            def values(h):
                k0, nk = att_keys(a, 2 * h)
                pe.wait_ge(m["pt"], 2 * h + 2)
                if h >= 2:
                    pe.wait_ge(m["low"], h - 1)
                pt = PT[a][h % 2].rearrange("p (k q) -> p k q", k=4)
                for k in range(nk // P):
                    kb = k0 // P + k
                    v = KV[:, kb, 256 + ((h % 4) // 2) * P:256 + ((h % 4) // 2 + 1) * P] if a == 0 else V1[:, kb, h * P:(h + 1) * P]
                    last = pe.matmul(PS[:, 4 + h % 2, 0:256], v, pt[:, k, :], start=(k == 0), stop=(k == nk // P - 1))
                last.then_inc(m["o"], 1)

            for i in range(n + 3):
                if i < n:
                    scores(i)
                if 2 <= i < n + 2:
                    turn(i - 2)
                if i >= 3 and (i - 3) % 2 == 1:
                    values((i - 3) // 2)

        def att_out(a, h, t):
            if a == 0:
                return t[0][:, 4 + h % 4, (h // 4) * SEQ:(h // 4 + 1) * SEQ]
            return t[1][:, h, :]

        def att_act(act, a, between=None):
            m = att[a]
            n = ATT[a]["n"]

            def exp(i):
                nk = att_keys(a, i)[1]
                act.wait_ge(m["bias"], i + 1)
                if i >= 2:
                    act.wait_ge(m["turned"], i - 1)
                act.activation(PB[a][:, (i % 2) * 512:(i % 2) * 512 + nk], PS[:, i % 2, 0:nk], ACT.Exp,
                               bias=sc[:, NBI + i:NBI + i + 1], scale=ATT[a]["scale"],
                               accum_out=sc[:, SUM + i:SUM + i + 1]).then_inc(m["exp"], 1)

            def copy(i):
                nk = att_keys(a, i)[1]
                h = i // 2
                act.wait_ge(m["turned"], i + 1)
                if h >= 2:
                    act.wait_ge(m["o"], h - 1)
                pt = PT[a][h % 2].rearrange("p (k q) -> p k q", k=4)
                act.activation(pt[:, 0:nk // P, (i % 2) * P:(i % 2 + 1) * P],
                               PS[:, 2 + i % 2, 0:nk].rearrange("p (k q) -> p k q", q=P), ACT.Copy).then_inc(m["pt"], 1)

            def upper(h):
                act.wait_ge(m["o"], h + 1)
                act.activation(att_out(a, h, (ahk, och)), PS[:, 4 + h % 2, 0:256], ACT.Copy).then_inc(m["high"], 1)

            for i in range(n + 3):
                if i < n:
                    exp(i)
                if 2 <= i < n + 2:
                    copy(i - 2)
                if i >= 3 and (i - 3) % 2 == 1:
                    upper((i - 3) // 2)
                if between and i in BETWEEN:
                    between(BETWEEN.index(i))

        def att_dve(dve, a, link, between=None):
            m = att[a]
            n = ATT[a]["n"]

            def peak(i):
                nk = att_keys(a, i)[1]
                dve.wait_ge(m["scored"], i + 1)
                link(dve.tensor_reduce(sc[:, MX + i:MX + i + 1], PS[:, i % 2, 0:nk], AXX, ALU.max))
                dve.tensor_scalar(sc[:, NBI + i:NBI + i + 1], sc[:, MX + i:MX + i + 1], -ATT[a]["scale"], None,
                                  ALU.mult).then_inc(m["bias"], 1)

            def norm(i):
                nk = att_keys(a, i)[1]
                dve.wait_ge(m["exp"], i + 1)
                link(dve.reciprocal(sc[:, REC + i:REC + i + 1], sc[:, SUM + i:SUM + i + 1]))
                p = PB[a][:, (i % 2) * 512:(i % 2) * 512 + nk]
                dve.tensor_scalar(p, p, sc[:, REC + i:REC + i + 1], None, ALU.mult).then_inc(m["p"], 1)

            def lower(h):
                dve.wait_ge(m["high"], h + 1)
                dve.tensor_tensor(att_out(a, h, (alk, ocl)), PS[:, 4 + h % 2, 0:256],
                                  att_out(a, h, (ahk, och)).bitcast(F32), ALU.subtract).then_inc(m["low"], 1)

            for i in range(n + 3):
                if i < n:
                    peak(i)
                if 1 <= i < n + 1:
                    norm(i - 1)
                if i >= 3 and (i - 3) % 2 == 1:
                    lower((i - 3) // 2)
                if between and i in BETWEEN:
                    between(BETWEEN.index(i))

        def ada_low(dve, g, it, n, buf, bank, first=False):
            for q in range(4):
                js = [(0, 1), (2, 3), (4, 5), ()][q]
                for j in js:
                    vector_low(dve, n + j + 3, it)
                dve.wait_ge(unit_used, n + 2 * q + 2 + it * 6)
                if q == 0 and not first:
                    dve.wait_ge(s["cols_turned"], g)
                dve.tensor_copy(rows[buf][32 * q:32 * q + 4, :], PS[0:4, bank + q, :]).then_inc(s["rows_copied"], 1)
            if not first:
                for j in (6, 7):
                    vector_low(dve, n + j + 3, it)

        def cols_take(dve, g, bank):
            dve.wait_ge(s["cols_turned"], g + 1)
            t = PS[:, bank, :].rearrange("p (k q r) -> p q k r", k=4, q=4)
            dst = modall[:, bass.ds(g * 16, 16), :].rearrange("p (q k) s -> p q k s", q=4)
            dve.tensor_copy(dst, t[:, :, :, 0:2]).then_inc(s["cols_taken"], 1)
            dve.wait_ge(s["cols_taken"], g * 2 + 1)
            dve.tensor_tensor(dst, dst, t[:, :, :, 2:4], ALU.add).then_inc(s["cols_taken"], 1)

        def rows_of(w):
            return w.rearrange("(k p) n -> p k n", p=P)

        abin, about = rows_of(ab_w_in[0]), rows_of(ab_w_out[0])
        fin, fout = rows_of(ffn_w_in[0]), rows_of(ffn_w_out[0])
        wdq, wdkv, wuq, wukv, wo = (rows_of(w[0]) for w in (mla_w_dq, mla_w_dkv, mla_w_uq, mla_w_ukv, mla_w_o))
        MLA_W = [4 * CQ] * 2 + [4 * (CKV + CROPE)] * 2 + [1536] * 3 + [2048] * 2 + [2048] * 4

        def mla_src(j):
            if j < 2:
                return wdq[:, 4 * j:4 * j + 4, :]
            if j < 4:
                return wdkv[:, 4 * (j - 2):4 * (j - 2) + 4, :]
            if j < 7:
                return wuq[:, j - 4:j - 3, :]
            if j < 9:
                return wukv[:, j - 7:j - 6, :]
            return wo[:, 2 * (j - 9):2 * (j - 9) + 2, :]

        NV = NE

        def late_expert(eng, j):
            return (eng.value_load(late[0:1, 0, bass.ds(j, 1)], min_val=0, max_val=NE),
                    eng.value_load(late[0:1, 1, bass.ds(j, 1)], min_val=0, max_val=NE - 1))


        U0 = N_MOE
        UC = N_MOE + 4

        block = es.enter_context(nc.Block())

        @block.sync
        def _(sp):
            sp.dma_start(K[:, :], consts).then_inc(s["consts_loaded"], 16)
            pk, pb = tmp[:, 0:P], tmp[:, P:2 * P]
            for r, n, src in ((0, 8, c[0].rearrange("(k p) -> k p", p=P)), (8, 8, c_ctx.rearrange("(k p) -> k p", p=P)),
                              (16, 16, g_pre_mix.rearrange("l (k p) -> (l k) p", p=P)),
                              (32, 16, g_pre_ffn.rearrange("l (k p) -> (l k) p", p=P)),
                              (48, 3, mla_qnorm_g[0].rearrange("(k p) -> k p", p=P)),
                              (51, 2, mla_kvnorm_g[0].rearrange("(k p) -> k p", p=P)), (53, 4, a_bs[0]),
                              (57, 16, g_post_mix.rearrange("l (k p) -> (l k) p", p=P)),
                              (73, 16, g_post_ffn.rearrange("l (k p) -> (l k) p", p=P))):
                sp.dma_start(pk[r:r + n, :], src).then_inc(s["pack_loaded"], 16)
            sp.dma_start(pb[0:96, :], ada_b.rearrange("l (k p) -> (l k) p", p=P)).then_inc(s["pack_loaded"], 16)

            def ada_group(layer, n, it, col):
                w = rows_of(ada_w[layer])
                for q in range(4):
                    for kh in range(2):
                        load_unit(sp, n + 2 * q + kh, w[:, 4 * kh:4 * kh + 4, bass.ds(col + q * 512, 512)], it)

            def abin_chunk(ch):
                for kh in range(2):
                    load_unit(sp, N_ABIN[ch] + kh, abin[:, 4 * kh:4 * kh + 4, ch * 512:(ch + 1) * 512])

            ada_group(0, N_ADA[0], 0, 0)
            abin_chunk(0)
            ada_group(0, N_ADA[1], 0, 2048)
            abin_chunk(1)
            ada_group(0, N_ADA[2], 0, 4096)
            abin_chunk(2)
            abin_chunk(3)
            for j in range(4):
                load_unit(sp, N_ABOUT + j, about[:, 2 * j:2 * j + 2, :])

            def fin_pair(n, it, col):
                load_unit(sp, n, fin[:, :, bass.ds(col, 256)], it)
                load_unit(sp, n + 1, fin[:, :, bass.ds(col + D_FF, 256)], it)

            for j in range(3):
                fin_pair(N_FIN + 2 * j, 0, j * 256)
            with sp.Fori(0, 3) as i:
                fin_pair(N_FIN + 6, i * 2, i * 512 + 3 * 256)
                ada_group(1, N_FIN + 8, i * 2, i * 2048)
                fin_pair(N_FIN + 16, i * 2, i * 512 + 4 * 256)
            for j in range(2):
                fin_pair(N_FIN + 42 + 2 * j, 0, (9 + j) * 256)
            for j in range(11):
                load_unit(sp, N_FOUT + j, fout[:, 2 * j:2 * j + 2, :])
            for j in range(13):
                load_unit(sp, N_MLA + j, mla_src(j))

            def visit(v, e):
                wi, wo_ = rows_of(moe_w_in[0, e]), rows_of(moe_w_out[0, e])

                def up(n, it, col):
                    for j in range(4):
                        load_unit(sp, n + j, wi[:, 4 * (j % 2):4 * (j % 2) + 4, bass.ds(col + (j // 2) * D_FFE, FCH)], it)

                def down(n, it, blk):
                    for j in range(2):
                        load_unit(sp, n + j, wo_[:, bass.ds(blk + 2 * j, 2), :], it)

                up(U0, v * NCH, 0)
                with sp.Fori(0, 3) as i:
                    for j in range(2):
                        up(UC + 6 * j, v * NCH + i * 2, i * 1024 + (j + 1) * FCH)
                        down(UC + 4 + 6 * j, v * NCH + i * 2, i * 8 + j * 4)
                down(UC + 36, v * NCH, 24)

            with sp.Fori(0, NE) as e:
                visit(e, e)
            sp.wait_ge(s["route_ready"], 1)
            with sp.Fori(0, NLATE) as j:
                some, e = late_expert(sp, j)
                with sp.If(some > 0):
                    visit(j + NV, e)
                with sp.Else():
                    for n in range(N_MOE, N_MOE + 6):
                        r = n % RAW
                        sp.wait_ge(raw_loaded[r], 16 * (n // RAW) + (j + NV) * (16 * NCH))
                        sp.sem_inc(raw_loaded[r], 16 * NCH)
            for b in range(LB):
                sp.wait_ge(s["resid_done" if b % 2 else "resid_pool"], 6)
                sp.dma_start(out[0, b * P:(b + 1) * P, :], X[:, b, :]).then_inc(s["out_stored"], 16)
            sp.wait_ge(s["out_stored"], 16 * LB)

        @block.gpsimd
        def _(pool):

            def unit(n):
                if n % SPL == SPL - 1:
                    pool_low(pool, n, 0, MLA_W[n - N_MLA] if N_MLA <= n < N_MOE else UNIT)

            for n in range(9):
                unit(n)
            pre_pool(pool, 0)
            for n in range(9, N_FIN + 2):
                unit(n)
            res_pool(pool, 0)
            pre_pool(pool, 1)
            unit(N_FIN + 2)
            for n in range(N_FIN + 3, N_FIN + 6):
                unit(n)
            with pool.Fori(0, 3) as i:
                for n in range(N_FIN + 6, N_FIN + 18):
                    if n % SPL == SPL - 1:
                        pool_low(pool, n, i * 2)
            for n in range(N_FIN + 42, N_MLA + 2):
                unit(n)
            res_pool(pool, 1)
            pre_pool(pool, 2)
            for n in range(N_MLA + 2, N_MOE):
                unit(n)
            res_pool(pool, 2)
            pre_pool(pool, 3)
            pool.memset(zero16, 0.0)
            pool.memset(SELT, 0.0)
            pool.memset(yg, 0.0).then_inc(s["y_gated"], 1)
            pool.memset(ACC, 0.0).then_inc(s["acc_made"], 1)
            first = next(n for n in range(N_MOE, N_MOE + 3) if n % SPL == SPL - 1)
            with pool.Fori(0, NE) as e:
                with pool.Fori(0, NCH) as i:
                    pool_low(pool, first, e * NCH + i)
                    pool_low(pool, first + 3, e * NCH + i)
            pool.wait_ge(s["route_ready"], 1)
            with pool.Fori(0, NLATE) as j:
                some, e = late_expert(pool, j)
                with pool.If(some > 0):
                    with pool.Fori(0, NCH) as i:
                        pool_low(pool, first, (j + NV) * NCH + i)
                        pool_low(pool, first + 3, (j + NV) * NCH + i)
                with pool.Else():
                    pool.wait_ge(low_made[SPL - 1], 2 * (first // SPL) + (j + NV) * (4 * NCH))
                    pool.sem_inc(low_made[SPL - 1], 2 * NCH)
            res_pool(pool, 3)

        @block.scalar
        def _(act):
            for b, src in enumerate((x[0], ctx[0])):
                act.dma_start(X[:, 2 * b:2 * b + 2, :], src.rearrange("(b p) d -> p b d", p=P)).then_inc(s["x_loaded"], 16)
            act.dma_start(anb, a_norm_g[0].partition_broadcast(P)).then_inc(s["mixc_loaded"], 16)
            act.dma_start(qgb, b_qnorm_g[0].partition_broadcast(P)).then_inc(s["mixc_loaded"], 16)
            act.dma_start(kgb, b_knorm_g[0].partition_broadcast(P)).then_inc(s["mixc_loaded"], 16)
            act.dma_start(work[:, 10240:10752].rearrange("p (g i) -> p g i", g=4),
                          a_ws[0].rearrange("g i j -> i g j")).then_inc(s["mixc_loaded"], 16)

            act.wait_ge(s["pack_turned"], 1)
            act.activation(sil[:, :, :].rearrange("p s k -> p (s k)"), PS[:, 7, 0:16], ACT.Silu).then_inc(s["silu_ready"], 1)
            act.wait_ge(s["silu_ready"], 1)
            act.activation(act4[:, :, 0:2], sil[:, :, :].rearrange("p s k -> p k s"), ACT.Copy).then_inc(s["act_high"], 1)
            pre_act(act, 0)
            for n in range(11):
                split_high(act, n)

            pre_act_chunks(act, 0)
            ahead = 11
            for ch in range(4):
                end = N_ABIN[ch] + 2
                for n in range(ahead, min(end + 3, N_ABOUT)):
                    split_high(act, n)
                ahead = max(ahead, min(end + 3, N_ABOUT))
                if ch >= 2:
                    act.wait_ge(s["gn_ms"], ch - 1)
                    act.activation(sc[:, 96:112], sc[:, 96:112], ACT.Sqrt).then_inc(s["gn_root"], 1)
                act.wait_ge(unit_used, end)
                for b in range(NB):
                    src = PS[:, (ch % 2) * 4 + b, :]
                    if ch < 2:
                        act.activation((U, V)[ch][:, b, :], src, ACT.Gelu_apprx_tanh).then_inc(s["gelu_made"], 1)
                    else:
                        act.activation((Q, KV)[ch - 2][:, b, :], src, ACT.Copy).then_inc(s[("q_copied", "kv_copied")[ch - 2]], 1)

            def gates_out(i, n, bank):
                act.wait_ge(s["gate_turned"], i + 1)
                act.activation(grow[0:8 * n, :], PS[0:8 * n, bank, 0:P], ACT.Copy).then_inc(s["gate_rows"], 1)
                act.wait_ge(s["gate_rows"], i + 1)
                act.dma_start(gg_dram[4 * i:4 * i + n].rearrange("g (k p) -> (g k) p", p=P), grow[0:8 * n, :]).then_inc(s["gg_stored"], 16)

            def qk_move(h):
                act.wait_ge(s["qk_turned"], h + 1)
                act.activation(qT[:, h, :] if h < 4 else kT[:, h - 4, :], PS[:, 6 + h % 2, :], ACT.Copy).then_inc(s["qk_ready"], 1)

            for h in range(4):
                qk_move(h)
            gates_out(0, 4, 0)
            act.wait_ge(s["gn_ms"], 3)
            act.activation(sc[:, 96:104], sc[:, 96:104], ACT.Sqrt).then_inc(s["gn_root"], 1)
            for g in range(4):
                act.wait_ge(s["cat_turned"], g + 1)
                act.activation(ahk[:, g, :], PS[:, 2 + g, :], ACT.Copy).then_inc(s["cat_high"], 1)
            for h in range(4, 6):
                qk_move(h)
            att_act(act, 0, lambda j: split_high(act, N_ABOUT + j))
            act.wait_ge(att[0]["o"], 8)
            act.wait_ge(s["gg_stored"], 16)
            act.dma_start(GG, gg_dram[0:2].partition_broadcast(P)).then_inc(s["gg_loaded"], 16)
            split_high(act, N_ABOUT + 3)
            for n in range(N_FIN, N_FIN + 2):
                split_high(act, n)
            res_act(act, 0, ps_rows, (unit_used, N_ABOUT + 4))
            split_high(act, N_FIN + 2)

            pre_act(act, 1)
            pre_act_chunks(act, 1)

            def ffn_silu(f0, n, it, i):
                if f0 % 2 == 0:
                    act.wait_ge(s["g_done"], f0 // 2 + 1 + i * 2)
                else:
                    act.wait_ge(unit_used, n + it * 6)
                if f0 >= 2:
                    act.wait_ge(s["hid_made"], f0 - 1 + i * 4)
                act.activation(sgf[:, f0 % 2, :], PS[:, 2 * (f0 % 2), :], ACT.Silu).then_inc(s["silu_made"], 1)

            def ffn_pair(f0, n, it, i):
                for j in range(2):
                    ffn_silu(f0 + j, n + j, it, i)
                    split_high(act, n + j + 3, it)

            for j in range(3):
                ffn_pair(2 * j, N_FIN + 2 * j, 0, 0)
            with act.Fori(0, 3) as i:
                ffn_pair(6, N_FIN + 6, i * 2, i)
                for j in range(8):
                    split_high(act, N_FIN + 8 + j + 3, i * 2)
                ffn_pair(8, N_FIN + 16, i * 2, i)
            ffn_pair(18, N_FIN + 42, 0, 0)
            ffn_silu(20, N_FIN + 44, 0, 0)
            split_high(act, N_FOUT + 1)
            ffn_silu(21, N_FIN + 45, 0, 0)
            act.wait_ge(unit_used, N_FOUT)
            def hidden_high(f):
                act.wait_ge(s["hid_made"], f + 1)
                act.activation(fh[:, f % 4, :], HID[:, f, :], ACT.Copy).then_inc(s["fd_high"], 1)

            for f in range(4):
                hidden_high(f)
            split_high(act, N_FOUT + 2)
            for d in range(10):
                act.wait_ge(unit_used, N_FOUT + d + 1)
                for f in range(2 * d + 4, min(2 * d + 6, 22)):
                    hidden_high(f)
                n = N_FOUT + d + 3
                split_high(act, n, 0, UNIT if n < N_MLA else MLA_W[n - N_MLA])
            act.wait_ge(s["fd_ready"], 22)
            act.dma_start(GG, gg_dram[2:4].partition_broadcast(P)).then_inc(s["gg_loaded"], 16)
            res_act(act, 1, ps_rows, (unit_used, N_FOUT + 11))
            split_high(act, N_MLA + 2, 0, MLA_W[2])

            pre_act(act, 2)
            pre_act_chunks(act, 2)
            gates_out(1, 2, 3)
            split_high(act, N_MLA + 3, 0, MLA_W[3])
            act.wait_ge(unit_used, N_MLA + 2)
            for b in range(2):
                act.activation(cqn[:, b, :], PS[:, b, 0:CQ], ACT.Copy).then_inc(s["c_copied"], 1)
            for j in (4, 5):
                split_high(act, N_MLA + j, 0, MLA_W[j])
            act.wait_ge(unit_used, N_MLA + 4)
            for b in range(NB):
                act.activation(ckvn[:, b, :], PS[:, 2 + b, 0:CKV], ACT.Copy).then_inc(s["c_copied"], 1)
                act.activation(kr2[:, b, 0:CROPE], PS[:, 2 + b, CKV:CKV + CROPE], ACT.Copy).then_inc(s["c_copied"], 1)
            act.wait_ge(s["gn_ms"], 4)
            act.activation(sc[:, 96:102], sc[:, 96:102], ACT.Sqrt).then_inc(s["gn_root"], 1)
            split_high(act, N_MLA + 6, 0, MLA_W[6])
            for k in range(5):
                act.wait_ge(s["c_scaled"], k + 1)
                dst = cqh[:, k, :] if k < 3 else ckh[:, k - 3, :]
                act.activation(dst, tmp[:, (k % 2) * 512:(k % 2) * 512 + (256 if k < 3 else 512)], ACT.Copy).then_inc(s["c_high"], 1)
            for b in range(2):
                act.wait_ge(s["qr_done"], b + 1)
                act.activation(qrt[:, b, :], PS[:, b, :], ACT.Copy).then_inc(s["qr_copied"], 1)
            for h in range(8):
                act.wait_ge(*((s["qn_done"], h + 1) if h < 7 else (unit_used, N_MLA + 7)))
                act.activation(qnT[:, h, :], PS[:, 2 + h % 4, 0:256], ACT.Copy).then_inc(s["qn_moved"], 1)
            act.wait_ge(s["kr_turned"], 1)
            act.activation(krT, PS[:, 7, :], ACT.Copy).then_inc(s["kr_copied"], 1)
            for n in range(N_MLA + 7, N_MLA + 9):
                split_high(act, n, 0, MLA_W[n - N_MLA])
            for p in range(4):
                act.wait_ge(s["qr_turned"], p + 1)
                act.activation(qrT[:, p, :], PS[:, 6 + p % 2, 0:256], ACT.Copy).then_inc(s["qr_moved"], 1)
            for j in range(16):
                act.wait_ge(*((s["kv_done"], j + 1) if j < 15 else (unit_used, N_MLA + 9)))
                dst = knT[:, j, :] if j < 8 else V1[:, (j - 8) // 2, ((j - 8) % 2) * 512:((j - 8) % 2 + 1) * 512]
                act.activation(dst, PS[:, j % 6, :], ACT.Copy).then_inc(s["kv_moved"], 1)
            att_act(act, 1, lambda j: split_high(act, N_MLA + 9 + j))
            act.wait_ge(att[1]["o"], 8)
            act.wait_ge(s["gg_stored"], 32)
            act.dma_start(GGm, gg_dram[4].partition_broadcast(P)).then_inc(s["gg_loaded"], 16)
            act.dma_start(RT, moe_router[0].rearrange("(k p) e -> p k e", p=P)).then_inc(s["rt_loaded"], 16)
            split_high(act, N_MLA + 12)
            act.wait_ge(s["rt_loaded"], 16)
            act.activation(RTh, RT, ACT.Copy).then_inc(s["rt_high"], 1)
            res_act(act, 2, ps_rows, (unit_used, N_MLA + 13))

            pre_act(act, 3)
            pre_act_chunks(act, 3)
            act.wait_ge(s["resid_done"], 5)
            act.dma_start(GGm, gg_dram[5].partition_broadcast(P)).then_inc(s["gg_loaded"], 16)
            act.wait_ge(s["route1"], 1)
            act.activation(rs[:, 32:34], rs[:, 32:34], ACT.Exp).then_inc(s["route_exp"], 1)

            def tokens(g, hf):
                act.wait_ge(s["xg_scaled"], g * 2 + hf + 1)
                act.activation(xgh[:, 4 * hf:4 * hf + 4, :].rearrange("p k t -> p (k t)"),
                               tmp[:, hf * 512:(hf + 1) * 512], ACT.Copy).then_inc(s["xg_high"], 1)

            def visit(v, chained):
                split_high(act, U0 + 3, v * NCH)
                silu(U0 + 2, v * NCH, 0)

                def body(n, it, par):
                    for j in range(3):
                        split_high(act, n + j, it)
                    turned(it + (n - UC) // 6 + 1, 1 - par)
                    for j in range(3, 5):
                        split_high(act, n + j, it)
                    silu(n + 2, it, par)
                    split_high(act, n + 5, it)

                with act.Fori(0, 3) as i:
                    body(UC, v * NCH + i * 2, 1)
                    body(UC + 6, v * NCH + i * 2, 0)
                split_high(act, UC + 36, v * NCH)
                split_high(act, UC + 37, v * NCH)
                if chained:
                    with act.If(v < NE - 1):
                        split_high(act, U0, v * NCH + NCH)
                turned(v * NCH + NCH, 0)
                if chained:
                    for hf in range(2):
                        tokens(v + 1, hf)

            def silu(n, it, par):
                act.wait_ge(unit_used, n + it * 6)
                act.activation(sg[:, par, :], PS[:, 2 * par, :], ACT.Silu).then_inc(s["esilu_made"], 1)

            def turned(count, par):
                act.wait_ge(s["ht_done"], count)
                act.activation(hth[:, par, :], PS[:, 4, :], ACT.Copy).then_inc(s["ht_high"], 1)

            for j in range(3):
                split_high(act, U0 + j)
            for hf in range(2):
                tokens(0, hf)
            with act.Fori(0, NE) as e:
                visit(e, True)
                with act.If(e < NE - 1):
                    for j in range(1, 3):
                        split_high(act, U0 + j, e * NCH + NCH)
            act.wait_ge(s["route_ready"], 1)
            with act.Fori(0, NLATE) as j:
                some, e = late_expert(act, j)
                v = j + NV
                with act.If(some > 0):
                    for n in range(U0, U0 + 3):
                        split_high(act, n, v * NCH)
                    for hf in range(2):
                        tokens(v + 1, hf)
                    visit(v, False)
                with act.Else():
                    act.wait_ge(high_made, N_MOE + v * VISIT)
                    act.sem_inc(high_made, VISIT)
                    for name, k, more in (("xg_high", 2, 2), ("esilu_made", NCH, 0), ("ht_high", NCH, 0)):
                        act.wait_ge(s[name], v * k + more)
                        act.sem_inc(s[name], k)
            res_act(act, 3, lambda b: ACC[:, b, :], (s["acc_made"], NE + NLATE + 2))

        @block.vector
        def _(dve):
            class Link:
                n = 0

                def __call__(self, ins):
                    ins.then_inc(s["dve_step"], 1)
                    self.n += 1
                    dve.wait_ge(s["dve_step"], self.n)

            link = Link()

            dve.wait_ge(s["pack_turned"], 1)
            dve.wait_ge(s["silu_ready"], 1)
            dve.tensor_copy(vec[:, 0:89], PS[:, 7, 0:89])
            dve.tensor_copy(vec[:, 96:192], PS[:, 7, 96:192]).then_inc(s["vec_ready"], 1)
            dve.wait_ge(s["act_high"], 1)
            dve.tensor_tensor(act4[:, :, 2:4], sil[:, :, :].rearrange("p s k -> p k s"),
                              act4[:, :, 0:2].bitcast(F32), ALU.subtract).then_inc(s["act_ready"], 1)

            def mod_ready(l, a0, a1):
                v = modv[:, l, a0:a1].rearrange("p a k s -> p (a k) s")
                bias = vec[:, 96 + 48 * l + 8 * a0:96 + 48 * l + 8 * a1].unsqueeze(2).broadcast_to([P, 8 * (a1 - a0), 2])
                link(dve.tensor_tensor(v, v, bias, ALU.add))

            def gain_scale(l, w):
                g = vec[:, 16 + 16 * w + 8 * l:24 + 16 * w + 8 * l].unsqueeze(2).broadcast_to([P, KD, 2])
                return dve.scalar_tensor_tensor(out=scol[:, l, w, :, :], in0=modc[:, l, w, 1, :, :], scalar=1.0,
                                                in1=g, op0=ALU.add, op1=ALU.mult)

            def gates(l, streams):
                for w in range(2):
                    for st in range(streams):
                        o = 8 * (w * streams + st)
                        last = dve.tensor_tensor(gcol[:, o:o + 8], modc[:, l, w, 2, :, st], g_post[w][:, l, :], ALU.mult)
                last.then_inc(s["gate_cols"], 1)

            link(dve.memset(rows[0], 0.0))
            pre_dve(dve, 0, link)
            for n in range(3):
                vector_low(dve, n)
            ada_low(dve, 0, 0, N_ADA[0], 0, 4, first=True)
            dve.wait_ge(s["ws_turned"], 1)
            dve.tensor_copy(wsT, PS[:, 3, :].rearrange("p (g i) -> p g i", g=4)).then_inc(s["ws_ready"], 1)
            cols_take(dve, 0, 7)
            dve.wait_ge(s["cols_taken"], 2)
            mod_ready(0, 0, 2)
            gain_scale(0, 0).then_inc(s["cols_ready"], 1)

            dve.wait_ge(s["cols_ready"], 1)
            pre_dve_chunks(dve, 0)
            for n in (9, 10):
                vector_low(dve, n)

            def rope(t, heads, width, cc, ss, scr):
                f = width // 4
                v = t.rearrange("p (h a s f) -> p h a s f", a=2, s=2, f=f)
                w = scr.rearrange("p (h a s f) -> p h a s f", a=2, s=2, f=f)
                sv = ss.rearrange("p (a s f) -> p a s f", a=2, s=2)
                for a_ in range(2):
                    for s_ in range(2):
                        sin = sv[:, a_, s_, :].unsqueeze(1).broadcast_to([P, heads, f])
                        last = dve.tensor_tensor(w[:, :, a_, s_, :], v[:, :, a_, 1 - s_, :], sin, ALU.mult)
                link(last)
                th = t.rearrange("p (h w) -> p h w", h=heads)
                link(dve.tensor_tensor(th, th, cc.unsqueeze(1).broadcast_to([P, heads, width]), ALU.mult))
                return dve.tensor_tensor(t, t, scr, ALU.add)

            def mean_squares(v, groups):
                for h0 in range(0, groups, 8):
                    sq = tmp[:, :].rearrange("p (g d) -> p g d", g=8)
                    link(dve.tensor_tensor(sq, v[:, h0:h0 + 8, :], v[:, h0:h0 + 8, :], ALU.mult))
                    link(dve.tensor_reduce(sc[:, 96 + h0:104 + h0], sq, AXX, ALU.add))
                dve.tensor_scalar(sc[:, 96:96 + groups], sc[:, 96:96 + groups], 1.0 / P, EPS, ALU.mult, ALU.add).then_inc(s["gn_ms"], 1)

            for n in range(11, 13):
                vector_low(dve, n)
            ada_low(dve, 1, 0, N_ADA[1], 0, 4)
            cols_take(dve, 1, 7)
            for n in range(21, 23):
                vector_low(dve, n)
            ada_low(dve, 2, 0, N_ADA[2], 0, 0)
            cols_take(dve, 2, 3)
            dve.wait_ge(s["cols_taken"], 6)
            mod_ready(0, 2, 6)
            gates(0, 2)
            gain_scale(0, 1).then_inc(s["cols_ready"], 1)
            dve.wait_ge(s["gelu_made"], 8)
            dve.wait_ge(s["mixc_loaded"], 64)
            vg = V.rearrange("p b (g d) -> p (b g) d", d=P)
            mean_squares(vg, 16)
            vector_low(dve, 31)
            dve.wait_ge(s["gn_root"], 1)
            link(dve.reciprocal(sc[:, 112:128], sc[:, 96:112]))
            link(dve.tensor_tensor(vg, vg, sc[:, 112:128].unsqueeze(2).broadcast_to([P, 16, P]), ALU.mult))
            dve.tensor_tensor(V, V, anb.unsqueeze(1).broadcast_to([P, NB, 512]), ALU.mult).then_inc(s["vn_ready"], 1)
            dve.wait_ge(s["q_copied"], NB)
            qg = Q.rearrange("p b (g d) -> p (b g) d", d=P)
            mean_squares(qg, 16)
            dve.wait_ge(s["gn_root"], 2)
            link(dve.reciprocal(sc[:, 112:128], sc[:, 96:112]))
            link(dve.tensor_tensor(qg, qg, sc[:, 112:128].unsqueeze(2).broadcast_to([P, 16, P]), ALU.mult))
            link(dve.tensor_tensor(qg, qg, qgb.unsqueeze(1).broadcast_to([P, 16, P]), ALU.mult))
            for b in range(LB):
                last = rope(Q[:, b, :], 4, HD, K[:, C_CB + b * HD:C_CB + (b + 1) * HD],
                            K[:, C_SB + b * HD:C_SB + (b + 1) * HD], tmp[:, 0:512])
                if b < LB - 1:
                    link(last)
            last.then_inc(s["qn_ready"], 1)
            for b in range(NB):
                dve.wait_ge(s["mix_done"], b + 1)
                for g in range(4):
                    last = dve.scalar_tensor_tensor(out=U[:, b, g * P:(g + 1) * P], in0=PS[:, b % 2, g * P:(g + 1) * P],
                                                    scalar=vec[:, 53 + g:54 + g], in1=U[:, b, g * P:(g + 1) * P],
                                                    op0=ALU.add, op1=ALU.mult)
                last.then_inc(s["gated"], 1)
            def cat_lower():
                for g in range(4):
                    dve.wait_ge(s["cat_high"], g + 1)
                    dve.tensor_tensor(alk[:, g, :], PS[:, 2 + g, :], ahk[:, g, :].bitcast(F32), ALU.subtract).then_inc(s["cat_low"], 1)

            dve.wait_ge(s["kv_copied"], NB)
            dve.wait_ge(s["qn_ready"], 1)
            kv4 = KV.rearrange("p b (g d) -> p b g d", d=P)[:, :, 0:2, :]
            sq = tmp[:, :].rearrange("p (b g d) -> p b g d", b=NB, g=2)
            kss = sc[:, 96:104].rearrange("p (b g) -> p b g", b=NB)
            link(dve.tensor_tensor(sq, kv4, kv4, ALU.mult))
            link(dve.tensor_reduce(kss, sq, AXX, ALU.add))
            dve.tensor_scalar(sc[:, 96:104], sc[:, 96:104], 1.0 / P, EPS, ALU.mult, ALU.add).then_inc(s["gn_ms"], 1)
            dve.wait_ge(s["gn_root"], 3)
            link(dve.reciprocal(sc[:, 112:120], sc[:, 96:104]))
            for b in range(NB):
                kb = kv4[:, b, :, :]
                link(dve.tensor_tensor(kb, kb, sc[:, 112 + 2 * b:114 + 2 * b].unsqueeze(2).broadcast_to([P, 2, P]), ALU.mult))
                last = dve.tensor_tensor(kb, kb, kgb.unsqueeze(1).broadcast_to([P, 2, P]), ALU.mult)
                if b < LB:
                    link(last)
                    last = rope(KV[:, b, 0:256], 2, HD, K[:, C_CB + b * HD:C_CB + (b + 1) * HD],
                                K[:, C_SB + b * HD:C_SB + (b + 1) * HD], tmp[:, 0:256])
                if b < NB - 1:
                    link(last)
            last.then_inc(s["kn_ready"], 1)
            cat_lower()
            att_dve(dve, 0, link, lambda j: vector_low(dve, N_ABOUT + j))
            vector_low(dve, N_ABOUT + 3)
            for n in range(N_FIN, N_FIN + 2):
                vector_low(dve, n)
            res_dve(dve, 0, ps_rows, lambda b: GG[:, b // LB, :], link)

            pre_dve(dve, 1, link)
            pre_dve_chunks(dve, 1)
            vector_low(dve, N_FIN + 2)

            def ffn_hidden(f0, f, n, it, i):
                dve.wait_ge(s["silu_made"], f0 + 1 + i * 4)
                if f0 % 2 == 0:
                    dve.wait_ge(s["u_done"], f0 // 2 + 1 + i * 2)
                else:
                    dve.wait_ge(unit_used, n + 1 + it * 6)
                dve.tensor_tensor(HID[:, bass.ds(f, 1), :].rearrange("p a t -> p (a t)"), sgf[:, f0 % 2, :],
                                  PS[:, 2 * (f0 % 2) + 1, :], ALU.mult).then_inc(s["hid_made"], 1)

            def ffn_pair(f0, f, n, it, i):
                for j in range(2):
                    ffn_hidden(f0 + j, f + j, n + j, it, i)
                    vector_low(dve, n + j + 3, it)

            for j in range(3):
                ffn_pair(2 * j, 2 * j, N_FIN + 2 * j, 0, 0)
            with dve.Fori(0, 3) as i:
                ffn_pair(6, i * 4 + 6, N_FIN + 6, i * 2, i)
                ada_low(dve, i + 3, i * 2, N_FIN + 8, 1, 4)
                ffn_pair(8, i * 4 + 8, N_FIN + 16, i * 2, i)
                cols_take(dve, i + 3, 7)
            ffn_pair(18, 18, N_FIN + 42, 0, 0)
            ffn_hidden(20, 20, N_FIN + 44, 0, 0)
            vector_low(dve, N_FOUT + 1)
            ffn_hidden(21, 21, N_FIN + 45, 0, 0)
            def hidden_low(f):
                dve.wait_ge(s["fd_high"], f + 1)
                dve.tensor_tensor(fl[:, f % 4, :], HID[:, f, :], fh[:, f % 4, :].bitcast(F32), ALU.subtract).then_inc(s["fd_ready"], 1)

            for f in range(4):
                hidden_low(f)
            vector_low(dve, N_FOUT + 2)
            dve.wait_ge(s["cols_taken"], 12)
            mod_ready(1, 0, 6)
            dve.wait_ge(s["gate_rows"], 1)
            gates(1, 1)
            link(gain_scale(1, 0))
            gain_scale(1, 1).then_inc(s["cols_ready"], 1)
            for d in range(10):
                for f in range(2 * d + 4, min(2 * d + 6, 22)):
                    hidden_low(f)
                n = N_FOUT + d + 3
                vector_low(dve, n, 0, UNIT if n < N_MLA else MLA_W[n - N_MLA])
            res_dve(dve, 1, ps_rows, lambda b: GG[:, b // LB, :], link)

            pre_dve(dve, 2, link)
            pre_dve_chunks(dve, 2)
            for j in (2, 3):
                vector_low(dve, N_MLA + j, 0, MLA_W[j])
            dve.wait_ge(s["c_copied"], 2)
            link(dve.tensor_tensor(tmp[:, 0:768].rearrange("p (b n) -> p b n", b=2), cqn, cqn, ALU.mult))
            link(dve.tensor_reduce(sc[:, 96:98], tmp[:, 0:768].rearrange("p (b n) -> p b n", b=2), AXX, ALU.add))
            link(dve.tensor_scalar(sc[:, 96:98], sc[:, 96:98], 1.0 / CQ, EPS, ALU.mult, ALU.add))
            for j in (4, 5):
                vector_low(dve, N_MLA + j, 0, MLA_W[j])
            dve.wait_ge(s["c_copied"], 10)
            link(dve.tensor_tensor(tmp[:, :].rearrange("p (b n) -> p b n", b=NB), ckvn, ckvn, ALU.mult))
            link(dve.tensor_reduce(sc[:, 98:102], tmp[:, :].rearrange("p (b n) -> p b n", b=NB), AXX, ALU.add))
            dve.tensor_scalar(sc[:, 98:102], sc[:, 98:102], 1.0 / CKV, EPS, ALU.mult, ALU.add).then_inc(s["gn_ms"], 1)
            dve.wait_ge(s["gn_root"], 4)
            link(dve.reciprocal(sc[:, 112:118], sc[:, 96:102]))
            for b in range(2):
                dve.tensor_scalar(cqn[:, b, :], cqn[:, b, :], sc[:, 112 + b:113 + b], None, ALU.mult)
            for b in range(NB):
                last = dve.tensor_scalar(ckvn[:, b, :], ckvn[:, b, :], sc[:, 114 + b:115 + b], None, ALU.mult)
            last.then_inc(s["c_copied"], 1)
            vector_low(dve, N_MLA + 6, 0, MLA_W[6])

            def c_lower(k):
                w = 256 if k < 3 else 512
                d, u = (cql[:, k, :], cqh[:, k, :]) if k < 3 else (ckl[:, k - 3, :], ckh[:, k - 3, :])
                dve.wait_ge(s["c_high"], k + 1)
                dve.tensor_tensor(d, tmp[:, (k % 2) * 512:(k % 2) * 512 + w], u.bitcast(F32), ALU.subtract).then_inc(s["c_ready"], 1)

            for k in range(5):
                w = 256 if k < 3 else 512
                dve.wait_ge(s["c_turned"], k + 1)
                if k >= 2:
                    dve.wait_ge(s["c_ready"], k - 1)
                dve.tensor_scalar(tmp[:, (k % 2) * 512:(k % 2) * 512 + w], PS[:, 6 + k % 2, 0:w], vec[:, 48 + k:49 + k], None,
                                  ALU.mult).then_inc(s["c_scaled"], 1)
                if k:
                    c_lower(k - 1)
            c_lower(4)
            for b in range(LB):
                link(rope(kr2[:, b, 0:CROPE], 1, CROPE, K[:, C_CC + b * CROPE:C_CC + (b + 1) * CROPE],
                          K[:, C_SC + b * CROPE:C_SC + (b + 1) * CROPE], rot[:, 0:CROPE]))
            dve.tensor_copy(kr2[:, :, CROPE:2 * CROPE], kr2[:, :, 0:CROPE]).then_inc(s["kr_ready"], 1)
            for b in range(LB):
                dve.wait_ge(s["qr_copied"], b + 1)
                last = rope(qrt[:, b, :], 8, CROPE, K[:, C_CC + b * CROPE:C_CC + (b + 1) * CROPE],
                            K[:, C_SC + b * CROPE:C_SC + (b + 1) * CROPE], rot[:, b * 512:(b + 1) * 512])
                last.then_inc(s["qr_ready"], 1)
            for n in range(N_MLA + 7, N_MLA + 9):
                vector_low(dve, n)
            att_dve(dve, 1, link, lambda j: vector_low(dve, N_MLA + 9 + j))
            vector_low(dve, N_MLA + 12)
            link(dve.memset(rs[:, 64:192], 1.0))
            link(dve.memset(tab, 0.0))
            dve.wait_ge(s["rt_high"], 1)
            dve.tensor_tensor(RTl, RT, RTh.bitcast(F32), ALU.subtract).then_inc(s["rt_ready"], 1)
            res_dve(dve, 2, ps_rows, lambda b: GGm, link)

            pre_dve(dve, 3, link)
            pre_dve_chunks(dve, 3)
            LOG, BEST, IDX, OH, SUMS, LATE = 0, 16, 192, 208, 34, 36
            dve.wait_ge(s["logits_done"], 1)
            dve.tensor_copy(lT, PS[0:NE, 0, 0:SEQ]).then_inc(s["lt_copied"], 1)
            dve.wait_ge(s["logits_turned"], 1)
            link(dve.tensor_copy(rs[:, LOG:LOG + 16], PS[:, 1, 0:16]))
            for b in range(LB):
                last = dve.max(rs[:, BEST + 8 * b:BEST + 8 * b + 8], rs[:, LOG + 8 * b:LOG + 8 * b + 8])
            link(last)
            best = rs[:, BEST:BEST + 16].rearrange("p (b e) -> p b e", b=LB)
            dve.tensor_tensor(rs[:, 32:34], best[:, :, 1], best[:, :, 0], ALU.subtract).then_inc(s["route1"], 1)
            for b in range(LB):
                last = dve.max_index(rs[:, IDX + 8 * b:IDX + 8 * b + 8].bitcast(U32), rs[:, BEST + 8 * b:BEST + 8 * b + 8],
                                     rs[:, LOG + 8 * b:LOG + 8 * b + 8])
            link(last)
            link(dve.tensor_copy(sc[:, 128:144], rs[:, IDX:IDX + 16].bitcast(U32)))
            idxf = sc[:, 128:144].rearrange("p (b e) -> p b e", b=LB)
            i8 = K[:, C_I8:C_I8 + NE].unsqueeze(1).broadcast_to([P, LB, NE])
            first, second = (rs[:, OH + 16 * t:OH + 16 * t + 16].rearrange("p (b e) -> p b e", b=LB) for t in range(2))
            for t, oh in enumerate((first, second)):
                last = dve.tensor_tensor(oh, i8, idxf[:, :, t:t + 1].broadcast_to([P, LB, NE]), ALU.is_equal)
            link(last)
            dve.tensor_tensor(tab[:, 1, :, 0:NE], first, second, ALU.add).then_inc(s["mask_made"], 1)
            for b in range(LB):
                dve.tensor_scalar(xn[:, b, :], X[:, b, :], sc[:, RSTD + b:RSTD + b + 1], None, ALU.mult)
            dve.wait_ge(s["route_exp"], 1)
            link(dve.tensor_scalar(rs[:, SUMS:SUMS + 2], rs[:, 32:34], 1.0, None, ALU.add))
            link(dve.reciprocal(sc[:, 146:148], rs[:, SUMS:SUMS + 2]))
            link(dve.tensor_tensor(sc[:, 148:150], sc[:, 146:148], rs[:, 32:34], ALU.mult))
            for t, oh in enumerate((first, second)):
                last = dve.tensor_tensor(oh, oh, sc[:, 146 + 2 * t:148 + 2 * t].unsqueeze(2).broadcast_to([P, LB, NE]), ALU.mult)
            link(last)
            link(dve.tensor_tensor(tab[:, 2, :, 0:NE], first, second, ALU.add))
            gsel = sc[:, 152:154]
            gslot = sc[:, 154:155]
            dve.wait_ge(s["pos_done"], 1)
            link(dve.tensor_copy(tab[:, 0, :, 0:NE], PS[:, 2, 0:16].rearrange("p (b e) -> p b e", b=LB)))
            key = rs[:, LATE:LATE + NE]
            link(dve.scalar_tensor_tensor(out=key, in0=PS[:, 2, 16:24], scalar=float(P), in1=K[:, C_D8:C_D8 + NE],
                                          op0=ALU.is_gt, op1=ALU.mult))
            top = rs[:, LATE + NE:LATE + 2 * NE]
            link(dve.max(top, key))
            link(dve.tensor_copy(late[:, 0, :], top))
            link(dve.tensor_scalar(key, top, -1.0, float(NE), ALU.mult, ALU.add))
            dve.tensor_scalar(late[:, 1, :], key, float(NE - 1), None, ALU.min).then_inc(s["route_ready"], 1)

            def low_units(n, it, js):
                for j in js:
                    vector_low(dve, n + j, it)

            def hidden(count, n, it, par):
                dve.wait_ge(s["esilu_made"], count)
                dve.wait_ge(unit_used, n + it * 6)
                dve.tensor_tensor(hh[:, par, :], sg[:, par, :], PS[:, 2 * par + 1, :], ALU.mult).then_inc(s["h_made"], 1)

            def turned(count, par):
                dve.wait_ge(s["ht_high"], count)
                dve.tensor_tensor(htl[:, par, :], PS[:, 4, :], hth[:, par, :].bitcast(F32), ALU.subtract).then_inc(s["ht_ready"], 1)

            def select(g, e, base):
                for b in range(LB):
                    dve.tensor_scalar(SEL[:, b, :], K[:, C_IOTA + base:C_IOTA + base + P],
                                      tab[:, 0, b, bass.ds(e, 1)], tab[:, 1, b, bass.ds(e, 1)], ALU.is_equal, ALU.mult)
                    last = dve.tensor_copy(gsel[:, b:b + 1], tab[:, 2, b, bass.ds(e, 1)])
                last.then_inc(s["sel_made"], 1)

            def scaled(g, hf):
                dve.wait_ge(s["gathered"], g * 2 + hf + 1)
                for k in range(4 * hf, 4 * hf + 4):
                    last = dve.tensor_scalar(tmp[:, k * P:(k + 1) * P], PS[:, 2 + hf, (k % 4) * P:(k % 4 + 1) * P],
                                             scol[:, 1, 1, k, 0:1], modc[:, 1, 1, 0, k, 0:1], ALU.mult, ALU.add)
                last.then_inc(s["xg_scaled"], 1)

            def tokens(g, hf):
                dve.wait_ge(s["xg_high"], g * 2 + hf + 1)
                dve.tensor_tensor(xgl[:, 4 * hf:4 * hf + 4, :].rearrange("p k t -> p (k t)"), tmp[:, hf * 512:(hf + 1) * 512],
                                  xgh[:, 4 * hf:4 * hf + 4, :].rearrange("p k t -> p (k t)").bitcast(F32),
                                  ALU.subtract).then_inc(s["xg_ready"], 1)

            def accumulate(w):
                dve.wait_ge(s["scattered"], w + 2)
                dve.wait_ge(s["acc_made"], w + 2)
                dve.tensor_tensor(ACC.rearrange("p b n -> p (b n)"), ACC.rearrange("p b n -> p (b n)"),
                                  PS[:, 2:6, :].rearrange("p a n -> p (a n)"), ALU.add).then_inc(s["acc_made"], 1)

            def visit(v, e, chained):
                low_units(U0, v * NCH, (3,))
                if chained:
                    accumulate(v - 1)
                hidden(v * NCH + 1, U0 + 4, v * NCH, 0)
                dve.wait_ge(s["selt_done"], v + 1)
                dve.tensor_copy(SELT, PS[:, 5, 0:256])
                dve.tensor_copy(gslot, PS[:, 5, 256:257]).then_inc(s["selt_copied"], 1)
                if chained:
                    select(v + 1, e + 1, 0)

                def body(n, it, par):
                    count = it + (n - UC) // 6 + 1
                    low_units(n, it, (0, 1, 2))
                    turned(count, 1 - par)
                    low_units(n, it, (3, 4, 5))
                    hidden(count + 1, n + 4, it, par)

                with dve.Fori(0, 3) as i:
                    body(UC, v * NCH + i * 2, 1)
                    body(UC + 6, v * NCH + i * 2, 0)
                low_units(UC + 36, v * NCH, (0, 1))
                if chained:
                    scaled(v + 1, 0)
                turned(v * NCH + NCH, 0)
                if chained:
                    scaled(v + 1, 1)
                    for hf in range(2):
                        tokens(v + 1, hf)
                    with dve.If(e < NE - 1):
                        low_units(U0, v * NCH + NCH, (0,))
                dve.wait_ge(unit_used, N_MOE + VISIT + v * VISIT)
                dve.wait_ge(s["selt_copied"], v + 1)
                dve.tensor_scalar(yg, PS[:, 6:8, :].rearrange("p a n -> p (a n)"), gslot, None, ALU.mult).then_inc(s["y_gated"], 1)
                if chained:
                    with dve.If(e < NE - 1):
                        low_units(U0, v * NCH + NCH, (1, 2))
                else:
                    accumulate(v)

            def gather_first(g, e, base, it):
                select(g, e, base)
                low_units(U0, it, (0,))
                for hf in range(2):
                    scaled(g, hf)
                for hf in range(2):
                    tokens(g, hf)
                low_units(U0, it, (1, 2))

            gather_first(0, 0, 0, 0)
            with dve.Fori(0, NE) as e:
                visit(e, e, True)
            accumulate(NE - 1)
            dve.wait_ge(s["route_ready"], 1)
            with dve.Fori(0, NLATE) as j:
                some, e = late_expert(dve, j)
                v = j + NV
                with dve.If(some > 0):
                    gather_first(v + 1, e, P, v * NCH)
                    visit(v, e, False)
                with dve.Else():
                    for sl in range(SPL):
                        m = makers(sl)
                        before = m * len([n for n in range(N_MOE) if n % SPL == sl])
                        dve.wait_ge(low_made[sl], before + v * (2 * NCH * m))
                        dve.sem_inc(low_made[sl], 2 * NCH)
                    for name, k, more in (("sel_made", 1, 1), ("xg_scaled", 2, 2), ("xg_ready", 2, 2), ("selt_copied", 1, 0),
                                          ("h_made", NCH, 0), ("ht_ready", NCH, 0), ("y_gated", 1, 1), ("acc_made", 1, 2)):
                        dve.wait_ge(s[name], v * k + more)
                        dve.sem_inc(s[name], k)
            dve.wait_ge(s["acc_made"], NE + NLATE + 2)
            res_dve(dve, 3, lambda b: ACC[:, b, :], lambda b: GGm, link)

        @block.tensor
        def _(pe):
            pe.wait_ge(s["consts_loaded"], 16)
            pe.wait_ge(s["pack_loaded"], 16 * 10)
            pe.transpose(PS[:, 7, 0:89], tmp[0:89, 0:P], K[0:89, C_ID:C_ID + 89])
            pe.transpose(PS[:, 7, 96:192], tmp[0:96, P:2 * P], K[0:96, C_ID:C_ID + 96]).then_inc(s["pack_turned"], 1)
            pe.wait_ge(s["act_ready"], 1)

            def ada(n, it, g, bank, first=False):
                for q in range(4):
                    if not first:
                        pe.wait_ge(s["rows_copied"], (g - 1) * 4 + (q + 1))
                        if q == 3:
                            pe.wait_ge(s["cols_taken"], g * 2)
                    for kh in range(2):
                        u = n + 2 * q + kh
                        unit_ready(pe, u, it)
                        wh, wl = halves(u, 4)
                        for k in range(4):
                            a = act4[:, 4 * kh + k, :]
                            pe.matmul(PS[0:4, bank + q, :], a, wh[:, k, :], start=(kh == 0 and k == 0), stop=False)
                            last = pe.matmul(PS[0:4, bank + q, :], a, wl[:, k, :], start=False, stop=(kh == 1 and k == 3))
                        last.then_inc(unit_used, 1)

            def ada_turn(g, buf, bank):
                pe.wait_ge(s["rows_copied"], g * 4 + 4)
                for k in range(4):
                    last = pe.transpose(PS[:, bank, k * P:(k + 1) * P], rows[buf][:, k * P:(k + 1) * P], ident)
                last.then_inc(s["cols_turned"], 1)

            pe.wait_ge(s["vec_ready"], 1)
            ada(N_ADA[0], 0, 0, 4, first=True)
            pe.wait_ge(s["mixc_loaded"], 64)
            for g in range(4):
                last = pe.transpose(PS[:, 3, g * P:(g + 1) * P], work[:, 10240 + g * P:10240 + (g + 1) * P], ident)
            last.then_inc(s["ws_turned"], 1)
            ada_turn(0, 0, 7)

            pe.wait_ge(s["ws_ready"], 1)
            pe.wait_ge(s["cols_taken"], 2)
            pre_pe(pe, 0)
            for ch in range(4):
                if ch in (1, 2):
                    bank = 4 * (ch % 2)
                    if ch == 2:
                        pe.wait_ge(s["gelu_made"], NB)
                    ada(N_ADA[ch], 0, ch, bank)
                    ada_turn(ch, 0, bank + 3)
                for kh in range(2):
                    u = N_ABIN[ch] + kh
                    unit_ready(pe, u)
                    wh, wl = halves(u, 4)
                    for b in range(NB):
                        if kh == 0 and ch >= 2:
                            pe.wait_ge(s["gelu_made"], (ch - 2) * NB + b + 1)
                        if kh == 0 and ch in (1, 2) and b == 3:
                            pe.wait_ge(s["cols_taken"], 2 * (ch + 1))
                        for k in range(4):
                            kk = 4 * kh + k
                            if ch == 0 and b == 0:
                                low_ready(pe, 0, kk)
                            last = product(pe, PS[:, (ch % 2) * 4 + b, :], ahk[:, kk, b * P:(b + 1) * P],
                                           alk[:, kk, b * P:(b + 1) * P], wh[:, k, :], wl[:, k, :],
                                           kk == 0, kk == KD - 1)
                    last.then_inc(unit_used, 1)
            pe.wait_ge(s["vn_ready"], 1)
            pe.wait_ge(s["q_copied"], NB)
            for b in range(NB):
                if b >= 2:
                    pe.wait_ge(s["gated"], b - 1)
                for g in range(4):
                    last = pe.matmul(PS[:, b % 2, g * P:(g + 1) * P], wsT[:, g, :], V[:, b, g * P:(g + 1) * P],
                                     start=True, stop=True)
                last.then_inc(s["mix_done"], 1)
            def qk_turn(h):
                if h >= 2:
                    pe.wait_ge(s["qk_ready"], h - 1)
                for b in range(NB):
                    t = Q[:, b, h * P:(h + 1) * P] if h < 4 else KV[:, b, (h - 4) * P:(h - 3) * P]
                    last = pe.transpose(PS[:, 6 + h % 2, b * P:(b + 1) * P], t, ident)
                last.then_inc(s["qk_turned"], 1)

            pe.wait_ge(s["qn_ready"], 1)
            pe.wait_ge(s["kv_copied"], NB)
            for h in range(4):
                qk_turn(h)
            pe.wait_ge(s["gated"], NB)
            pe.wait_ge(s["gate_cols"], 1)
            pe.transpose(PS[0:32, 0, 0:P], gcol[:, 0:32], ident).then_inc(s["gate_turned"], 1)
            for g in range(4):
                for b in range(NB):
                    last = pe.transpose(PS[:, 2 + g, b * P:(b + 1) * P], U[:, b, g * P:(g + 1) * P], ident)
                last.then_inc(s["cat_turned"], 1)
            pe.wait_ge(s["kn_ready"], 1)
            for h in range(4, 6):
                qk_turn(h)
            pe.wait_ge(s["qk_ready"], 6)
            att_pe(pe, 0)
            pe.wait_ge(att[0]["low"], 8)
            pe.wait_ge(s["cat_low"], 4)
            for j in range(4):
                u = N_ABOUT + j
                unit_ready(pe, u)
                wh, wl = halves(u, 2)
                for b in range(NB):
                    for k in range(2):
                        kk = 2 * j + k
                        for hf in range(2):
                            last = product(pe, PS[:, 2 * b + hf, :], ahk[:, kk, b * P:(b + 1) * P], alk[:, kk, b * P:(b + 1) * P],
                                           wh[:, k, hf * 512:(hf + 1) * 512], wl[:, k, hf * 512:(hf + 1) * 512],
                                           kk == 0, kk == KD - 1)
                    if j == 3 and b < NB - 1:
                        last.then_inc(s["y_done"], 1)
                last.then_inc(unit_used, 1)

            pre_pe(pe, 1)

            def ffn_pair(f0, n, it, i):
                for j in range(2):
                    f = f0 + j
                    for gu in range(2):
                        if j == 0:
                            unit_ready(pe, n + gu, it)
                        if gu == 0 and f >= 2:
                            pe.wait_ge(s["hid_made"], f - 1 + i * 4)
                        wh, wl = (t[:, :, j * P:(j + 1) * P] for t in halves(n + gu, KD))
                        for k in range(KD):
                            if f == gu == 0:
                                low_ready(pe, 1, k)
                            last = product(pe, PS[:, 2 * (f % 2) + gu, :], wh[:, k, :], wl[:, k, :], ahk[:, k, :], alk[:, k, :],
                                           k == 0, k == KD - 1)
                        last.then_inc(s[("g_done", "u_done")[gu]] if j == 0 else unit_used, 1)

            for j in range(3):
                ffn_pair(2 * j, N_FIN + 2 * j, 0, 0)
            with pe.Fori(0, 3) as i:
                ffn_pair(6, N_FIN + 6, i * 2, i)
                ada(N_FIN + 8, i * 2, i + 3, 4)
                ffn_pair(8, N_FIN + 16, i * 2, i)
                ada_turn(i + 3, 1, 7)
            for j in range(2):
                ffn_pair(18 + 2 * j, N_FIN + 42 + 2 * j, 0, 0)
            pe.wait_ge(s["cols_taken"], 12)
            pe.wait_ge(s["hid_made"], 22)
            for d in range(11):
                u = N_FOUT + d
                unit_ready(pe, u)
                wh, wl = halves(u, 2)
                for k in range(2):
                    f = 2 * d + k
                    pe.wait_ge(s["fd_ready"], f + 1)
                    for b in range(NB):
                        for hf in range(2):
                            last = product(pe, PS[:, 2 * b + hf, :], fh[:, f % 4, b * P:(b + 1) * P], fl[:, f % 4, b * P:(b + 1) * P],
                                           wh[:, k, hf * 512:(hf + 1) * 512], wl[:, k, hf * 512:(hf + 1) * 512],
                                           f == 0, f == 21)
                        if f == 21 and b < NB - 1:
                            last.then_inc(s["y_done"], 1)
                last.then_inc(unit_used, 1)

            pre_pe(pe, 2)
            pe.wait_ge(s["gate_cols"], 2)
            pe.transpose(PS[0:16, 3, 0:P], gcol[:, 0:16], ident).then_inc(s["gate_turned"], 1)
            for j in range(4):
                if j == 2:
                    pe.wait_ge(s["gate_rows"], 2)
                u = N_MLA + j
                unit_ready(pe, u)
                wh, wl = halves(u, 4, MLA_W[j])
                w = CQ if j < 2 else CKV + CROPE
                for b in range(LB if j < 2 else NB):
                    for k in range(4):
                        kk = 4 * (j % 2) + k
                        if j < 2 and b == 0:
                            low_ready(pe, 2, kk)
                        last = product(pe, PS[:, b if j < 2 else 2 + b, 0:w], ahk[:, kk, b * P:(b + 1) * P],
                                       alk[:, kk, b * P:(b + 1) * P], wh[:, k, :], wl[:, k, :], kk == 0, kk == KD - 1)
                last.then_inc(unit_used, 1)
            pe.wait_ge(s["c_copied"], 11)
            for k in range(5):
                if k >= 2:
                    pe.wait_ge(s["c_scaled"], k - 1)
                for b in range(LB if k < 3 else NB):
                    t = cqn[:, b, k * P:(k + 1) * P] if k < 3 else ckvn[:, b, (k - 3) * P:(k - 2) * P]
                    last = pe.transpose(PS[:, 6 + k % 2, b * P:(b + 1) * P], t, ident)
                last.then_inc(s["c_turned"], 1)
            for j in range(3):
                unit_ready(pe, N_MLA + 4 + j)
            pe.wait_ge(s["c_ready"], 3)
            uq = [[t.rearrange("p a (h d) -> p (a h) d", h=8) for t in halves(N_MLA + 4 + k, 1, 1536)] for k in range(3)]
            for b in range(LB):
                for k in range(3):
                    wh, wl = (t[:, :, HD:HD + CROPE] for t in uq[k])
                    last = product(pe, PS[:, b, :], cqh[:, k, b * P:(b + 1) * P], cql[:, k, b * P:(b + 1) * P], wh, wl, k == 0, k == 2)
                last.then_inc(s["qr_done"], 1)
            for h in range(8):
                if h >= 4:
                    pe.wait_ge(s["qn_moved"], h - 3)
                for k in range(3):
                    wh, wl = (t[:, h, 0:HD] for t in uq[k])
                    last = product(pe, PS[:, 2 + h % 4, 0:256], wh, wl, cqh[:, k, :], cql[:, k, :], k == 0, k == 2)
                if h < 7:
                    last.then_inc(s["qn_done"], 1)
            last.then_inc(unit_used, 3)
            pe.wait_ge(s["c_scaled"], 5)
            pe.wait_ge(s["kr_ready"], 1)
            for b in range(NB):
                last = pe.transpose(PS[:, 7, b * P:(b + 1) * P], kr2[:, b, :], ident)
            last.then_inc(s["kr_turned"], 1)
            pe.wait_ge(s["kr_copied"], 1)
            pe.wait_ge(s["qr_ready"], LB)
            for p in range(4):
                if p >= 2:
                    pe.wait_ge(s["qr_moved"], p - 1)
                for b in range(LB):
                    last = pe.transpose(PS[:, 6 + p % 2, b * P:(b + 1) * P], qrt[:, b, p * P:(p + 1) * P], ident)
                last.then_inc(s["qr_turned"], 1)
            for j in range(2):
                unit_ready(pe, N_MLA + 7 + j)
            pe.wait_ge(s["c_ready"], 5)
            pe.wait_ge(s["qn_moved"], 8)
            ukv = [[t.rearrange("p a (h d) -> p (a h) d", h=8) for t in halves(N_MLA + 7 + k, 1)] for k in range(2)]
            for j in range(16):
                if j >= 6:
                    pe.wait_ge(s["kv_moved"], j - 5)
                for k in range(2):
                    if j < 8:
                        wh, wl = (t[:, j, 0:HD] for t in ukv[k])
                        last = product(pe, PS[:, j % 6, :], wh, wl, ckh[:, k, :], ckl[:, k, :], k == 0, k == 1)
                    else:
                        b, hf = (j - 8) // 2, (j - 8) % 2
                        wh, wl = (t[:, 4 * hf:4 * hf + 4, HD:2 * HD] for t in ukv[k])
                        last = product(pe, PS[:, j % 6, :], ckh[:, k, b * P:(b + 1) * P], ckl[:, k, b * P:(b + 1) * P], wh, wl, k == 0, k == 1)
                if j < 15:
                    last.then_inc(s["kv_done"], 1)
            last.then_inc(unit_used, 2)
            pe.wait_ge(s["kv_moved"], 16)
            pe.wait_ge(s["qr_moved"], 4)
            att_pe(pe, 1)
            pe.wait_ge(att[1]["low"], 8)
            for j in range(4):
                u = N_MLA + 9 + j
                unit_ready(pe, u)
                wh, wl = halves(u, 2)
                for b in range(LB):
                    for k in range(2):
                        kk = 2 * j + k
                        for hf in range(2):
                            last = product(pe, PS[:, 2 * b + hf, :], och[:, kk, b * P:(b + 1) * P], ocl[:, kk, b * P:(b + 1) * P],
                                           wh[:, k, hf * 512:(hf + 1) * 512], wl[:, k, hf * 512:(hf + 1) * 512],
                                           kk == 0, kk == KD - 1)
                    if j == 3 and b < LB - 1:
                        last.then_inc(s["y_done"], 1)
                last.then_inc(unit_used, 1)

            pre_pe(pe, 3)
            pe.wait_ge(s["rt_ready"], 1)
            for k in range(KD):
                low_ready(pe, 3, k)
                last = product(pe, PS[0:NE, 0, 0:SEQ], RTh[:, k, :], RTl[:, k, :], ahk[:, k, 0:SEQ], alk[:, k, 0:SEQ], k == 0, k == KD - 1)
            last.then_inc(s["logits_done"], 1)
            pe.wait_ge(s["lt_copied"], 1)
            for b in range(LB):
                last = pe.transpose(PS[:, 1, NE * b:NE * (b + 1)], lT[:, b * P:(b + 1) * P], K[0:NE, C_ID:C_ID + NE])
            last.then_inc(s["logits_turned"], 1)
            pe.wait_ge(s["mask_made"], 1)
            mk = [tab[:, 1, b, 0:NE] for b in range(LB)]
            ones = rs[:, 64:192]
            tri = K[:, C_TRI:C_TRI + P]
            pe.matmul(PS[:, 2, 0:8], tri, mk[0], start=True, stop=True)
            pe.matmul(PS[:, 2, 8:16], tri, mk[1], start=True, stop=False)
            pe.matmul(PS[:, 2, 8:16], ones, mk[0], start=False, stop=True)
            pe.matmul(PS[:, 2, 16:24], ones, mk[0], start=True, stop=False)
            pe.matmul(PS[:, 2, 16:24], ones, mk[1], start=False, stop=True).then_inc(s["pos_done"], 1)

            gsel = sc[:, 152:154]

            def turn(count, par):
                pe.wait_ge(s["h_made"], count)
                for j in range(4):
                    last = pe.transpose(PS[:, 4, j * P:(j + 1) * P], hh[:, par, j * P:(j + 1) * P], ident)
                last.then_inc(s["ht_done"], 1)

            def up(n, it, par, parts=(0, 1)):
                for gu in parts:
                    for kh in range(2):
                        u = n + 2 * gu + kh
                        unit_ready(pe, u, it)
                        wh, wl = halves(u, 4)
                        for k in range(4):
                            kk = 4 * kh + k
                            last = product(pe, PS[:, 2 * par + gu, :], xgh[:, kk, :], xgl[:, kk, :], wh[:, k, :], wl[:, k, :],
                                           kk == 0, kk == KD - 1)
                        last.then_inc(unit_used, 1)

            def down(n, it, count, par):
                pe.wait_ge(s["ht_ready"], count)
                for j in range(2):
                    unit_ready(pe, n + j, it)
                    wh, wl = halves(n + j, 2)
                    for k in range(2):
                        f = 2 * j + k
                        for hf in range(2):
                            o = PS[:, 6 + hf, :]
                            a_h, a_l = hth[:, par, f * P:(f + 1) * P], htl[:, par, f * P:(f + 1) * P]
                            mh, ml = wh[:, k, hf * 512:(hf + 1) * 512], wl[:, k, hf * 512:(hf + 1) * 512]
                            pe.matmul(o, a_h, mh, start=False, stop=True, skip_group_check=True)
                            pe.matmul(o, a_h, ml, start=False, stop=True, skip_group_check=True)
                            last = pe.matmul(o, a_l, mh, start=False, stop=True, skip_group_check=True)
                    last.then_inc(unit_used, 1)

            def gather(g, halves=(0, 1)):
                if 0 in halves:
                    pe.wait_ge(s["sel_made"], g + 1)
                for hf in halves:
                    for k in range(4 * hf, 4 * hf + 4):
                        for b in range(LB):
                            last = pe.matmul(PS[:, 2 + hf, (k % 4) * P:(k % 4 + 1) * P], xn[:, b, k * P:(k + 1) * P],
                                             SEL[:, b, :], start=(b == 0), stop=(b == LB - 1))
                    last.then_inc(s["gathered"], 1)

            def scatter(w):
                pe.wait_ge(s["y_gated"], w + 2)
                for b in range(LB):
                    for hf in range(2):
                        last = pe.matmul(PS[:, 2 + 2 * b + hf, :], SELT[:, b * P:(b + 1) * P], yg[:, hf * 512:(hf + 1) * 512],
                                         start=True, stop=True)
                last.then_inc(s["scattered"], 1)

            def visit(v, chained):
                pe.wait_ge(s["xg_ready"], v * 2 + (2 if chained else 4))
                up(U0, v * NCH, 0, (0,))
                if chained:
                    scatter(v - 1)
                for hf in range(2):
                    pe.matmul(PS[:, 6 + hf, :], zero16[:, 0:P], zero16[:, 0:512], start=True, stop=True)
                up(U0, v * NCH, 0, (1,))
                pe.wait_ge(s["acc_made"], v + 2)
                for b in range(LB):
                    pe.transpose(PS[:, 5, b * P:(b + 1) * P], SEL[:, b, :], ident)
                for b in range(LB):
                    last = pe.matmul(PS[:, 5, 256:257], SEL[:, b, :], gsel[:, b:b + 1], start=(b == 0), stop=(b == LB - 1))
                last.then_inc(s["selt_done"], 1)
                with pe.Fori(0, 3) as i:
                    for j in range(2):
                        it = v * NCH + i * 2
                        turn(it + j + 1, j)
                        up(UC + 6 * j, it, 1 - j)
                        down(UC + 6 * j + 4, it, it + j + 1, j)
                if chained:
                    gather(v + 1, (0,))
                turn(v * NCH + NCH, 0)
                if chained:
                    gather(v + 1, (1,))
                down(UC + 36, v * NCH, v * NCH + NCH, 0)
                if not chained:
                    scatter(v)

            gather(0)
            with pe.Fori(0, NE) as e:
                visit(e, True)
            scatter(NE - 1)
            pe.wait_ge(s["route_ready"], 1)
            with pe.Fori(0, NLATE) as j:
                some, e = late_expert(pe, j)
                v = j + NV
                with pe.If(some > 0):
                    gather(v + 1)
                    visit(v, False)
                with pe.Else():
                    pe.wait_ge(unit_used, N_MOE + v * VISIT)
                    pe.sem_inc(unit_used, VISIT)
                    for name, k, more in (("gathered", 2, 2), ("selt_done", 1, 0), ("ht_done", NCH, 0), ("scattered", 1, 1)):
                        pe.wait_ge(s[name], v * k + more)
                        pe.sem_inc(s[name], k)


_INS = ['x', 'c', 'ctx', 'c_ctx', 'ada_w', 'ada_b', 'g_pre_mix', 'g_post_mix', 'g_pre_ffn', 'g_post_ffn',
        'ab_w_in', 'a_norm_g', 'a_ws', 'a_bs', 'b_qnorm_g', 'b_knorm_g', 'ab_w_out', 'ffn_w_in', 'ffn_w_out',
        'mla_w_dq', 'mla_qnorm_g', 'mla_w_uq', 'mla_w_dkv', 'mla_kvnorm_g', 'mla_w_ukv', 'mla_w_o',
        'moe_router', 'moe_w_in', 'moe_w_out']


def kernel(**inputs):
    import concourse.bacc as _bacc
    from concourse.bass_utils import run_bass_kernel_spmd as _run

    nc = _bacc.Bacc("TRN2", target_bir_lowering=False, num_devices=1)
    arrays, args = {}, []
    for name in _INS + ["consts"]:
        a = np.ascontiguousarray(constants() if name == "consts" else inputs[name])
        arrays[f"in_{name}_dram"] = a
        args.append(nc.dram_tensor(f"in_{name}_dram", a.shape, mybir.dt.from_np(a.dtype), kind="ExternalInput").ap())
    args.append(nc.dram_tensor("out_0_dram", (1, SEQ, D), F32, kind="ExternalOutput").ap())
    trunk(nc, *args)
    r = _run(nc, [arrays], core_ids=[0])
    return r.results[0]["out_0_dram"]
```
